# Optimizing a Trainium2 kernel written in Bass

```python
import math
import jax
import jax.numpy as jnp
from jax import lax
import numpy as np
import jax, jax.numpy as jnp

D_MODEL = 1024
BATCH = 1
SEQ = 256
DEPTH = 2

D_MIX = D_MODEL
HG_HEADS = 4
HG_DK = 64
HG_DV = 64
HG_QK = HG_HEADS * HG_DK
HG_W = HG_HEADS * HG_DV
GD_HEADS = 4
GD_DK = 128
GD_DV = 128
GD_QK = GD_HEADS * GD_DK
GD_W = GD_HEADS * GD_DV
RG_W = D_MIX - HG_W - GD_W
RG_BLOCKS = 4
RG_BD = RG_W // RG_BLOCKS
RG_C = 8.0
CONV_W = 4
D_FF = 2816
CHUNK = 64
EPS = 1e-6
SPLIT_SIZES = (HG_QK, HG_QK, HG_W, HG_W, GD_QK, GD_QK, GD_W, GD_W, GD_HEADS, GD_HEADS, RG_W, RG_W)
SPLIT_POINTS = tuple(int(p) for p in np.cumsum(SPLIT_SIZES)[:-1])
N_IN = int(sum(SPLIT_SIZES))


def rmsnorm(x, w):
    xf = x.astype(jnp.float32)
    y = xf * lax.rsqrt(jnp.mean(xf * xf, axis=-1, keepdims=True) + EPS)
    return (y * w.astype(jnp.float32)).astype(x.dtype)

def head_rmsnorm(o, w):
    return o * lax.rsqrt(jnp.mean(o * o, axis=-1, keepdims=True) + EPS) * w.astype(jnp.float32)

def l2norm(t):
    return t * lax.rsqrt(jnp.sum(t * t, axis=-1, keepdims=True) + EPS)

def causal_depthwise_conv(x, w):
    return lax.conv_general_dilated(
        x, w[:, None, :].astype(x.dtype), window_strides=(1,), padding=[(CONV_W - 1, 0)],
        dimension_numbers=('NWC', 'WIO', 'NWC'), feature_group_count=x.shape[-1])

def to_chunks(t):
    b, l, h, d = t.shape
    return t.reshape(b, l // CHUNK, CHUNK, h, d).transpose(1, 0, 3, 2, 4)

def from_chunks(t):
    n, b, h, c, d = t.shape
    return t.transpose(1, 0, 3, 2, 4).reshape(b, n * c, h, d)

def swiglu(h, w_gate, w_up, w_down):
    return (jax.nn.silu(h @ w_gate) * (h @ w_up)) @ w_down

def hgrn2_chunked(q, k, v, logf):
    qc, kc, vc, gc = to_chunks(q), to_chunks(k), to_chunks(v), to_chunks(logf)
    _, b, h, _, dk = qc.shape
    dv = vc.shape[-1]
    causal = jnp.tril(jnp.ones((CHUNK, CHUNK), dtype=bool))[:, :, None]

    def step(state, inp):
        qi, ki, vi, gi = inp
        cum = jnp.cumsum(gi, axis=2)
        diff = cum[:, :, :, None, :] - cum[:, :, None, :, :]
        decay = jnp.exp(jnp.where(causal, diff, -jnp.inf))
        scores = jnp.einsum('bhtd,bhsd,bhtsd->bhts', qi, ki, decay)
        o = (jnp.einsum('bhts,bhsv->bhtv', scores, vi)
             + jnp.einsum('bhtd,bhdv->bhtv', qi * jnp.exp(cum), state))
        last = cum[:, :, -1:, :]
        state = (state * jnp.exp(last[:, :, 0, :, None])
                 + jnp.einsum('bhsd,bhsv->bhdv', ki * jnp.exp(last - cum), vi))
        return state, o

    s0 = jnp.zeros((b, h, dk, dv), jnp.float32)
    _, o = lax.scan(step, s0, (qc, kc, vc, gc))
    return from_chunks(o)

def gated_delta_chunked(q, k, v, g, beta):
    qc, kc, vc = to_chunks(q), to_chunks(k), to_chunks(v)
    gc = to_chunks(g[..., None])[..., 0]
    bc = to_chunks(beta[..., None])[..., 0]
    _, b, h, _, dk = qc.shape
    dv = vc.shape[-1]
    incl = jnp.tril(jnp.ones((CHUNK, CHUNK), dtype=bool))
    strict = jnp.tril(jnp.ones((CHUNK, CHUNK), dtype=bool), k=-1)
    eye = jnp.eye(CHUNK, dtype=jnp.float32)

    def step(state, inp):
        qi, ki, vi, gi, bi = inp
        cum = jnp.cumsum(gi, axis=-1)
        decay = jnp.exp(jnp.where(incl, cum[..., :, None] - cum[..., None, :], -jnp.inf))
        kb = ki * bi[..., None]
        lower = jnp.where(strict, jnp.einsum('bhtd,bhsd->bhts', kb, ki) * decay, 0.0)
        rhs = jnp.concatenate([vi * bi[..., None], kb * jnp.exp(cum)[..., None]], axis=-1)
        sol = lax.linalg.triangular_solve(eye + lower, rhs, left_side=True, lower=True,
                                          unit_diagonal=True)
        u, w = sol[..., :dv], sol[..., dv:]
        v_new = u - jnp.einsum('bhtd,bhdv->bhtv', w, state)
        scores = jnp.einsum('bhtd,bhsd->bhts', qi, ki) * decay
        o = (jnp.einsum('bhtd,bhdv->bhtv', qi * jnp.exp(cum)[..., None], state)
             + jnp.einsum('bhts,bhsv->bhtv', scores, v_new))
        last = cum[..., -1:]
        state = (state * jnp.exp(last)[..., None]
                 + jnp.einsum('bhsd,bhsv->bhdv', ki * jnp.exp(last - cum)[..., None], v_new))
        return state, o

    s0 = jnp.zeros((b, h, dk, dv), jnp.float32)
    _, o = lax.scan(step, s0, (qc, kc, vc, gc, bc))
    return from_chunks(o)

def rg_lru(xc, wr, br, wi, bi, lam):
    b, l, _ = xc.shape
    xb = xc.reshape(b, l, RG_BLOCKS, RG_BD)
    r = jax.nn.sigmoid(jnp.einsum('blni,nio->blno', xb, wr.astype(jnp.float32)).reshape(b, l, RG_W)
                       + br.astype(jnp.float32))
    ig = jax.nn.sigmoid(jnp.einsum('blni,nio->blno', xb, wi.astype(jnp.float32)).reshape(b, l, RG_W)
                        + bi.astype(jnp.float32))
    log_a = -RG_C * r * jax.nn.softplus(-lam.astype(jnp.float32))
    a = jnp.exp(log_a)
    bx = jnp.sqrt(-jnp.expm1(2.0 * log_a)) * (ig * xc)

    def combine(c1, c2):
        a1, b1 = c1
        a2, b2 = c2
        return a1 * a2, a2 * b1 + b2

    _, hs = lax.associative_scan(combine, (a, bx), axis=1)
    return hs

def hybrid_mixer(h, lb, w_in, hg_norm_w, gd_conv_w, gd_a_log, gd_dt_bias, gd_norm_w,
                 rg_conv_w, rg_conv_b, rg_wr, rg_br, rg_wi, rg_bi, rg_lambda, w_out):
    b, l, _ = h.shape
    f32 = jnp.float32
    proj = (h @ w_in).astype(f32)
    (hg_q, hg_f, hg_i, hg_g, gd_q, gd_k, gd_v, gd_z, gd_b, gd_a,
     rg_x, rg_gate) = jnp.split(proj, SPLIT_POINTS, axis=-1)

    lbf = lb.reshape(HG_HEADS, HG_DK)
    q = jax.nn.silu(hg_q).reshape(b, l, HG_HEADS, HG_DK) * (HG_DK ** -0.5)
    f = lbf + (1.0 - lbf) * jax.nn.sigmoid(hg_f.reshape(b, l, HG_HEADS, HG_DK))
    o_hg = hgrn2_chunked(q, 1.0 - f, hg_i.reshape(b, l, HG_HEADS, HG_DV), jnp.log(f))
    o_hg = head_rmsnorm(o_hg, hg_norm_w) * jax.nn.silu(hg_g.reshape(b, l, HG_HEADS, HG_DV))

    qkv = jax.nn.silu(causal_depthwise_conv(jnp.concatenate([gd_q, gd_k, gd_v], axis=-1), gd_conv_w))
    cq, ck, cv = jnp.split(qkv, (GD_QK, 2 * GD_QK), axis=-1)
    cq = l2norm(cq.reshape(b, l, GD_HEADS, GD_DK)) * (GD_DK ** -0.5)
    ck = l2norm(ck.reshape(b, l, GD_HEADS, GD_DK))
    beta = jax.nn.sigmoid(gd_b)
    g = -jnp.exp(gd_a_log.astype(f32)) * jax.nn.softplus(gd_a + gd_dt_bias.astype(f32))
    o_gd = gated_delta_chunked(cq, ck, cv.reshape(b, l, GD_HEADS, GD_DV), g, beta)
    o_gd = head_rmsnorm(o_gd, gd_norm_w) * jax.nn.silu(gd_z.reshape(b, l, GD_HEADS, GD_DV))

    xc = causal_depthwise_conv(rg_x, rg_conv_w) + rg_conv_b.astype(f32)
    o_rg = rg_lru(xc, rg_wr, rg_br, rg_wi, rg_bi, rg_lambda) * jax.nn.gelu(rg_gate, approximate=True)

    y = jnp.concatenate([o_hg.reshape(b, l, HG_W), o_gd.reshape(b, l, GD_W), o_rg], axis=-1)
    return y.astype(h.dtype) @ w_out

def first_inputs(seed: int = 0) -> dict:
    key = jax.random.key(seed)
    ks = jax.random.split(key, 32)
    f32 = jnp.float32

    def nrm(k, shape, scale):
        return jax.random.normal(k, shape, f32) * scale

    def gain(k, shape):
        return 1.0 + 0.02 * jax.random.normal(k, shape, f32)

    dt = jnp.exp(jax.random.uniform(ks[12], (DEPTH, GD_HEADS), f32, math.log(1e-3), math.log(1e-1)))
    a0 = jax.random.uniform(ks[19], (DEPTH, RG_W), f32, 0.9, 0.999) ** (1.0 / RG_C)
    return {
        'x': nrm(ks[0], (BATCH, SEQ, D_MODEL), 1.0),
        'norm_ffn1': gain(ks[1], (DEPTH, D_MODEL)),
        'ffn1_gate': nrm(ks[2], (DEPTH, D_MODEL, D_FF), D_MODEL ** -0.5),
        'ffn1_up': nrm(ks[3], (DEPTH, D_MODEL, D_FF), D_MODEL ** -0.5),
        'ffn1_down': nrm(ks[4], (DEPTH, D_FF, D_MODEL), D_FF ** -0.5),
        'norm_mix': gain(ks[5], (DEPTH, D_MODEL)),
        'w_in': nrm(ks[6], (DEPTH, D_MODEL, N_IN), D_MODEL ** -0.5),
        'hg_lb': nrm(ks[7], (DEPTH, HG_QK), 1.0),
        'hg_norm_w': gain(ks[8], (DEPTH, HG_DV)),
        'gd_conv_w': nrm(ks[9], (DEPTH, CONV_W, 2 * GD_QK + GD_W), CONV_W ** -0.5),
        'gd_a_log': jnp.log(jax.random.uniform(ks[10], (DEPTH, GD_HEADS), f32, 1.0, 16.0)),
        'gd_dt_bias': dt + jnp.log(-jnp.expm1(-dt)),
        'gd_norm_w': gain(ks[11], (DEPTH, GD_DV)),
        'rg_conv_w': nrm(ks[13], (DEPTH, CONV_W, RG_W), CONV_W ** -0.5),
        'rg_conv_b': nrm(ks[14], (DEPTH, RG_W), 0.02),
        'rg_wr': nrm(ks[15], (DEPTH, RG_BLOCKS, RG_BD, RG_BD), RG_BD ** -0.5),
        'rg_br': nrm(ks[16], (DEPTH, RG_W), 0.1),
        'rg_wi': nrm(ks[17], (DEPTH, RG_BLOCKS, RG_BD, RG_BD), RG_BD ** -0.5),
        'rg_bi': nrm(ks[18], (DEPTH, RG_W), 0.1),
        'rg_lambda': jnp.log(a0) - jnp.log1p(-a0),
        'w_out': nrm(ks[20], (DEPTH, D_MIX, D_MODEL), D_MIX ** -0.5),
        'norm_ffn2': gain(ks[21], (DEPTH, D_MODEL)),
        'ffn2_gate': nrm(ks[22], (DEPTH, D_MODEL, D_FF), D_MODEL ** -0.5),
        'ffn2_up': nrm(ks[23], (DEPTH, D_MODEL, D_FF), D_MODEL ** -0.5),
        'ffn2_down': nrm(ks[24], (DEPTH, D_FF, D_MODEL), D_FF ** -0.5),
        'norm_final': gain(ks[25], (D_MODEL,)),
    }

def first_block(x, norm_ffn1, ffn1_gate, ffn1_up, ffn1_down, norm_mix, w_in, hg_lb, hg_norm_w,
              gd_conv_w, gd_a_log, gd_dt_bias, gd_norm_w, rg_conv_w, rg_conv_b, rg_wr, rg_br,
              rg_wi, rg_bi, rg_lambda, w_out, norm_ffn2, ffn2_gate, ffn2_up, ffn2_down, norm_final):
    lb_all = jnp.cumsum(jax.nn.softmax(hg_lb.astype(jnp.float32), axis=0), axis=0)
    lb_all = lb_all - lb_all[0]
    for layer in range(DEPTH):
        x = x + 0.5 * swiglu(rmsnorm(x, norm_ffn1[layer]), ffn1_gate[layer], ffn1_up[layer],
                             ffn1_down[layer])
        x = x + hybrid_mixer(rmsnorm(x, norm_mix[layer]), lb_all[layer], w_in[layer], hg_norm_w[layer],
                             gd_conv_w[layer], gd_a_log[layer], gd_dt_bias[layer], gd_norm_w[layer],
                             rg_conv_w[layer], rg_conv_b[layer], rg_wr[layer], rg_br[layer],
                             rg_wi[layer], rg_bi[layer], rg_lambda[layer], w_out[layer])
        x = x + 0.5 * swiglu(rmsnorm(x, norm_ffn2[layer]), ffn2_gate[layer], ffn2_up[layer],
                             ffn2_down[layer])
    return rmsnorm(x, norm_final)


CTX_LEN = 256
GRID_W = 64
HEAD_DIM = 64
ROPE_THETA = 10000.0
NEG_INF = -1e30

NA_HEADS = 8
NA_WIN_H = 8
NA_WIN_W = 16
DIFF_HEADS = 4
DIFF_QK_DIM = 64
DIFF_V_DIM = 128
DENSE_BLOCK = 128
SWA_Q_HEADS = 16
SWA_KV_HEADS = 4
SWA_WINDOW = 128
SWA_BLOCK = 128
PEER_HEADS = 8
PEER_NKEYS = 128
PEER_EXPERTS = PEER_NKEYS * PEER_NKEYS
PEER_QDIM = 256
PEER_TOPK = 16
PEER_CHUNK = 128

EVEN_IN = 3 * NA_HEADS * HEAD_DIM + DIFF_HEADS * (4 * DIFF_QK_DIM + DIFF_V_DIM)
EVEN_OUT = NA_HEADS * HEAD_DIM + DIFF_HEADS * DIFF_V_DIM
ODD_IN = (SWA_Q_HEADS + 2 * SWA_KV_HEADS) * HEAD_DIM
ODD_OUT = SWA_Q_HEADS * HEAD_DIM
N_EVEN = (DEPTH + 1) // 2
N_ODD = DEPTH // 2


def rmsnorm_2(x, g):
    xf = x.astype(jnp.float32)
    y = xf * lax.rsqrt(jnp.mean(xf * xf, axis=-1, keepdims=True) + EPS)
    return (y * g.astype(jnp.float32)).astype(x.dtype)

def split_mod(m, lead):
    m = m.reshape(lead + (6, D_MODEL))
    return tuple(m[..., k, :] for k in range(6))

def rope_tables(n_tokens):
    t = jnp.arange(n_tokens)
    row = (t // GRID_W).astype(jnp.float32)
    col = (t % GRID_W).astype(jnp.float32)
    half = HEAD_DIM // 2
    inv = ROPE_THETA ** (-jnp.arange(0, half, 2, dtype=jnp.float32) / half)
    ar = row[:, None] * inv
    ac = col[:, None] * inv
    ang = jnp.concatenate([ar, ar, ac, ac], axis=-1)
    return jnp.cos(ang), jnp.sin(ang)

def apply_rope2d(x, cos, sin):
    q = HEAD_DIM // 4
    rot = jnp.concatenate([-x[..., q:2 * q], x[..., :q], -x[..., 3 * q:], x[..., 2 * q:3 * q]], axis=-1)
    shp = (x.shape[1],) + (1,) * (x.ndim - 3) + (HEAD_DIM,)
    return (x * cos.reshape(shp) + rot * sin.reshape(shp)).astype(x.dtype)

def plain_ctx_attention(qc, kc, vc):
    B, C, H, d = qc.shape
    s = jnp.einsum('bqhd,bkhd->bhqk', qc, kc).astype(jnp.float32) * (d ** -0.5)
    p = jax.nn.softmax(s, axis=-1).astype(vc.dtype)
    return jnp.einsum('bhqk,bkhd->bqhd', p, vc).reshape(B, C, H * d)

def neighborhood_attention(q, k, v, qc, kc, vc, rpb, need_ctx):
    B, S, H, d = q.shape
    rows = S // GRID_W
    kh = min(NA_WIN_H, rows)
    kw = NA_WIN_W
    scale = d ** -0.5
    qg = q.reshape(B, rows, GRID_W, H, d)
    kg = k.reshape(B, rows, GRID_W, H, d)
    vg = v.reshape(B, rows, GRID_W, H, d)
    cols = jnp.arange(GRID_W)
    col_start = jnp.clip(cols - kw // 2, 0, GRID_W - kw)
    col_idx = col_start[:, None] + jnp.arange(kw)
    dc = col_idx - cols[:, None] + (NA_WIN_W - 1)
    rpb_c = rpb[:, :, dc]

    def one_row(args):
        r, q_row = args
        rs = jnp.clip(r - kh // 2, 0, rows - kh)
        k_rows = lax.dynamic_slice_in_dim(kg, rs, kh, axis=1)
        v_rows = lax.dynamic_slice_in_dim(vg, rs, kh, axis=1)
        k_nb = k_rows[:, :, col_idx]
        v_nb = v_rows[:, :, col_idx]
        dr = rs + jnp.arange(kh) - r + (NA_WIN_H - 1)
        bias = rpb_c[:, dr].transpose(0, 2, 1, 3)
        s_nb = jnp.einsum('bqhd,brqwhd->bhqrw', q_row, k_nb).astype(jnp.float32) * scale
        s_nb = (s_nb + bias[None].astype(jnp.float32)).reshape(B, H, GRID_W, kh * kw)
        s_ctx = jnp.einsum('bqhd,bchd->bhqc', q_row, kc).astype(jnp.float32) * scale
        p = jax.nn.softmax(jnp.concatenate([s_nb, s_ctx], axis=-1), axis=-1).astype(v.dtype)
        p_nb = p[..., :kh * kw].reshape(B, H, GRID_W, kh, kw)
        p_ctx = p[..., kh * kw:]
        return (jnp.einsum('bhqrw,brqwhd->bqhd', p_nb, v_nb)
                + jnp.einsum('bhqc,bchd->bqhd', p_ctx, vc))

    out = lax.map(one_row, (jnp.arange(rows), qg.transpose(1, 0, 2, 3, 4)))
    out = out.transpose(1, 0, 2, 3, 4).reshape(B, S, H * d)
    out_c = plain_ctx_attention(qc, kc, vc) if need_ctx else None
    return out, out_c

def diff_attention(q, k, v, qc, kc, vc, lam_p, subln_g, lam_init, need_ctx):
    B, S, H, _, dq = q.shape
    dv = v.shape[-1]
    scale = dq ** -0.5
    lp = lam_p.astype(jnp.float32)
    lam = jnp.exp(jnp.sum(lp[0] * lp[1])) - jnp.exp(jnp.sum(lp[2] * lp[3])) + lam_init

    def attend(qb, kk, vv):
        s = jnp.einsum('bqhmd,bkhmd->bmhqk', qb, kk).astype(jnp.float32) * scale
        p = jax.nn.softmax(s, axis=-1)
        pd = (p[:, 0] - lam * p[:, 1]).astype(vv.dtype)
        o = jnp.einsum('bhqk,bkhd->bqhd', pd, vv)
        return (rmsnorm_2(o, subln_g) * (1.0 - lam_init)).astype(vv.dtype)

    k_all = jnp.concatenate([kc, k], axis=1)
    v_all = jnp.concatenate([vc, v], axis=1)
    nb = S // DENSE_BLOCK
    qblocks = q.reshape(B, nb, DENSE_BLOCK, H, 2, dq).transpose(1, 0, 2, 3, 4, 5)
    out = lax.map(lambda qb: attend(qb, k_all, v_all), qblocks)
    out = out.transpose(1, 0, 2, 3, 4).reshape(B, S, H * dv)
    out_c = attend(qc, kc, vc).reshape(B, qc.shape[1], H * dv) if need_ctx else None
    return out, out_c

def window_gqa(q, k, v, qc, kc, vc, sink, need_ctx):
    B, S, Hq, d = q.shape
    Hkv = k.shape[2]
    G = Hq // Hkv
    scale = d ** -0.5
    blk = SWA_BLOCK
    nb = S // blk
    pad = ((0, 0), (blk, blk), (0, 0), (0, 0))
    kp = jnp.pad(k, pad)
    vp = jnp.pad(v, pad)
    qi = jnp.arange(blk)
    kj = jnp.arange(3 * blk)
    band = jnp.abs(kj[None, :] - blk - qi[:, None]) <= SWA_WINDOW
    sink_f = sink.astype(jnp.float32).reshape(Hkv, G)

    def sink_attend(qg, s_parts, v_parts):
        n = qg.shape[1]
        s_sink = jnp.broadcast_to(sink_f[None, :, :, None, None], (B, Hkv, G, n, 1))
        p = jax.nn.softmax(jnp.concatenate([s_sink] + s_parts, axis=-1), axis=-1)
        o = 0.0
        off = 1
        for s_i, v_i in zip(s_parts, v_parts):
            w = s_i.shape[-1]
            o = o + jnp.einsum('bngqj,bjnd->bqngd', p[..., off:off + w].astype(v_i.dtype), v_i)
            off += w
        return o.reshape(B, n, Hq * d).astype(v_parts[0].dtype)

    def one_block(args):
        bi, qb = args
        start = bi * blk
        kb = lax.dynamic_slice_in_dim(kp, start, 3 * blk, axis=1)
        vb = lax.dynamic_slice_in_dim(vp, start, 3 * blk, axis=1)
        kpos = start - blk + kj
        valid = band & ((kpos >= 0) & (kpos < S))[None, :]
        qg = qb.reshape(B, blk, Hkv, G, d)
        s_loc = jnp.einsum('bqngd,bjnd->bngqj', qg, kb).astype(jnp.float32) * scale
        s_loc = jnp.where(valid, s_loc, NEG_INF)
        s_ctx = jnp.einsum('bqngd,bjnd->bngqj', qg, kc).astype(jnp.float32) * scale
        return sink_attend(qg, [s_loc, s_ctx], [vb, vc])

    qblocks = q.reshape(B, nb, blk, Hq, d).transpose(1, 0, 2, 3, 4)
    out = lax.map(one_block, (jnp.arange(nb), qblocks))
    out = out.transpose(1, 0, 2, 3).reshape(B, S, Hq * d)
    out_c = None
    if need_ctx:
        qcg = qc.reshape(B, qc.shape[1], Hkv, G, d)
        s_c = jnp.einsum('bqngd,bjnd->bngqj', qcg, kc).astype(jnp.float32) * scale
        out_c = sink_attend(qcg, [s_c], [vc])
    return out, out_c

def even_mixer(hx, hc, w_in, w_out, rpb, lam_p, subln_g, cos, sin, lam_init, need_ctx):
    B, S, _ = hx.shape
    a = NA_HEADS * HEAD_DIM
    bqk = DIFF_HEADS * 2 * DIFF_QK_DIM

    def split(p, n):
        qa = p[..., :a].reshape(B, n, NA_HEADS, HEAD_DIM)
        ka = p[..., a:2 * a].reshape(B, n, NA_HEADS, HEAD_DIM)
        va = p[..., 2 * a:3 * a].reshape(B, n, NA_HEADS, HEAD_DIM)
        o = 3 * a
        qb = p[..., o:o + bqk].reshape(B, n, DIFF_HEADS, 2, DIFF_QK_DIM)
        kb = p[..., o + bqk:o + 2 * bqk].reshape(B, n, DIFF_HEADS, 2, DIFF_QK_DIM)
        vb = p[..., o + 2 * bqk:].reshape(B, n, DIFF_HEADS, DIFF_V_DIM)
        return qa, ka, va, qb, kb, vb

    qa, ka, va, qb, kb, vb = split(hx @ w_in, S)
    qac, kac, vac, qbc, kbc, vbc = split(hc @ w_in, hc.shape[1])
    qb = apply_rope2d(qb, cos, sin)
    kb = apply_rope2d(kb, cos, sin)
    oa, oac = neighborhood_attention(qa, ka, va, qac, kac, vac, rpb, need_ctx)
    ob, obc = diff_attention(qb, kb, vb, qbc, kbc, vbc, lam_p, subln_g, lam_init, need_ctx)
    y = jnp.concatenate([oa, ob], axis=-1) @ w_out
    yc = jnp.concatenate([oac, obc], axis=-1) @ w_out if need_ctx else None
    return y, yc

def odd_mixer(hx, hc, w_in, w_out, sink, cos, sin, need_ctx):
    B, S, _ = hx.shape
    nq = SWA_Q_HEADS * HEAD_DIM
    nkv = SWA_KV_HEADS * HEAD_DIM

    def split(p, n):
        return (p[..., :nq].reshape(B, n, SWA_Q_HEADS, HEAD_DIM),
                p[..., nq:nq + nkv].reshape(B, n, SWA_KV_HEADS, HEAD_DIM),
                p[..., nq + nkv:].reshape(B, n, SWA_KV_HEADS, HEAD_DIM))

    q, k, v = split(hx @ w_in, S)
    qc, kc, vc = split(hc @ w_in, hc.shape[1])
    q = apply_rope2d(q, cos, sin)
    k = apply_rope2d(k, cos, sin)
    o, oc = window_gqa(q, k, v, qc, kc, vc, sink, need_ctx)
    y = o @ w_out
    yc = oc @ w_out if need_ctx else None
    return y, yc

def peer(h, w_q, sub_keys, u, v):
    T, D = h.shape
    q = (h @ w_q).reshape(T, PEER_HEADS, 2, PEER_QDIM // 2)
    s = jnp.einsum('thpd,hpnd->thpn', q, sub_keys).astype(jnp.float32)
    sv, si = lax.top_k(s, PEER_TOPK)
    cand = (sv[:, :, 0, :, None] + sv[:, :, 1, None, :]).reshape(T, PEER_HEADS, PEER_TOPK * PEER_TOPK)
    fv, fi = lax.top_k(cand, PEER_TOPK)
    i1 = jnp.take_along_axis(si[:, :, 0], fi // PEER_TOPK, axis=-1)
    i2 = jnp.take_along_axis(si[:, :, 1], fi % PEER_TOPK, axis=-1)
    idx = (i1 * PEER_NKEYS + i2).reshape(T, PEER_HEADS * PEER_TOPK)
    g = jax.nn.softmax(fv, axis=-1).reshape(T, PEER_HEADS * PEER_TOPK).astype(h.dtype)
    nc = T // PEER_CHUNK

    def chunk(args):
        hc, ic, gc = args
        ue = u[ic]
        ve = v[ic]
        act = jax.nn.gelu(jnp.einsum('td,ted->te', hc, ue), approximate=False)
        return jnp.einsum('te,ted->td', gc * act, ve)

    out = lax.map(chunk, (h.reshape(nc, PEER_CHUNK, D),
                          idx.reshape(nc, PEER_CHUNK, -1),
                          g.reshape(nc, PEER_CHUNK, -1)))
    return out.reshape(T, D)

def second_inputs(seed: int = 0) -> dict:
    key = jax.random.key(seed)
    ks = jax.random.split(key, 24)
    D = D_MODEL

    def nrm(k, shape, s):
        return jax.random.normal(k, shape, jnp.float32) * s

    return {
        "x": nrm(ks[0], (BATCH, SEQ, D), 1.0),
        "c": nrm(ks[1], (BATCH, D), 1.0),
        "ctx": nrm(ks[2], (BATCH, CTX_LEN, D), 1.0),
        "c_ctx": nrm(ks[3], (D,), 1.0),
        "w_mod": nrm(ks[4], (DEPTH, D, 6 * D), 0.5 * D ** -0.5),
        "b_mod": nrm(ks[5], (DEPTH, 6 * D), 0.02),
        "norm1_g": 1.0 + nrm(ks[6], (DEPTH, D), 0.05),
        "norm2_g": 1.0 + nrm(ks[7], (DEPTH, D), 0.05),
        "w_in_even": nrm(ks[8], (N_EVEN, D, EVEN_IN), D ** -0.5),
        "w_out_even": nrm(ks[9], (N_EVEN, EVEN_OUT, D), EVEN_OUT ** -0.5),
        "na_rpb": nrm(ks[10], (N_EVEN, NA_HEADS, 2 * NA_WIN_H - 1, 2 * NA_WIN_W - 1), 0.1),
        "diff_lambda": nrm(ks[11], (N_EVEN, 4, DIFF_QK_DIM), 0.1),
        "diff_subln_g": 1.0 + nrm(ks[12], (N_EVEN, DIFF_V_DIM), 0.05),
        "w_in_odd": nrm(ks[13], (N_ODD, D, ODD_IN), D ** -0.5),
        "w_out_odd": nrm(ks[14], (N_ODD, ODD_OUT, D), ODD_OUT ** -0.5),
        "swa_sink": nrm(ks[15], (N_ODD, SWA_Q_HEADS), 0.5),
        "peer_wq": nrm(ks[16], (DEPTH, D, PEER_HEADS * PEER_QDIM), D ** -0.5),
        "peer_keys": nrm(ks[17], (DEPTH, PEER_HEADS, 2, PEER_NKEYS, PEER_QDIM // 2), (PEER_QDIM // 2) ** -0.5),
        "peer_u": nrm(ks[18], (DEPTH, PEER_EXPERTS, D), D ** -0.5),
        "peer_v": nrm(ks[19], (DEPTH, PEER_EXPERTS, D), 0.25),
        "final_g": 1.0 + nrm(ks[20], (D,), 0.05),
    }

def second_block(x, c, ctx, c_ctx, w_mod, b_mod, norm1_g, norm2_g, w_in_even, w_out_even,
              na_rpb, diff_lambda, diff_subln_g, w_in_odd, w_out_odd, swa_sink,
              peer_wq, peer_keys, peer_u, peer_v, final_g):
    B, S, D = x.shape
    C = ctx.shape[1]
    cos, sin = rope_tables(S)
    sc = jax.nn.silu(c)
    scc = jax.nn.silu(c_ctx)
    for i in range(DEPTH):
        need_ctx = i < DEPTH - 1
        sh1, sc1, g1, sh2, sc2, g2 = split_mod(sc @ w_mod[i] + b_mod[i], (B, 1))
        ch1, cc1, cg1, ch2, cc2, cg2 = split_mod(scc @ w_mod[i] + b_mod[i], (1, 1))
        hx = rmsnorm_2(x, norm1_g[i]) * (1.0 + sc1) + sh1
        hc = rmsnorm_2(ctx, norm1_g[i]) * (1.0 + cc1) + ch1
        if i % 2 == 0:
            j = i // 2
            lam_init = 0.8 - 0.6 * math.exp(-0.3 * i)
            y, yc = even_mixer(hx, hc, w_in_even[j], w_out_even[j], na_rpb[j], diff_lambda[j],
                               diff_subln_g[j], cos, sin, lam_init, need_ctx)
        else:
            j = i // 2
            y, yc = odd_mixer(hx, hc, w_in_odd[j], w_out_odd[j], swa_sink[j], cos, sin, need_ctx)
        x = x + g1 * y
        hx = rmsnorm_2(x, norm2_g[i]) * (1.0 + sc2) + sh2
        if need_ctx:
            ctx = ctx + cg1 * yc
            hc = rmsnorm_2(ctx, norm2_g[i]) * (1.0 + cc2) + ch2
            tokens = jnp.concatenate([hx.reshape(B * S, D), hc.reshape(B * C, D)], axis=0)
            f = peer(tokens, peer_wq[i], peer_keys[i], peer_u[i], peer_v[i])
            x = x + g2 * f[:B * S].reshape(B, S, D)
            ctx = ctx + cg2 * f[B * S:].reshape(B, C, D)
        else:
            f = peer(hx.reshape(B * S, D), peer_wq[i], peer_keys[i], peer_u[i], peer_v[i])
            x = x + g2 * f.reshape(B, S, D)
    return rmsnorm_2(x, final_g)


def setup_inputs(seed=0):
    out = dict(first_inputs(seed))
    for name, value in second_inputs(seed + 1).items():
        if name != "x":
            out[name + "_2"] = value
    return out


def reference(
    x, norm_ffn1, ffn1_gate, ffn1_up, ffn1_down, norm_mix, w_in, hg_lb, hg_norm_w, gd_conv_w,
    gd_a_log, gd_dt_bias, gd_norm_w, rg_conv_w, rg_conv_b, rg_wr, rg_br, rg_wi, rg_bi,
    rg_lambda, w_out, norm_ffn2, ffn2_gate, ffn2_up, ffn2_down, norm_final, c_2, ctx_2, c_ctx_2,
    w_mod_2, b_mod_2, norm1_g_2, norm2_g_2, w_in_even_2, w_out_even_2, na_rpb_2, diff_lambda_2,
    diff_subln_g_2, w_in_odd_2, w_out_odd_2, swa_sink_2, peer_wq_2, peer_keys_2, peer_u_2,
    peer_v_2, final_g_2,
):
    x = first_block(
        x, norm_ffn1, ffn1_gate, ffn1_up, ffn1_down, norm_mix, w_in, hg_lb, hg_norm_w,
        gd_conv_w, gd_a_log, gd_dt_bias, gd_norm_w, rg_conv_w, rg_conv_b, rg_wr, rg_br, rg_wi,
        rg_bi, rg_lambda, w_out, norm_ffn2, ffn2_gate, ffn2_up, ffn2_down, norm_final,
    )
    return second_block(
        x, c_2, ctx_2, c_ctx_2, w_mod_2, b_mod_2, norm1_g_2, norm2_g_2, w_in_even_2,
        w_out_even_2, na_rpb_2, diff_lambda_2, diff_subln_g_2, w_in_odd_2, w_out_odd_2,
        swa_sink_2, peer_wq_2, peer_keys_2, peer_u_2, peer_v_2, final_g_2,
    )


_drawn_inputs = setup_inputs


def setup_inputs(seed=0):
    import zlib

    import numpy as np

    out = dict(_drawn_inputs(seed))
    spreads = {}
    factors = {'norm_ffn1': 3.533,
     'hg_norm_w': 5.753,
     'gd_norm_w': 4.359,
     'rg_br': 7.647,
     'rg_bi': 5.608,
     'norm_ffn2': 4.644,
     'norm1_g_2': 5.355,
     'norm2_g_2': 4.049,
     'na_rpb_2': 8.0,
     'diff_lambda_2': 4.514,
     'diff_subln_g_2': 4.985,
     'swa_sink_2': 8.0}
    for name, (base, spread) in spreads.items():
        noise = np.random.default_rng([zlib.crc32(name.encode()), seed]).standard_normal(out[name].shape)
        drawn = base * np.exp(spread * noise) if base else spread * noise
        out[name] = jnp.asarray(drawn.astype(out[name].dtype))
    for name, factor in factors.items():
        out[name] = (out[name] * factor).astype(out[name].dtype)
    return out
```

```python
from contextlib import ExitStack, contextmanager

import numpy as np

import concourse.bass as bass
from concourse import mybir

F32 = mybir.dt.float32
U32 = mybir.dt.uint32
ALU = mybir.AluOpType
ACT = mybir.ActivationFunctionType
AX = mybir.AxisListType.X

P = 128
D = 1024
DC = D // P
T = 256
TT = T // P
DEPTH = 2
D_FF = 2816
FC = D_FF // P
EPS = 1e-6

HG_DK = 64
HG_PAIRS = 2
GD_HEADS = 4
RG_C = 8.0
CONV_W = 4
N_PROJ = 28
PAD = CONV_W - 1
TPAD = T + 4
HG_Q, HG_F, HG_I, HG_G, GD_Q, GD_K, GD_V, GD_Z, RG_X, RG_GATE = 0, 2, 4, 6, 8, 12, 16, 20, 24, 26

HEAD = 64
GRID_W = 64
NA_WIN_H, NA_WIN_W, NA_HEADS = 8, 16, 8
DIFF_HEADS = 4
SWA_Q_HEADS, SWA_KV_HEADS, SWA_WINDOW = 16, 4, 128
ROPE_THETA = 10000.0
NEG = -1e30
LAM_INIT = 0.8 - 0.6
PEER_HEADS, PEER_NKEYS, PEER_TOPK = 8, 128, 16
SLOTS = PEER_HEADS * PEER_TOPK

COL, _at = {}, 0
for _name, _n in (("norm_ffn1", DC), ("norm_mix", DC), ("norm_ffn2", DC), ("hg_norm", 1),
                  ("gd_norm", 1), ("gd_conv", 12 * CONV_W), ("rg_conv", 2 * CONV_W), ("rg_conv_b", 2),
                  ("rg_br", 2), ("rg_bi", 2), ("rg_lambda", 2), ("gd_a_log", 4), ("gd_dt_bias", 4)):
    COL[_name] = (_at, _n)
    _at += _n
N_COLS = _at

COL2, _at = {}, 0
for _name, _n in (("norm1", 2 * DC), ("norm2", 2 * DC), ("b_mod", 2 * 48), ("c", 2 * DC), ("final", DC),
                  ("norm_last", DC), ("subln", 1), ("lambda", 4 * HEAD), ("sink", SWA_Q_HEADS)):
    COL2[_name] = (_at, _n)
    _at += _n
N_COLS2 = _at

CST, _at = {}, 0
for _name, _n in (("ident", P), ("ones", P), ("halves", P), ("tri_incl", P), ("tri_strict", P),
                  ("slide", 2 * P - HEAD - 1), ("iota", P), ("rot", P), ("cos", T), ("sin", T),
                  ("band", TT * T), ("level", 7 * P), ("level_t", 7 * P)):
    CST[_name] = (_at, _n)
    _at += _n
N_CST = _at


_names = {}


def unique(name):
    _names[name] = _names.get(name, -1) + 1
    return f"{name}_{_names[name]}"


def sbuf(nc, name, shape, dtype):
    return nc.sbuf_tensor(unique(name), shape, dtype)


def psum(nc, name, shape, dtype):
    return nc.psum_tensor(unique(name), shape, dtype)


@contextmanager
def stage(nc, *names):
    def take():
        held = [nc.semaphore(n) for n in names]
        return held, [s.__enter__() for s in held]

    def give(held):
        for s in held:
            s.__exit__(None, None, None)

    held, sems = take()
    if sems[-1].num - sems[0].num != len(sems) - 1:
        give(held)
        held, sems = take()
    first = sems[0].num
    assert [s.num for s in sems] == list(range(first, first + len(sems)))
    with nc.Block() as block:
        yield (block, *sems)
    nc.all_engine_barrier(sems_to_clear=range(first, first + len(sems)))
    give(held)


class Order:

    def __init__(self, engine, sem):
        self.engine, self.sem, self.n = engine, sem, 0

    def __call__(self, ins):
        ins.then_inc(self.sem, 1)
        self.n += 1
        self.engine.wait_ge(self.sem, self.n)


class Buffers:
    pass


class Constants:

    def __init__(self, cst):
        def part(name, i=0, n=None):
            a = CST[name][0] + i
            return cst[:, a:a + (CST[name][1] if n is None else n)]

        self.ident, self.ones, self.halves = part("ident"), part("ones"), part("halves")
        self.tri_incl, self.tri_strict = part("tri_incl"), part("tri_strict")
        self.slide, self.iota, self.rot = part("slide"), part("iota"), part("rot")
        self.cos, self.sin, self.band = part("cos"), part("sin"), part("band")
        self.level = lambda m: part("level", m * P, P)
        self.level_t = lambda m: part("level_t", m * P, P)


def load_stage(nc, pairs):
    with stage(nc, "loaded") as (block, loaded):
        @block.sync
        def _(sp):
            for dst, src in pairs:
                sp.dma_start(dst, src).then_inc(loaded, 16)
            sp.wait_ge(loaded, 16 * len(pairs))


def norm_stage(nc, k, src, gain, dst, shift=None):
    with ExitStack() as ctx:
        sq = ctx.enter_context(sbuf(nc, "sq", [P, DC, T], F32))
        rstd = ctx.enter_context(sbuf(nc, "rstd", [P, T], F32))
        mean = ctx.enter_context(psum(nc, "mean", [P, 512], F32))
        with stage(nc, "squared", "summed", "inverse", "rooted", "scaled", "own") as (
                block, squared, summed, inverse, rooted, scaled, own):
            @block.scalar
            def _(act):
                for h in range(2):
                    half = slice(h * DC // 2, (h + 1) * DC // 2)
                    act.activation(sq[:, half, :], src[:, half, :], ACT.Square).then_inc(squared, 1)
                act.wait_ge(inverse, 1)
                act.activation(rstd[:], rstd[:], ACT.Sqrt).then_inc(rooted, 1)
                if shift is not None:
                    for c in range(DC):
                        act.wait_ge(scaled, c + 1)
                        act.activation(dst[:, c, :], dst[:, c, :], ACT.Identity, bias=shift[:, c:c + 1])

            @block.tensor
            def _(pe):
                for c in range(DC):
                    if c % (DC // 2) == 0:
                        pe.wait_ge(squared, 2 * c // DC + 1)
                    last = pe.matmul(mean[:, 0:T], k.ones, sq[:, c, :], start=(c == 0), stop=(c == DC - 1))
                last.then_inc(summed, 1)

            @block.vector
            def _(dve):
                order = Order(dve, own)
                dve.wait_ge(summed, 1)
                order(dve.tensor_scalar(rstd[:], mean[:, 0:T], 1.0 / D, EPS, ALU.mult, ALU.add))
                dve.reciprocal(rstd[:], rstd[:]).then_inc(inverse, 1)
                dve.wait_ge(rooted, 1)
                for c in range(DC):
                    dve.scalar_tensor_tensor(dst[:, c, :], src[:, c, :], gain[:, c:c + 1], rstd[:],
                                             ALU.mult, ALU.mult).then_inc(scaled, 1)


def ffn_stage(nc, k, h, x, wg, wu, wd):
    W = 3
    with ExitStack() as ctx:
        wgt = ctx.enter_context(sbuf(nc, "wgt", [P, 2 * W, 2, D], F32))
        wdt = ctx.enter_context(sbuf(nc, "wdt", [P, 2, FC * P], F32))
        sg = ctx.enter_context(sbuf(nc, "sg", [P, 2, T], F32))
        gu = ctx.enter_context(sbuf(nc, "gu", [P, FC, T], F32))
        gate_up = [[ctx.enter_context(psum(nc, f"{n}{i}", [P, 512], F32)) for n in ("gate", "up")]
                   for i in range(2)]
        down = [ctx.enter_context(psum(nc, f"down{i}", [P, 512], F32)) for i in range(2)]
        with stage(nc, "w_in0", "w_in1", "w_free", "projected", "gated", "gu_free", "wd_in0", "wd_in1",
                   "wd_free", "downed", "down_free") as (
                block, w_in0, w_in1, w_free, projected, gated, gu_free, wd_in0, wd_in1, wd_free, downed,
                down_free):
            w_in, wd_in = (w_in0, w_in1), (wd_in0, wd_in1)

            @block.sync
            def _(sp):
                for s in range(2):
                    sp.dma_start(wgt[:, s, 0, :], wg[s]).then_inc(w_in[s], 16)
                    sp.dma_start(wgt[:, s, 1, :], wu[s]).then_inc(w_in[s], 16)
                for s in range(2):
                    sp.dma_start(wdt[:, s, :], wd[s]).then_inc(wd_in[s], 16)
                with sp.Fori(1, FC // 2) as i:
                    for s in range(2):
                        sp.wait_ge(w_free, 2 * i + (s - 1))
                        sp.dma_start(wgt[:, s, 0, :], wg[2 * i + s]).then_inc(w_in[s], 16)
                        sp.dma_start(wgt[:, s, 1, :], wu[2 * i + s]).then_inc(w_in[s], 16)
                with sp.Fori(1, DC // 2) as i:
                    for s in range(2):
                        sp.wait_ge(wd_free, 2 * i + (s - 1))
                        sp.dma_start(wdt[:, s, :], wd[2 * i + s]).then_inc(wd_in[s], 16)

            @block.tensor
            def _(pe):
                with pe.Fori(0, FC // 2) as i:
                    for s in range(2):
                        pe.wait_ge(w_in[s], 32 * i + 32)
                        pe.wait_ge(gu_free, 2 * i + (s + 1))
                        for m in range(2):
                            for c in range(DC):
                                last = pe.matmul(gate_up[s][m][:, 0:T], wgt[:, s, m, c * P:(c + 1) * P],
                                                 h[:, c, :], start=(c == 0), stop=(c == DC - 1))
                            if m == 0:
                                last.then_inc(projected, 1)
                            else:
                                last.then_inc(w_free, 1)
                pe.wait_ge(gu_free, FC + 2)
                with pe.Fori(0, DC // 2) as i:
                    for s in range(2):
                        pe.wait_ge(wd_in[s], 16 * i + 16)
                        pe.wait_ge(down_free, 2 * i + (s + 1))
                        for f in range(FC):
                            last = pe.matmul(down[s][:, 0:T], wdt[:, s, f * P:(f + 1) * P], gu[:, f, :],
                                             start=(f == 0), stop=(f == FC - 1))
                        last.then_inc(wd_free, 1)

            @block.scalar
            def _(act):
                with act.Fori(0, FC // 2) as i:
                    for s in range(2):
                        act.wait_ge(projected, 2 * i + (s + 1))
                        act.activation(sg[:, s, :], gate_up[s][0][:, 0:T], ACT.Silu).then_inc(gated, 1)

            @block.vector
            def _(dve):
                dve.sem_inc(gu_free, 2)
                dve.sem_inc(down_free, 2)
                with dve.Fori(0, FC // 2) as i:
                    for s in range(2):
                        dve.wait_ge(gated, 2 * i + (s + 1))
                        dve.wait_ge(w_free, 2 * i + (s + 1))
                        dve.tensor_tensor(gu[:, 2 * i + s, :], sg[:, s, :], gate_up[s][1][:, 0:T],
                                          ALU.mult).then_inc(gu_free, 1)
                with dve.Fori(0, DC // 2) as i:
                    for s in range(2):
                        dve.wait_ge(wd_free, 2 * i + (s + 1))
                        dve.scalar_tensor_tensor(x[:, 2 * i + s, :], down[s][:, 0:T], 0.5, x[:, 2 * i + s, :],
                                                 ALU.mult, ALU.add).then_inc(down_free, 1)


def project_stage(nc, w, n, h, write):
    tokens = h.shape[2]
    with ExitStack() as ctx:
        wt = ctx.enter_context(sbuf(nc, "wt", [P, 4, D], F32))
        ps = [ctx.enter_context(psum(nc, f"ps{i}", [P, 512], F32)) for i in range(2)]
        with stage(nc, "w_in0", "w_in1", "projected", "written") as (block, w_in0, w_in1, projected, written):
            w_in = (w_in0, w_in1)

            @block.sync
            def _(sp):
                for s in range(2):
                    sp.dma_start(wt[:, s, :], w[s]).then_inc(w_in[s], 16)
                with sp.Fori(1, n // 2) as i:
                    for s in range(2):
                        sp.wait_ge(projected, 2 * i + (s - 1))
                        sp.dma_start(wt[:, s, :], w[2 * i + s]).then_inc(w_in[s], 16)

            @block.tensor
            def _(pe):
                with pe.Fori(0, n // 2) as i:
                    for s in range(2):
                        pe.wait_ge(w_in[s], 16 * i + 16)
                        pe.wait_ge(written, 2 * i + (s + 1))
                        for c in range(DC):
                            last = pe.matmul(ps[s][:, 0:tokens], wt[:, s, c * P:(c + 1) * P], h[:, c, :],
                                             start=(c == 0), stop=(c == DC - 1))
                        last.then_inc(projected, 1)

            @block.vector
            def _(dve):
                dve.sem_inc(written, 2)
                with dve.Fori(0, n // 2) as i:
                    for s in range(2):
                        dve.wait_ge(projected, 2 * i + (s + 1))
                        write(dve, 2 * i + s, ps[s], written)


def mixer_gates(nc, k, h, proj, cols, lb, wba, wrg, b):
    col = lambda name, i=0: cols[:, COL[name][0] + i:COL[name][0] + i + 1]
    with ExitStack() as ctx:
        ba = ctx.enter_context(psum(nc, "ba", [P, TT, T], F32))
        cum = ctx.enter_context(psum(nc, "cum", [P, TT, T], F32))
        tmp = ctx.enter_context(sbuf(nc, "tmp", [P, 6, TT, 4], F32))
        ea = ctx.enter_context(sbuf(nc, "ea", [P, 4], F32))
        with stage(nc, "projected", "prepared", "exped", "logged", "betad", "decayed", "summed", "own",
                   "ea_ready") as (
                block, projected, prepared, exped, logged, betad, decayed, summed, own, ea_ready):
            @block.tensor
            def _(pe):
                for t in range(TT):
                    for c in range(DC):
                        last = pe.matmul(ba[:, t, 0:8], h[:, c, t * P:(t + 1) * P], wba[:, c, :],
                                         start=(c == 0), stop=(c == DC - 1))
                last.then_inc(projected, 1)
                pe.wait_ge(decayed, 1)
                for t in range(TT):
                    last = pe.matmul(cum[:, t, 0:4], k.tri_incl, b.g[:, t, :], start=True, stop=True)
                last.then_inc(summed, 1)

            @block.vector
            def _(dve):
                order = Order(dve, own)
                dve.wait_ge(projected, 1)
                dt = cols[:, COL["gd_dt_bias"][0]:COL["gd_dt_bias"][0] + 4]
                for t in range(TT):
                    last = dve.tensor_tensor(tmp[:, 0, t, :], ba[:, t, 4:8], dt, ALU.add)
                order(last)
                order(dve.tensor_scalar(tmp[:, 1], tmp[:, 0], -1.0, None, ALU.mult))
                dve.tensor_tensor(tmp[:, 2], tmp[:, 0], tmp[:, 1], ALU.min).then_inc(prepared, 1)
                dve.wait_ge(exped, 1)
                dve.wait_ge(logged, 1)
                order(dve.scalar_tensor_tensor(tmp[:, 4], tmp[:, 0], 0.0, tmp[:, 3], ALU.max, ALU.add))
                dve.wait_ge(ea_ready, 1)
                for t in range(TT):
                    last = dve.scalar_tensor_tensor(b.g[:, t, :], tmp[:, 4, t, :], -1.0, ea[:],
                                                    ALU.mult, ALU.mult)
                last.then_inc(decayed, 1)
                dve.wait_ge(summed, 1)
                dve.tensor_copy(b.cum[:], cum[:, :, 0:4])

            @block.scalar
            def _(act):
                act.activation(ea[:], cols[:, COL["gd_a_log"][0]:COL["gd_a_log"][0] + 4],
                               ACT.Exp).then_inc(ea_ready, 1)
                act.wait_ge(prepared, 1)
                act.activation(tmp[:, 3], tmp[:, 2], ACT.Exp).then_inc(exped, 1)
                act.wait_ge(exped, 1)
                act.activation(tmp[:, 3], tmp[:, 3], ACT.Ln, bias=1.0).then_inc(logged, 1)
                act.activation(b.beta[:], ba[:, :, 0:4], ACT.Sigmoid)

    with ExitStack() as ctx:
        conv = ctx.enter_context(sbuf(nc, "conv", [P, 14, T], F32))
        with stage(nc, "own") as (block, own):
            @block.vector
            def _(dve):
                n = 0
                chunks = [(GD_Q + c, c) for c in range(12)] + [(RG_X + c, 12 + c) for c in range(2)]
                for j in range(CONV_W):
                    for src, c in chunks:
                        base = COL["gd_conv"][0] if c < 12 else COL["rg_conv"][0] - 12 * CONV_W
                        w = cols[:, base + c * CONV_W + j:base + c * CONV_W + j + 1]
                        tap = proj[:, src, j:j + T]
                        if j == 0:
                            ins = dve.tensor_scalar(conv[:, c, :], tap, w, None, ALU.mult)
                        else:
                            dve.wait_ge(own, n - len(chunks) + 1)
                            ins = dve.scalar_tensor_tensor(conv[:, c, :], tap, w, conv[:, c, :],
                                                           ALU.mult, ALU.add)
                        ins.then_inc(own, 1)
                        n += 1

            @block.scalar
            def _(act):
                for c in range(12):
                    act.wait_ge(own, 14 * (CONV_W - 1) + c + 1)
                    act.activation(proj[:, GD_Q + c, PAD:PAD + T], conv[:, c, :], ACT.Silu)
                for c in range(2):
                    act.wait_ge(own, 14 * (CONV_W - 1) + 12 + c + 1)
                    act.activation(b.xc[:, c, :], conv[:, 12 + c, :], ACT.Identity, bias=col("rg_conv_b", c))
                for c in (HG_Q, HG_Q + 1, HG_G, HG_G + 1, GD_Z, GD_Z + 1, GD_Z + 2, GD_Z + 3):
                    act.activation(proj[:, c, PAD:PAD + T], proj[:, c, PAD:PAD + T], ACT.Silu)
                for c in range(2):
                    act.activation(b.f[:, c, :], proj[:, HG_F + c, PAD:PAD + T], ACT.Sigmoid)

    with ExitStack() as ctx:
        sq = ctx.enter_context(sbuf(nc, "sq", [P, 8, T], F32))
        inv = ctx.enter_context(sbuf(nc, "inv", [P, 8, T], F32))
        norm = [ctx.enter_context(psum(nc, f"norm{i}", [P, 2, T], F32)) for i in range(4)]
        with stage(nc, "squared", "summed", "inverse", "rooted", "own") as (
                block, squared, summed, inverse, rooted, own):
            qk = proj[:, GD_Q:GD_Q + 8, PAD:PAD + T]

            @block.scalar
            def _(act):
                act.activation(sq[:], qk, ACT.Square).then_inc(squared, 1)
                act.wait_ge(inverse, 1)
                act.activation(inv[:], inv[:], ACT.Sqrt).then_inc(rooted, 1)

            @block.tensor
            def _(pe):
                pe.wait_ge(squared, 1)
                for c in range(8):
                    last = pe.matmul(norm[c // 2][:, c % 2, :], k.ones, sq[:, c, :], start=True, stop=True)
                last.then_inc(summed, 1)

            @block.vector
            def _(dve):
                order = Order(dve, own)
                for c in range(2):
                    dve.tensor_scalar(b.f[:, c, :], b.f[:, c, :], lb[:, 2 + c:3 + c], lb[:, c:c + 1],
                                      ALU.mult, ALU.add).then_inc(own, 1)
                dve.wait_ge(own, 2)
                order.n = 2
                for c in range(2):
                    dve.tensor_scalar(b.k[:, c, :], b.f[:, c, :], -1.0, 1.0, ALU.mult, ALU.add)
                    dve.tensor_scalar(b.q[:, c, :], proj[:, HG_Q + c, PAD:PAD + T], HG_DK ** -0.5, None,
                                      ALU.mult)
                    for r in range(2):
                        dve.tensor_copy(b.f0[:, c, r, 1:T], b.f[:, c, 1:T])
                dve.memset(b.f0[:, :, :, 0:1], 0.0)
                dve.wait_ge(summed, 1)
                for c in range(4):
                    last = dve.tensor_scalar(inv[:, 2 * c:2 * c + 2, :], norm[c][:], EPS, None, ALU.add)
                order(last)
                dve.reciprocal(inv[:], inv[:]).then_inc(inverse, 1)
                dve.wait_ge(rooted, 1)
                dve.scalar_tensor_tensor(proj[:, GD_Q:GD_Q + 4, PAD:PAD + T], proj[:, GD_Q:GD_Q + 4, PAD:PAD + T],
                                         float(P) ** -0.5, inv[:, 0:4, :], ALU.mult, ALU.mult)
                dve.tensor_tensor(proj[:, GD_K:GD_K + 4, PAD:PAD + T], proj[:, GD_K:GD_K + 4, PAD:PAD + T],
                                  inv[:, 4:8, :], ALU.mult)


def picks_stage(nc, k, picks):
    with stage(nc, "made") as (block, made):
        @block.gpsimd
        def _(pool):
            for hh in range(2):
                pool.tensor_copy(picks[:, :, hh * HEAD:(hh + 1) * HEAD],
                                 k.ident[:, hh * HEAD:(hh + 1) * HEAD].unsqueeze(2).to_broadcast([P, HEAD, HEAD]))


def hgrn2_stage(nc, k, proj, b, picks, pair):
    V = HEAD
    with ExitStack() as ctx:
        kv = ctx.enter_context(sbuf(nc, "kv", [P, 2, 2, T], F32))
        st = ctx.enter_context(sbuf(nc, "st", [P, 2, 2, T], F32))
        qs = ctx.enter_context(sbuf(nc, "qs", [P, 2, 2, T], F32))
        rows = [ctx.enter_context(psum(nc, f"rows{i}", [P, 2, T], F32)) for i in range(2)]
        out = ctx.enter_context(psum(nc, "out", [P, 512], F32))
        steps = V // 2
        with stage(nc, "spread", "outer", "scanned", "read", "reduced") as (
                block, spread, outer, scanned, read, reduced):
            @block.tensor
            def _(pe):
                def spread_rows(n):
                    if n >= 2:
                        pe.wait_ge(outer, n - 1)
                    for j in range(2):
                        v = 2 * n + j
                        last = pe.matmul(rows[n % 2][:, j, :], picks[:, v, :], proj[:, HG_I + pair, PAD:PAD + T],
                                         start=True, stop=True)
                    last.then_inc(spread, 1)

                spread_rows(0)
                for n in range(steps):
                    if n + 1 < steps:
                        spread_rows(n + 1)
                    pe.wait_ge(read, n + 1)
                    for j in range(2):
                        v = 2 * n + j
                        last = pe.matmul(out[:, 0:T], k.slide[:, V - 1 - v:V - 1 - v + P], qs[:, n % 2, j, :],
                                         start=(v == 0), stop=(v == V - 1))
                    last.then_inc(reduced, 1)

            @block.vector
            def _(dve):
                kk = b.k[:, pair, :].unsqueeze(1).to_broadcast([P, 2, T])
                f0 = b.f0[:, pair, :, :].rearrange("p r t -> p (r t)")

                def outer_step(n):
                    dve.wait_ge(spread, n + 1)
                    if n >= 2:
                        dve.wait_ge(scanned, n - 1)
                    dve.tensor_tensor(kv[:, n % 2], rows[n % 2][:], kk, ALU.mult).then_inc(outer, 1)

                outer_step(0)
                for n in range(steps):
                    if n + 1 < steps:
                        outer_step(n + 1)
                    dve.wait_ge(outer, n + 1)
                    if n >= 2:
                        dve.wait_ge(read, n - 1)
                    dve.tensor_tensor_scan(st[:, n % 2].rearrange("p r t -> p (r t)"), f0,
                                           kv[:, n % 2].rearrange("p r t -> p (r t)"), 0.0,
                                           ALU.mult, ALU.add).then_inc(scanned, 1)
                dve.wait_ge(reduced, steps)
                dve.tensor_copy(b.o[:, pair, :], out[:, 0:T])

            @block.gpsimd
            def _(pool):
                qq = b.q[:, pair, :].unsqueeze(1).to_broadcast([P, 2, T])
                for n in range(steps):
                    pool.wait_ge(scanned, n + 1)
                    if n >= 2:
                        pool.wait_ge(reduced, n - 1)
                    pool.tensor_tensor(qs[:, n % 2], st[:, n % 2], qq, ALU.mult).then_inc(read, 1)


def head_norm_stage(nc, k, o, n, summing, width, weight, proj, gate, y):
    with ExitStack() as ctx:
        sq = ctx.enter_context(sbuf(nc, "sq", [P, n, T], F32))
        ms = [ctx.enter_context(psum(nc, f"ms{i}", [P, 2, T], F32)) for i in range(n // 2)]
        with stage(nc, "squared", "summed", "inverse", "rooted", "own") as (
                block, squared, summed, inverse, rooted, own):
            @block.scalar
            def _(act):
                act.activation(sq[:], o[:, 0:n, :], ACT.Square).then_inc(squared, 1)
                act.wait_ge(inverse, 1)
                act.activation(sq[:], sq[:], ACT.Sqrt).then_inc(rooted, 1)

            @block.tensor
            def _(pe):
                pe.wait_ge(squared, 1)
                for c in range(n):
                    last = pe.matmul(ms[c // 2][:, c % 2, :], summing, sq[:, c, :], start=True, stop=True)
                last.then_inc(summed, 1)

            @block.vector
            def _(dve):
                order = Order(dve, own)
                dve.wait_ge(summed, 1)
                for c in range(n // 2):
                    last = dve.tensor_scalar(sq[:, 2 * c:2 * c + 2, :], ms[c][:], 1.0 / width, EPS,
                                             ALU.mult, ALU.add)
                order(last)
                dve.reciprocal(sq[:], sq[:]).then_inc(inverse, 1)
                dve.wait_ge(rooted, 1)
                order(dve.scalar_tensor_tensor(y, o[:, 0:n, :], weight, sq[:], ALU.mult, ALU.mult))
                dve.tensor_tensor(y, y, proj[:, gate:gate + n, PAD:PAD + T], ALU.mult)


def delta_stages(nc, k, proj, b):
    H = GD_HEADS
    with ExitStack() as ctx:
        sb = lambda name, shape: ctx.enter_context(sbuf(nc, name, shape, F32))
        ktok, vtok = sb("ktok", [P, TT, H, P]), sb("vtok", [P, TT, H, P])
        crow, brow = sb("crow", [P, TT, H, P]), sb("brow", [P, TT, H, P])
        decay, sct = sb("decay", [P, TT, H, P]), sb("sct", [P, TT, H, P])
        low, lowt = sb("low", [P, TT, H, P]), sb("lowt", [P, TT, H, P])
        pst = [ctx.enter_context(psum(nc, f"pst{i}", [P, H, P], F32)) for i in range(8)]
        with stage(nc, "moved") as (block, moved):
            jobs = [(ktok, "k"), (vtok, "v"), (crow, "cum"), (brow, "beta")]

            @block.tensor
            def _(pe):
                for n, (_dst, what) in enumerate(jobs):
                    for t in range(TT):
                        tok = slice(PAD + t * P, PAD + (t + 1) * P)
                        for hh in range(H):
                            o = pst[2 * n + t][:, hh, :]
                            if what == "k":
                                last = pe.transpose(o, proj[:, GD_K + hh, tok], k.ident)
                            elif what == "v":
                                last = pe.transpose(o, proj[:, GD_V + hh, tok], k.ident)
                            elif what == "cum":
                                last = pe.matmul(o, b.g[:, t, hh:hh + 1].to_broadcast([P, P]), k.tri_incl,
                                                 start=True, stop=True)
                            else:
                                last = pe.matmul(o, b.beta[:, t, hh:hh + 1].to_broadcast([P, P]), k.ident,
                                                 start=True, stop=True)
                        last.then_inc(moved, 1)

            @block.vector
            def _(dve):
                for n in (0, 2):
                    for t in range(TT):
                        dve.wait_ge(moved, 2 * n + t + 1)
                        dve.tensor_copy(jobs[n][0][:, t], pst[2 * n + t][:])

            @block.scalar
            def _(act):
                for n in (1, 3):
                    for t in range(TT):
                        act.wait_ge(moved, 2 * n + t + 1)
                        act.activation(jobs[n][0][:, t], pst[2 * n + t][:], ACT.Copy)

        with stage(nc, "products", "differenced", "exped", "masked", "own", "lowered", "flipped") as (
                block, products, differenced, exped, masked, own, lowered, flipped):
            @block.tensor
            def _(pe):
                for t in range(TT):
                    tok = slice(PAD + t * P, PAD + (t + 1) * P)
                    for hh in range(H):
                        pe.matmul(pst[2 * t][:, hh, :], proj[:, GD_K + hh, tok], proj[:, GD_K + hh, tok],
                                  start=True, stop=True)
                    for hh in range(H):
                        last = pe.matmul(pst[2 * t + 1][:, hh, :], proj[:, GD_K + hh, tok],
                                         proj[:, GD_Q + hh, tok], start=True, stop=True)
                    last.then_inc(products, 1)
                for t in range(TT):
                    pe.wait_ge(lowered, t + 1)
                    for hh in range(H):
                        last = pe.transpose(pst[4 + t][:, hh, :], lowt[:, t, hh, :], k.ident)
                    last.then_inc(flipped, 1)

            @block.vector
            def _(dve):
                order = Order(dve, own)
                for t in range(TT):
                    for hh in range(H):
                        last = dve.tensor_scalar(decay[:, t, hh, :], crow[:, t, hh, :], b.cum[:, t, hh:hh + 1], 0.0,
                                                 ALU.subtract, ALU.min)
                    last.then_inc(differenced, 1)
                for t in range(TT):
                    incl = k.tri_incl.unsqueeze(1).to_broadcast([P, H, P])
                    strict = k.tri_strict.unsqueeze(1).to_broadcast([P, H, P])
                    dve.wait_ge(exped, t + 1)
                    order(dve.tensor_tensor(decay[:, t], decay[:, t], incl, ALU.mult))
                    dve.wait_ge(products, t + 1)
                    dve.tensor_tensor(sct[:, t], pst[2 * t + 1][:], decay[:, t], ALU.mult)
                    order(dve.tensor_tensor(lowt[:, t], pst[2 * t][:], brow[:, t], ALU.mult))
                    order(dve.tensor_tensor(lowt[:, t], lowt[:, t], decay[:, t], ALU.mult))
                    dve.tensor_tensor(lowt[:, t], lowt[:, t], strict, ALU.mult).then_inc(lowered, 1)

            @block.scalar
            def _(act):
                for t in range(TT):
                    act.wait_ge(differenced, t + 1)
                    act.activation(decay[:, t], decay[:, t], ACT.Exp).then_inc(exped, 1)
                for t in range(TT):
                    act.wait_ge(flipped, t + 1)
                    act.activation(low[:, t], pst[4 + t][:], ACT.Copy)

        xi, xit, yy = sb("xi", [P, TT, H, P]), sb("xit", [P, TT, H, P]), sb("yy", [P, TT, H, P])
        bm, bmt = sb("bm", [P, TT, H, P]), sb("bmt", [P, TT, H, P])
        LEVELS = 7
        wide = lambda ap: ap.unsqueeze(1).to_broadcast([P, H, P])
        with stage(nc, "cut", "ydone", "ycopied", "zdone", "updated", "own") as (
                block, cut, ydone, ycopied, zdone, updated, own):
            @block.vector
            def _(dve):
                order = Order(dve, own)
                for t in range(TT):
                    order(dve.tensor_tensor(bm[:, t], low[:, t], wide(k.level(0)), ALU.mult))
                    order(dve.tensor_tensor(bmt[:, t], lowt[:, t], wide(k.level_t(0)), ALU.mult))
                    dve.tensor_tensor(xi[:, t], wide(k.ident), bm[:, t], ALU.subtract).then_inc(updated, 1)
                    dve.tensor_tensor(xit[:, t], wide(k.ident), bmt[:, t], ALU.subtract).then_inc(updated, 1)
                dve.wait_ge(updated, 2 * TT)
                for lev in range(1, LEVELS):
                    for t in range(TT):
                        if lev > 1:
                            dve.wait_ge(ydone, (lev - 2) * TT + t + 1)
                        dve.tensor_tensor(bmt[:, t], lowt[:, t], wide(k.level_t(lev)), ALU.mult).then_inc(cut, 1)
                    for t in range(TT):
                        n = (lev - 1) * TT + t
                        dve.wait_ge(zdone, n + 1)
                        dve.tensor_tensor(xi[:, t], xi[:, t], pst[4 * t + 1][:], ALU.subtract).then_inc(updated, 1)
                        dve.tensor_tensor(xit[:, t], xit[:, t], pst[4 * t + 2][:],
                                          ALU.subtract).then_inc(updated, 1)

            @block.tensor
            def _(pe):
                for lev in range(1, LEVELS):
                    for t in range(TT):
                        n = (lev - 1) * TT + t
                        pe.wait_ge(cut, n + 1)
                        pe.wait_ge(updated, 2 * n + 2)
                        for hh in range(H):
                            last = pe.matmul(pst[4 * t][:, hh, :], bmt[:, t, hh, :], xi[:, t, hh, :],
                                             start=True, stop=True)
                        last.then_inc(ydone, 1)
                    for t in range(TT):
                        n = (lev - 1) * TT + t
                        pe.wait_ge(ycopied, n + 1)
                        for hh in range(H):
                            pe.matmul(pst[4 * t + 1][:, hh, :], xit[:, t, hh, :], yy[:, t, hh, :],
                                      start=True, stop=True)
                        for hh in range(H):
                            last = pe.matmul(pst[4 * t + 2][:, hh, :], yy[:, t, hh, :], xit[:, t, hh, :],
                                             start=True, stop=True)
                        last.then_inc(zdone, 1)

            @block.scalar
            def _(act):
                for lev in range(1, LEVELS):
                    for t in range(TT):
                        n = (lev - 1) * TT + t
                        act.wait_ge(ydone, n + 1)
                        if lev > 1:
                            act.wait_ge(zdone, n - TT + 1)
                        act.activation(yy[:, t], pst[4 * t][:], ACT.Copy).then_inc(ycopied, 1)

        qe, vb, kbe, kl = bm, bmt, yy, low
        erow = crow
        ecol, lcol = sb("ecol", [P, TT, H]), sb("lcol", [P, TT, H])
        with stage(nc, "exped", "last", "own") as (block, exped, lasts, own):
            @block.vector
            def _(dve):
                order = Order(dve, own)
                for t in range(TT):
                    order(dve.tensor_tensor(lcol[:, t], crow[:, t, :, P - 1], b.cum[:, t], ALU.subtract))
                lasts_ready = dve.tensor_copy(b.last[:], crow[:, :, :, P - 1])
                lasts_ready.then_inc(lasts, 1)
                dve.wait_ge(exped, 1)
                order(dve.tensor_tensor(qe[:], erow[:], proj_q(proj), ALU.mult))
                for t in range(TT):
                    order(dve.tensor_tensor(ecol[:, t], ecol[:, t], b.beta[:, t], ALU.mult))
                    for hh in range(H):
                        dve.tensor_scalar(vb[:, t, hh, :], vtok[:, t, hh, :], b.beta[:, t, hh:hh + 1], None, ALU.mult)
                        dve.tensor_scalar(kbe[:, t, hh, :], ktok[:, t, hh, :], ecol[:, t, hh:hh + 1], None, ALU.mult)
                        dve.tensor_scalar(kl[:, t, hh, :], ktok[:, t, hh, :], lcol[:, t, hh:hh + 1], None, ALU.mult)

            @block.scalar
            def _(act):
                act.wait_ge(lasts, 1)
                act.activation(erow[:], crow[:], ACT.Exp)
                act.activation(ecol[:], b.cum[:], ACT.Exp)
                act.activation(lcol[:], lcol[:], ACT.Exp)
                act.activation(b.last[:], b.last[:], ACT.Exp).then_inc(exped, 1)

        wt, vn, state = decay, vtok, ktok[:, 0]
        with stage(nc, "w_done", "w_copied", "v_done", "v_copied", "o_done", "s_done", "s_copied") as (
                block, w_done, w_copied, v_done, v_copied, o_done, s_done, s_copied):
            @block.tensor
            def _(pe):
                for t in range(TT):
                    for hh in range(H):
                        last = pe.matmul(pst[t][:, hh, :], kbe[:, t, hh, :], xit[:, t, hh, :], start=True, stop=True)
                    last.then_inc(w_done, 1)
                for t in range(TT):
                    if t:
                        pe.wait_ge(w_copied, t + 1)
                        pe.wait_ge(s_copied, t)
                    for hh in range(H):
                        last = pe.matmul(pst[2 + t][:, hh, :], xit[:, t, hh, :], vb[:, t, hh, :],
                                         start=True, stop=(t == 0))
                        if t:
                            last = pe.matmul(pst[2 + t][:, hh, :], wt[:, t, hh, :], state[:, hh, :],
                                             start=False, stop=True)
                    last.then_inc(v_done, 1)
                    pe.wait_ge(v_copied, t + 1)
                    if t + 1 < TT:
                        for hh in range(H):
                            last = pe.matmul(pst[6 + t][:, hh, :], kl[:, t, hh, :], vn[:, t, hh, :],
                                             start=True, stop=True)
                        last.then_inc(s_done, 1)
                    for hh in range(H):
                        last = pe.matmul(pst[4 + t][:, hh, :], vn[:, t, hh, :], sct[:, t, hh, :],
                                         start=True, stop=(t == 0))
                        if t:
                            last = pe.matmul(pst[4 + t][:, hh, :], state[:, hh, :], qe[:, t, hh, :],
                                             start=False, stop=True)
                    last.then_inc(o_done, 1)

            @block.scalar
            def _(act):
                for t in range(TT):
                    act.wait_ge(w_done, t + 1)
                    act.activation(wt[:, t], pst[t][:], ACT.Copy, scale=-1.0).then_inc(w_copied, 1)
                for t in range(TT):
                    act.wait_ge(o_done, t + 1)
                    act.activation(b.ogd[:, :, t * P:(t + 1) * P], pst[4 + t][:], ACT.Copy)

            @block.vector
            def _(dve):
                for t in range(TT):
                    dve.wait_ge(v_done, t + 1)
                    dve.tensor_copy(vn[:, t], pst[2 + t][:]).then_inc(v_copied, 1)
                    if t + 1 < TT:
                        dve.wait_ge(s_done, t + 1)
                        dve.tensor_copy(state, pst[6 + t][:]).then_inc(s_copied, 1)


def proj_q(proj):
    return proj[:, GD_Q:GD_Q + GD_HEADS, PAD:PAD + T].rearrange("p h (t c) -> p t h c", t=TT)


def rg_stage(nc, k, proj, cols, b, wrg, y):
    at = lambda name: COL[name][0]
    with ExitStack() as ctx:
        sb = lambda name, shape: ctx.enter_context(sbuf(nc, name, shape, F32))
        gates = sb("gates", [P, 2, 2, T])
        sp_ = sb("softplus", [P, 4, 2])
        la, a, th, bx = sb("la", [P, 2, T]), sb("a", [P, 2, T]), sb("th", [P, 2, T]), sb("bx", [P, 2, T])
        ge = sb("ge", [P, 2, T])
        ps = [ctx.enter_context(psum(nc, f"ps{i}", [P, 2, T], F32)) for i in range(2)]
        with stage(nc, "multiplied", "absed", "logged", "sigmoided", "coefficient", "exped", "ready",
                   "rooted", "own", "gelued", "aown") as (
                block, multiplied, absed, logged, sigmoided, coefficient, exped, ready, rooted, own,
                gelued, aown):
            @block.tensor
            def _(pe):
                for m in range(2):
                    for c in range(2):
                        last = pe.matmul(ps[m][:, c, :], wrg[:, m, c, :], b.xc[:, c, :], start=True, stop=True)
                last.then_inc(multiplied, 1)

            @block.vector
            def _(dve):
                order = Order(dve, own)
                lam = cols[:, at("rg_lambda"):at("rg_lambda") + 2]
                order(dve.tensor_scalar(sp_[:, 0], lam, -1.0, None, ALU.mult))
                dve.tensor_tensor(sp_[:, 1], sp_[:, 0], lam, ALU.min).then_inc(absed, 1)
                dve.wait_ge(logged, 1)
                order(dve.scalar_tensor_tensor(sp_[:, 3], sp_[:, 0], 0.0, sp_[:, 2], ALU.max, ALU.add))
                order(dve.tensor_scalar(sp_[:, 3], sp_[:, 3], -RG_C, None, ALU.mult))
                dve.wait_ge(sigmoided, 1)
                for c in range(2):
                    last = dve.tensor_scalar(la[:, c, :], gates[:, 0, c, :], sp_[:, 3, c:c + 1], None, ALU.mult)
                last.then_inc(coefficient, 1)
                order(dve.tensor_tensor(bx[:], gates[:, 1], b.xc[:], ALU.mult))
                dve.wait_ge(exped, 1)
                order(dve.tensor_tensor(la[:], a[:], a[:], ALU.mult))
                order(dve.tensor_scalar(la[:], la[:], 1.0, None, ALU.add))
                dve.scalar_tensor_tensor(th[:], th[:], -1.0, la[:], ALU.mult, ALU.mult).then_inc(ready, 1)
                dve.wait_ge(rooted, 1)
                order(dve.tensor_tensor(bx[:], bx[:], th[:], ALU.mult))
                for c in range(2):
                    last = dve.tensor_tensor_scan(la[:, c, :], a[:, c, :], bx[:, c, :], 0.0, ALU.mult, ALU.add)
                order(last)
                dve.wait_ge(gelued, 1)
                dve.tensor_tensor(y, la[:], ge[:], ALU.mult)

            @block.scalar
            def _(act):
                order = Order(act, aown)
                act.wait_ge(absed, 1)
                order(act.activation(sp_[:, 2], sp_[:, 1], ACT.Exp))
                act.activation(sp_[:, 2], sp_[:, 2], ACT.Ln, bias=1.0).then_inc(logged, 1)
                act.wait_ge(multiplied, 1)
                for m, name in enumerate(("rg_br", "rg_bi")):
                    for c in range(2):
                        last = act.activation(gates[:, m, c, :], ps[m][:, c, :], ACT.Sigmoid,
                                              bias=cols[:, at(name) + c:at(name) + c + 1])
                last.then_inc(sigmoided, 1)
                act.wait_ge(coefficient, 1)
                act.activation(a[:], la[:], ACT.Exp)
                act.activation(th[:], la[:], ACT.Tanh).then_inc(exped, 1)
                act.activation(ge[:], proj[:, RG_GATE:RG_GATE + 2, PAD:PAD + T], ACT.Gelu_apprx_tanh).then_inc(gelued, 1)
                act.wait_ge(ready, 1)
                act.activation(th[:], th[:], ACT.Sqrt).then_inc(rooted, 1)


def lower_bounds(nc, raw, lb):
    with ExitStack() as ctx:
        t = ctx.enter_context(sbuf(nc, "lbt", [P, 6, 2], F32))
        with stage(nc, "centred", "exped", "own") as (block, centred, exped, own):
            @block.vector
            def _(dve):
                order = Order(dve, own)
                order(dve.tensor_tensor(t[:, 0], raw[:, 0], raw[:, 1], ALU.max))
                order(dve.tensor_tensor(t[:, 1], raw[:, 0], t[:, 0], ALU.subtract))
                dve.tensor_tensor(t[:, 2], raw[:, 1], t[:, 0], ALU.subtract).then_inc(centred, 1)
                dve.wait_ge(exped, 1)
                order(dve.tensor_tensor(t[:, 0], t[:, 3], t[:, 4], ALU.add))
                order(dve.reciprocal(t[:, 0], t[:, 0]))
                order(dve.memset(lb[:, 0, 0:2], 0.0))
                order(dve.memset(lb[:, 0, 2:4], 1.0))
                order(dve.tensor_tensor(lb[:, 1, 0:2], t[:, 4], t[:, 0], ALU.mult))
                dve.tensor_scalar(lb[:, 1, 2:4], lb[:, 1, 0:2], -1.0, 1.0, ALU.mult, ALU.add)

            @block.scalar
            def _(act):
                act.wait_ge(centred, 1)
                act.activation(t[:, 3:5], t[:, 1:3], ACT.Exp).then_inc(exped, 1)


def first_block(nc, k, x, d):
    with ExitStack() as ctx:
        sb = lambda name, shape: ctx.enter_context(sbuf(nc, name, shape, F32))
        h = sb("h", [P, DC, T])
        cols, lb, lbl, raw = sb("cols", [P, N_COLS]), sb("lb", [P, DEPTH, 4]), sb("lbl", [P, 4]), sb("raw", [P, DEPTH, 2])
        load_stage(nc, [(raw[:], d.hg_lb)])
        lower_bounds(nc, raw, lb)
        with nc.Fori(0, DEPTH) as layer:
            with stage(nc, "loaded") as (block, loaded):
                @block.sync
                def _(sp):
                    sp.dma_start(cols[:], d.cols[layer]).then_inc(loaded, 16)
                    sp.wait_ge(loaded, 16)

                @block.vector
                def _(dve):
                    dve.tensor_copy(lbl[:], lb[:, layer, :])
            gain = lambda name: cols[:, COL[name][0]:COL[name][0] + DC]
            norm_stage(nc, k, x, gain("norm_ffn1"), h)
            ffn_stage(nc, k, h, x, d.wg0[layer], d.wu0[layer], d.wd0[layer])
            norm_stage(nc, k, x, gain("norm_mix"), h)
            mixer(nc, k, h, x, cols, lbl, layer, d)
            norm_stage(nc, k, x, gain("norm_ffn2"), h)
            ffn_stage(nc, k, h, x, d.wg1[layer], d.wu1[layer], d.wd1[layer])


def mixer(nc, k, h, x, cols, lb, layer, d):
    with ExitStack() as ctx:
        sb = lambda name, shape: ctx.enter_context(sbuf(nc, name, shape, F32))
        proj = sb("proj", [P, N_PROJ, TPAD])
        wba, wrg = sb("wba", [P, DC, 8]), sb("wrg", [P, 2, 2, P])
        b = Buffers()
        b.g, b.cum, b.beta, b.last = (sb(n, [P, TT, 4]) for n in ("g", "cumt", "beta", "last"))
        b.xc, b.f, b.k, b.q, b.o = (sb(n, [P, 2, T]) for n in ("xc", "fg", "kg", "qg", "o_hg"))
        b.f0, b.ogd = sb("f0", [P, 2, 2, T]), sb("ogd", [P, GD_HEADS, T])
        with stage(nc, "loaded") as (block, loaded):
            @block.sync
            def _(sp):
                sp.dma_start(wba[:], d.wba[layer]).then_inc(loaded, 16)
                sp.dma_start(wrg[:], d.wrg[layer]).then_inc(loaded, 16)
                sp.wait_ge(loaded, 32)

            @block.vector
            def _(dve):
                dve.memset(proj[:, :, 0:PAD], 0.0)
        project_stage(nc, d.w_in[layer], N_PROJ, h,
                      lambda dve, n, ps, done: dve.tensor_copy(proj[:, n, PAD:PAD + T], ps[:, 0:T]).then_inc(done, 1))
        mixer_gates(nc, k, h, proj, cols, lb, wba, wrg, b)
        y = h
        rg_stage(nc, k, proj, cols, b, wrg, y[:, 6:8, :])
        delta_stages(nc, k, proj, b)
        with ExitStack() as own:
            picks = own.enter_context(sbuf(nc, "picks", [P, HEAD, P], F32))
            picks_stage(nc, k, picks)
            for pair in range(HG_PAIRS):
                hgrn2_stage(nc, k, proj, b, picks, pair)
        head_norm_stage(nc, k, b.o, 2, k.halves, HG_DK, cols[:, COL["hg_norm"][0]:COL["hg_norm"][0] + 1],
                        proj, HG_G, y[:, 0:2, :])
        head_norm_stage(nc, k, b.ogd, 4, k.ones, P, cols[:, COL["gd_norm"][0]:COL["gd_norm"][0] + 1],
                        proj, GD_Z, y[:, 2:6, :])
        project_stage(nc, d.w_out[layer], DC, y,
                      lambda dve, n, ps, done: dve.tensor_tensor(x[:, n, :], ps[:, 0:T], x[:, n, :],
                                                                 ALU.add).then_inc(done, 1))


def modulation(nc, k, sc, w_mod, cols, layer, mod, gains):
    b_mod = COL2["b_mod"][0] + 48 * layer
    project_stage(nc, w_mod, 48, sc,
                  lambda dve, n, ps, done: dve.tensor_scalar(mod[:, :, n], ps[:, 0:2], cols[:, bass.ds(n + b_mod, 1)],
                                                             None, ALU.add).then_inc(done, 1))
    with stage(nc, "own") as (block, own):
        @block.vector
        def _(dve):
            for m, name in enumerate(("norm1", "norm2")):
                a = COL2[name][0] + DC * layer
                g = cols[:, a:a + DC].unsqueeze(1).to_broadcast([P, 2, DC])
                dve.scalar_tensor_tensor(gains[:, m], mod[:, :, (3 * m + 1) * DC:(3 * m + 2) * DC], 1.0, g,
                                         ALU.add, ALU.mult)


def qkv_stage(nc, k, h, loads, nq, tq, rope, q, kt, v):
    n = nq + 2
    with ExitStack() as ctx:
        wt = ctx.enter_context(sbuf(nc, "wt", [P, n, D], F32))
        raw = ctx.enter_context(sbuf(nc, "raw", [P, nq + 1, T], F32))
        part = ctx.enter_context(sbuf(nc, "part", [P, nq + 1, 2, T], F32))
        ps = [ctx.enter_context(psum(nc, f"ps{i}", [P, 512], F32)) for i in range(n)]
        rot = [ctx.enter_context(psum(nc, f"rot{i}", [P, 512], F32)) for i in range(nq + 1)] if rope else None
        tk = 2 * T
        with stage(nc, "loaded", "projected", "raw_ready", "rotated", "own") as (
                block, loaded, projected, raw_ready, rotated, own):
            @block.sync
            def _(sp):
                for i, src in enumerate(loads):
                    sp.dma_start(wt[:, i, :], src).then_inc(loaded, 16)

            @block.tensor
            def _(pe):
                pe.wait_ge(loaded, 16 * n)
                for i in range(nq + 1):
                    tokens = tq if i < nq else tk
                    for c in range(DC):
                        last = pe.matmul(ps[i][:, 0:tokens], wt[:, i, c * P:(c + 1) * P], h[:, c, 0:tokens],
                                         start=(c == 0), stop=(c == DC - 1))
                    last.then_inc(projected, 1)
                for t in range(tk // P):
                    for c in range(DC):
                        last = pe.matmul(ps[nq + 1][:, t * P:(t + 1) * P], h[:, c, t * P:(t + 1) * P],
                                         wt[:, nq + 1, c * P:(c + 1) * P], start=(c == 0), stop=(c == DC - 1))
                last.then_inc(projected, 1)
                if rope:
                    for i in range(nq + 1):
                        pe.wait_ge(raw_ready, i + 1)
                        pe.matmul(rot[i][:, 0:T], k.rot, raw[:, i, :], start=True, stop=True).then_inc(rotated, 1)

            @block.scalar
            def _(act):
                for i in range(nq + 1):
                    act.wait_ge(projected, i + 1)
                    scale = HEAD ** -0.5 if i < nq else 1.0
                    if rope:
                        act.activation(raw[:, i, :], ps[i][:, 0:T], ACT.Copy, scale=scale).then_inc(raw_ready, 1)
                    first = T if rope else 0
                    if i == nq:
                        act.activation(kt[:, first:tk], ps[i][:, first:tk], ACT.Copy)
                    elif tq > first:
                        for m in range(2):
                            rows = slice(m * HEAD, (m + 1) * HEAD)
                            act.activation(q[rows, 2 * i + m, first:tq], ps[i][rows, first:tq], ACT.Copy, scale=scale)
                act.wait_ge(projected, n)
                act.activation(v[:], ps[nq + 1][:].rearrange("p (t f) -> p t f", f=P), ACT.Copy)

            if rope:
                @block.vector
                def _(dve):
                    for i in range(nq + 1):
                        dve.wait_ge(raw_ready, i + 1)
                        dve.tensor_tensor(part[:, i, 0, :], raw[:, i, :], k.cos, ALU.mult).then_inc(own, 1)
                        dve.wait_ge(rotated, i + 1)
                        dve.tensor_tensor(part[:, i, 1, :], rot[i][:, 0:T], k.sin, ALU.mult).then_inc(own, 1)
                        dve.wait_ge(own, 2 * i + 2)
                        if i == nq:
                            dve.tensor_tensor(kt[:, 0:T], part[:, i, 0, :], part[:, i, 1, :], ALU.add)
                        else:
                            for m in range(2):
                                rows = slice(m * HEAD, (m + 1) * HEAD)
                                dve.tensor_tensor(q[rows, 2 * i + m, 0:T], part[rows, i, 0, :],
                                                  part[rows, i, 1, :], ALU.add)


def attend_stage(nc, k, groups, q, kt, v, width, out, bias=None, sink=None, lam=None):
    nm = len(groups[0][0])
    G = len(groups)
    K = 2 * T
    with ExitStack() as ctx:
        sb = lambda name, shape: ctx.enter_context(sbuf(nc, name, shape, F32))
        p = sb("p", [P, 2, nm, K])
        lg = sb("lg", [P, 2, K]) if bias is not None else None
        pts = sb("pts", [P, 2, K])
        neg, tot, inv, snk = (sb(n, [P, G * nm]) for n in ("neg", "tot", "inv", "snk"))
        s_ps = [ctx.enter_context(psum(nc, f"s_ps{i}", [P, 512], F32)) for i in range(2 * nm)]
        pt_ps = [ctx.enter_context(psum(nc, f"pt_ps{i}", [P, 512], F32)) for i in range(2)]
        o_ps = [ctx.enter_context(psum(nc, f"o_ps{i}", [P, 512], F32)) for i in range(2)]
        with stage(nc, "scored", "biased", "maxed", "exped", "weighted", "flipped", "flip_copied",
                   "gathered", "written", "own") as (
                block, scored, biased, maxed, exped, weighted, flipped, flip_copied, gathered, written, own):
            @block.tensor
            def _(pe):
                for step in range(G + 2):
                    if step < G:
                        g = step
                        heads, qt, k0 = groups[g][:3]
                        if g >= 2:
                            pe.wait_ge(exped, (g - 1) * nm)
                        for m, head in enumerate(heads):
                            last = pe.matmul(s_ps[(g % 2) * nm + m][:, k0:K], q[:, head, qt * P:(qt + 1) * P],
                                             kt[:, k0:K], start=True, stop=True)
                        last.then_inc(scored, 1)
                    if 0 <= step - 1 < G:
                        g = step - 1
                        k0 = groups[g][2]
                        pe.wait_ge(weighted if nm == 2 else exped, g + 1)
                        if g >= 2:
                            pe.wait_ge(flip_copied, g - 1)
                        for t in range(k0 // P, K // P):
                            last = pe.transpose(pt_ps[g % 2][:, t * P:(t + 1) * P],
                                                p[:, g % 2, 0, t * P:(t + 1) * P], k.ident)
                        last.then_inc(flipped, 1)
                    if 0 <= step - 2:
                        g = step - 2
                        k0, v0 = groups[g][2:4]
                        pe.wait_ge(flip_copied, g + 1)
                        if g >= 2:
                            pe.wait_ge(written, g - 1)
                        for t in range(k0 // P, K // P):
                            last = pe.matmul(o_ps[g % 2][:, 0:width], pts[:, g % 2, t * P:(t + 1) * P],
                                             v[:, t, v0:v0 + width], start=(t == k0 // P), stop=(t == K // P - 1))
                        last.then_inc(gathered, 1)

            @block.scalar
            def _(act):
                for step in range(G + 1):
                    if step < G:
                        g = step
                        k0 = groups[g][2]
                        act.wait_ge(maxed, g + 1)
                        if g >= 2:
                            act.wait_ge(flipped, g - 1)
                        for m in range(nm):
                            i = g * nm + m
                            src = s_ps[(g % 2) * nm + m] if bias is None else lg[:, g % 2, :]
                            act.activation(p[:, g % 2, m, k0:K], src[:, k0:K], ACT.Exp, bias=neg[:, i:i + 1],
                                           accum_out=tot[:, i:i + 1]).then_inc(exped, 1)
                        if sink is not None:
                            col = groups[g][5]
                            act.activation(snk[:, g:g + 1], neg[:, g:g + 1], ACT.Exp, bias=sink[0][:, col:col + 1],
                                           ).then_inc(weighted, 1)
                    if step >= 1:
                        g = step - 1
                        k0 = groups[g][2]
                        act.wait_ge(flipped, g + 1)
                        if g >= 2:
                            act.wait_ge(gathered, g - 1)
                        act.activation(pts[:, g % 2, k0:K], pt_ps[g % 2][:, k0:K], ACT.Copy).then_inc(flip_copied, 1)

            @block.vector
            def _(dve):
                order = Order(dve, own)
                for step in range(G + 2):
                    if step < G:
                        g = step
                        _h, qt, k0, _v, bi, si = groups[g][:6]
                        dve.wait_ge(scored, g + 1)
                        if bias is not None:
                            if g >= 2:
                                dve.wait_ge(exped, g - 1)
                            s = s_ps[g % 2]
                            if k0 == 0:
                                dve.tensor_tensor(lg[:, g % 2, 0:T], s[:, 0:T], bias[bi], ALU.add)
                            order(dve.tensor_copy(lg[:, g % 2, T:K], s[:, T:K]))
                            order(dve.tensor_reduce(neg[:, g:g + 1], lg[:, g % 2, k0:K], AX, ALU.max, negate=True))
                            if sink is not None:
                                order(dve.tensor_tensor(neg[:, g:g + 1], neg[:, g:g + 1],
                                                        sink[1][:, si:si + 1], ALU.min))
                        else:
                            for m in range(nm):
                                i = g * nm + m
                                order(dve.tensor_reduce(neg[:, i:i + 1], s_ps[(g % 2) * nm + m][:, k0:K], AX,
                                                        ALU.max, negate=True))
                        dve.sem_inc(maxed, 1)
                    if 0 <= step - 1 < G:
                        g = step - 1
                        k0 = groups[g][2]
                        dve.wait_ge(exped, (g + 1) * nm)
                        one = slice(g * nm, (g + 1) * nm)
                        if sink is not None:
                            dve.wait_ge(weighted, g + 1)
                            order(dve.tensor_tensor(tot[:, one], tot[:, one], snk[:, one], ALU.add))
                        order(dve.reciprocal(inv[:, one], tot[:, one]))
                        if nm == 2:
                            order(dve.tensor_scalar(inv[:, 2 * g + 1:2 * g + 2], inv[:, 2 * g + 1:2 * g + 2], lam,
                                                    None, ALU.mult))
                            order(dve.tensor_scalar(p[:, g % 2, 0, k0:K], p[:, g % 2, 0, k0:K],
                                                    inv[:, 2 * g:2 * g + 1], None, ALU.mult))
                            dve.scalar_tensor_tensor(p[:, g % 2, 0, k0:K], p[:, g % 2, 1, k0:K],
                                                     inv[:, 2 * g + 1:2 * g + 2], p[:, g % 2, 0, k0:K],
                                                     ALU.mult, ALU.add).then_inc(weighted, 1)
                    if 0 <= step - 2:
                        g = step - 2
                        dve.wait_ge(gathered, g + 1)
                        if nm == 2:
                            dve.tensor_copy(out(groups[g][6]), o_ps[g % 2][:, 0:width]).then_inc(written, 1)
                        else:
                            dve.tensor_scalar(out(groups[g][6]), o_ps[g % 2][:, 0:width], inv[:, g:g + 1], None,
                                              ALU.mult).then_inc(written, 1)


def to_features_stage(nc, k, o, y, tiles):
    with ExitStack() as ctx:
        ps = [ctx.enter_context(psum(nc, f"ps{i}", [P, 4, P], F32)) for i in range(4)]
        n = tiles * DC // 4
        with stage(nc, "flipped", "copied") as (block, flipped, copied):
            @block.tensor
            def _(pe):
                for i in range(n):
                    if i >= 4:
                        pe.wait_ge(copied, i - 3)
                    for j in range(4):
                        t, c = divmod(4 * i + j, DC)
                        last = pe.transpose(ps[i % 4][:, j, :], o[:, t, c * P:(c + 1) * P], k.ident)
                    last.then_inc(flipped, 1)

            @block.vector
            def _(dve):
                for i in range(n):
                    t, c = divmod(4 * i, DC)
                    dve.wait_ge(flipped, i + 1)
                    dve.tensor_copy(y[:, c:c + 4, t * P:(t + 1) * P], ps[i % 4][:]).then_inc(copied, 1)


def diff_norm_stage(nc, o, tiles, weight, first):
    n = tiles * DIFF_HEADS
    with ExitStack() as ctx:
        sq = ctx.enter_context(sbuf(nc, "sq", [P, n, P], F32))
        ms = ctx.enter_context(sbuf(nc, "ms", [P, n], F32))
        with stage(nc, "own", "inverse", "rooted") as (block, own, inverse, rooted):
            part = lambda t: o[:, t, first:first + DIFF_HEADS * P].rearrange("p (h f) -> p h f", f=P)

            @block.vector
            def _(dve):
                order = Order(dve, own)
                for t in range(tiles):
                    last = dve.tensor_tensor(sq[:, t * 4:t * 4 + 4, :], part(t), part(t), ALU.mult)
                order(last)
                order(dve.tensor_reduce(ms[:], sq[:], AX, ALU.add))
                order(dve.tensor_scalar(ms[:], ms[:], 1.0 / P, EPS, ALU.mult, ALU.add))
                dve.reciprocal(ms[:], ms[:]).then_inc(inverse, 1)
                dve.wait_ge(rooted, 1)
                for t in range(tiles):
                    for hh in range(DIFF_HEADS):
                        i = t * 4 + hh
                        dve.tensor_scalar(part(t)[:, hh, :], part(t)[:, hh, :], ms[:, i:i + 1], 1.0 - LAM_INIT,
                                          ALU.mult, ALU.mult)

            @block.scalar
            def _(act):
                act.wait_ge(inverse, 1)
                act.activation(ms[:], ms[:], ACT.Sqrt).then_inc(rooted, 1)


def lambda_stage(nc, raw, lam):
    with ExitStack() as ctx:
        t = ctx.enter_context(sbuf(nc, "lam_t", [P, 2, HEAD], F32))
        s = ctx.enter_context(sbuf(nc, "lam_s", [P, 2], F32))
        with stage(nc, "own", "summed", "exped") as (block, own, summed, exped):
            @block.vector
            def _(dve):
                order = Order(dve, own)
                pairs = raw.rearrange("p (a b f) -> p a b f", a=2, b=2)
                order(dve.tensor_tensor(t[:], pairs[:, :, 0, :], pairs[:, :, 1, :], ALU.mult))
                dve.tensor_reduce(s[:], t[:], AX, ALU.add).then_inc(summed, 1)
                dve.wait_ge(exped, 1)
                order(dve.tensor_tensor(lam[:], s[:, 1:2], s[:, 0:1], ALU.subtract))
                dve.tensor_scalar(lam[:], lam[:], LAM_INIT, None, ALU.subtract)

            @block.scalar
            def _(act):
                act.wait_ge(summed, 1)
                act.activation(s[:], s[:], ACT.Exp).then_inc(exped, 1)


def clear_stage(nc, tile):
    with stage(nc, "cleared") as (block, _c):
        @block.vector
        def _(dve):
            dve.memset(tile[:], 0.0)


def even_mixer(nc, k, h, x, ctx_x, cols, mod, d):
    with ExitStack() as ctx:
        sb = lambda name, shape: ctx.enter_context(sbuf(nc, name, shape, F32))
        o = sb("o", [P, 4, D])
        q, kt, v = sb("q", [P, 2, 2 * T]), sb("kt", [P, 2 * T]), sb("v", [P, 4, P])
        bias, lam = sb("bias", [P, 2, TT, T]), sb("lam", [P, 1])
        a = COL2["lambda"][0]
        lambda_stage(nc, cols[:, a:a + 4 * HEAD], lam)
        clear_stage(nc, q)
        w = d.w_even
        with nc.Fori(0, 4) as c:
            qkv_stage(nc, k, h, [w[c], w[4 + c], w[8 + c]], 1, 2 * T, False, q, kt, v)
            load_stage(nc, [(bias[:], d.bias[c])])
            groups = [((m,), t, 0 if t < TT else T, m * HEAD, (m, t), None, (t, m * HEAD))
                      for t in range(4) for m in range(2)]
            attend_stage(nc, k, groups, q, kt, v, HEAD,
                         lambda at: o[:, at[0], bass.ds(c * P + at[1], HEAD)],
                         bias={(m, t): bias[:, m, t, :] for m in range(2) for t in range(TT)} | {
                             (m, t): None for m in range(2) for t in (2, 3)})
        with nc.Fori(0, DIFF_HEADS) as c:
            qkv_stage(nc, k, h, [w[12 + c], w[16 + c], w[20 + c]], 1, 2 * T, True, q, kt, v)
            groups = [((0, 1), t, 0 if t < TT else T, 0, None, None, t) for t in range(4)]
            attend_stage(nc, k, groups, q, kt, v, P,
                         lambda t: o[:, t, bass.ds(c * P + 4 * P, P)], lam=lam[:])
        diff_norm_stage(nc, o, 4, None, 4 * P)
        to_features_stage(nc, k, o, h, 4)
        a = COL2["subln"][0]
        with stage(nc, "own") as (block, own):
            @block.vector
            def _(dve):
                dve.tensor_scalar(h[:, 4:8, :], h[:, 4:8, :], cols[:, a:a + 1], None, ALU.mult)

        def residual(dve, n, ps, done):
            dve.scalar_tensor_tensor(x[:, n, :], ps[:, 0:T], mod[:, 0, bass.ds(n + 2 * DC, 1)], x[:, n, :],
                                     ALU.mult, ALU.add)
            dve.scalar_tensor_tensor(ctx_x[:, n, :], ps[:, T:2 * T], mod[:, 1, bass.ds(n + 2 * DC, 1)],
                                     ctx_x[:, n, :], ALU.mult, ALU.add).then_inc(done, 1)

        project_stage(nc, d.w_out_even, DC, h, residual)


def odd_mixer(nc, k, h, x, cols, mod, d):
    with ExitStack() as ctx:
        sb = lambda name, shape: ctx.enter_context(sbuf(nc, name, shape, F32))
        o = sb("o", [P, TT, D])
        q, kt, v = sb("q", [P, 4, T]), sb("kt", [P, 2 * T]), sb("v", [P, 4, P])
        snk, nsnk = sb("snk4", [P, 4]), sb("nsnk4", [P, 4])
        clear_stage(nc, q)
        w = d.w_odd
        a = COL2["sink"][0]
        band = k.band.rearrange("p (t k) -> p t k", t=TT)
        with nc.Fori(0, SWA_KV_HEADS) as n:
            qkv_stage(nc, k, h, [w[2 * n], w[2 * n + 1], w[8 + n], w[12 + n]], 2, T, True, q, kt, v)
            with stage(nc, "own") as (block, own):
                @block.vector
                def _(dve):
                    dve.tensor_copy(snk[:], cols[:, bass.ds(4 * n + a, 4)])
                    dve.tensor_scalar(nsnk[:], cols[:, bass.ds(4 * n + a, 4)], -1.0, None, ALU.mult)
            groups = [((g,), t, 0, 0, t, g, (t, g * HEAD)) for t in range(TT) for g in range(4)]
            attend_stage(nc, k, groups, q, kt, v, HEAD,
                         lambda at: o[:, at[0], bass.ds(n * (4 * HEAD) + at[1], HEAD)],
                         bias=[band[:, t, :] for t in range(TT)], sink=(snk, nsnk))
        to_features_stage(nc, k, o, h, TT)
        project_stage(nc, d.w_out_odd, DC, h[:, :, 0:T],
                      lambda dve, n, ps, done: dve.scalar_tensor_tensor(
                          x[:, n, :], ps[:, 0:T], mod[:, 0, bass.ds(n + 2 * DC, 1)], x[:, n, :],
                          ALU.mult, ALU.add).then_inc(done, 1))


def peer_route(nc, k, h, keys_dram, wq, route):
    R = PEER_TOPK
    with ExitStack() as ctx:
        sb = lambda name, shape, dt=F32: ctx.enter_context(sbuf(nc, name, shape, dt))
        qp, keys = sb("qp", [P, 16, T]), sb("keys", [P, 16, P])
        load_stage(nc, [(keys[:], keys_dram)])
        project_stage(nc, wq, 16, h,
                      lambda dve, n, ps, done: dve.tensor_copy(qp[:, n, :], ps[:, 0:T]).then_inc(done, 1))
        s, s2 = sb("s", [P, 16, P]), sb("s2", [P, 16, P])
        sv, si, sif = sb("sv", [P, 16, R]), sb("si", [P, 16, R], U32), sb("sif", [P, 16, R])
        cand, cand2 = sb("cand", [P, 8, R, R]), sb("cand2", [P, 8, R * R])
        fv, fi = sb("fv", [P, 8, R]), sb("fi", [P, 8, R], U32)
        hi, hif = sb("hi", [P, 2, 8 * R], U32), sb("hif", [P, 2, 8 * R])
        eq, sm = sb("eq", [P, 8 * R, R]), sb("sm", [P, 8])
        res = sb("res", [P, 3, SLOTS])
        ps = [ctx.enter_context(psum(nc, f"ps{i}", [P, 4, P], F32)) for i in range(4)]
        pt = [ctx.enter_context(psum(nc, f"pt{i}", [P, P], F32)) for i in range(3)]
        for t in range(TT):
            with stage(nc, "scored", "own", "centred", "exped", "decoded", "flipped", "copied") as (
                    block, scored, own, centred, exped, decoded, flipped, copied):
                @block.tensor
                def _(pe):
                    for i in range(16):
                        last = pe.matmul(ps[i // 4][:, i % 4, :], qp[:, i, t * P:(t + 1) * P], keys[:, i, :],
                                         start=True, stop=True)
                        if i % 4 == 3:
                            last.then_inc(scored, 1)
                    pe.wait_ge(decoded, 1)
                    for i in range(3):
                        pe.transpose(pt[i][:], res[:, i, :], k.ident).then_inc(flipped, 1)

                @block.scalar
                def _(act):
                    for i in range(4):
                        act.wait_ge(scored, i + 1)
                        act.activation(s[:, 4 * i:4 * i + 4, :], ps[i][:], ACT.Copy).then_inc(copied, 1)
                    act.wait_ge(centred, 1)
                    act.activation(fv[:], fv[:], ACT.Exp).then_inc(exped, 1)
                    for i in range(3):
                        act.wait_ge(flipped, i + 1)
                        act.activation(route[:, i, t * P:(t + 1) * P], pt[i][:], ACT.Copy)

                @block.vector
                def _(dve):
                    order = Order(dve, own)

                    def top(values, rest, best, index, n):
                        for lo in (0, 8):
                            src = values if lo == 0 else rest
                            for i in range(n):
                                last = dve.max(best[:, i, lo:lo + 8], src[:, i, :])
                            order(last)
                            for i in range(n):
                                last = dve.max_index(index[:, i, lo:lo + 8], best[:, i, lo:lo + 8], src[:, i, :])
                                if lo == 0:
                                    last = dve.match_replace(rest[:, i, :], best[:, i, 0:8], values[:, i, :], -3e38)
                            order(last)

                    dve.wait_ge(copied, 4)
                    top(s, s2, sv, si, 16)
                    order(dve.tensor_copy(sif[:], si[:]))
                    pair = sv[:].rearrange("p (h two) r -> p h two r", two=2)
                    for hh in range(8):
                        last = dve.tensor_tensor(cand[:, hh], pair[:, hh, 0, :].unsqueeze(2).to_broadcast([P, R, R]),
                                                 pair[:, hh, 1, :].unsqueeze(1).to_broadcast([P, R, R]), ALU.add)
                    order(last)
                    flat = cand[:].rearrange("p h a b -> p h (a b)")
                    top(flat, cand2, fv, fi, 8)
                    fif = fi[:].rearrange("p h r -> p (h r)")
                    dve.tensor_scalar(hi[:, 0, :], fif, 4, None, ALU.logical_shift_right)
                    order(dve.tensor_scalar(hi[:, 1, :], fif, R - 1, None, ALU.bitwise_and))
                    order(dve.tensor_copy(hif[:], hi[:]))
                    dve.tensor_tensor(fv[:], fv[:], res_max(dve, order, sm, fv), ALU.subtract).then_inc(centred, 1)
                    sip = sif[:].rearrange("p (h two) r -> p h two r", two=2)
                    io = k.iota[:, 0:R].unsqueeze(1).to_broadcast([P, 8 * R, R])
                    for half in range(2):
                        order(dve.tensor_tensor(eq[:], hif[:, half, :].unsqueeze(2).to_broadcast([P, 8 * R, R]), io,
                                                ALU.is_equal))
                        for hh in range(8):
                            row = sip[:, hh, half, :].unsqueeze(1).to_broadcast([P, R, R])
                            e = eq[:, hh * R:(hh + 1) * R, :]
                            last = dve.tensor_tensor(e, e, row, ALU.mult)
                        order(last)
                        order(dve.tensor_reduce(res[:, half, :], eq[:], AX, ALU.add))
                    dve.wait_ge(exped, 1)
                    order(dve.tensor_reduce(sm[:], fv[:], AX, ALU.add))
                    order(dve.reciprocal(sm[:], sm[:]))
                    dve.tensor_tensor(res[:, 2, :].rearrange("p (h r) -> p h r", r=R), fv[:],
                                      sm[:].unsqueeze(2).to_broadcast([P, 8, R]), ALU.mult).then_inc(decoded, 1)


def res_max(dve, order, sm, fv):
    order(dve.tensor_copy(sm[:], fv[:, :, 0]))
    return sm[:].unsqueeze(2).to_broadcast([P, 8, PEER_TOPK])


def peer_gates(nc, k, route, gates):
    B = 4
    with ExitStack() as ctx:
        sb = lambda name, shape: ctx.enter_context(sbuf(nc, name, shape, F32))
        one, two = sb("one", [P, 2, B, P]), sb("two", [P, 2, B, P])
        ps = [ctx.enter_context(psum(nc, f"ps{i}", [P, B, P], F32)) for i in range(2)]
        with stage(nc, "spelled", "multiplied", "kept") as (block, spelled, multiplied, kept):
            @block.vector
            def _(dve):
                with dve.Fori(0, T // (2 * B)) as i:
                    for s in range(2):
                        dve.wait_ge(multiplied, 2 * i + (s + 1))
                        for j in range(B):
                            t = 2 * B * i + (s * B + j)
                            dve.tensor_scalar(one[:, s, j, :], k.iota, route[:, 0, bass.ds(t, 1)],
                                              route[:, 2, bass.ds(t, 1)], ALU.is_equal, ALU.mult)
                            last = dve.tensor_scalar(two[:, s, j, :], k.iota, route[:, 1, bass.ds(t, 1)], None,
                                                     ALU.is_equal)
                        last.then_inc(spelled, 1)

            @block.tensor
            def _(pe):
                pe.sem_inc(multiplied, 2)
                with pe.Fori(0, T // (2 * B)) as i:
                    for s in range(2):
                        pe.wait_ge(spelled, 2 * i + (s + 1))
                        pe.wait_ge(kept, 2 * i + (s + 1))
                        for j in range(B):
                            last = pe.matmul(ps[s][:, j, :], two[:, s, j, :], one[:, s, j, :], start=True, stop=True)
                        last.then_inc(multiplied, 1)

            @block.scalar
            def _(act):
                act.sem_inc(kept, 2)
                with act.Fori(0, T // (2 * B)) as i:
                    for s in range(2):
                        act.wait_ge(multiplied, 2 * i + (s + 3))
                        act.activation(gates[:, :, bass.ds(2 * B * i + s * B, B)],
                                       ps[s][:].rearrange("p t e -> p e t"), ACT.Copy).then_inc(kept, 1)


def peer_experts(nc, k, h, u, v, gates, x, gain):
    C = PEER_NKEYS
    with ExitStack() as ctx:
        sb = lambda name, shape: ctx.enter_context(sbuf(nc, name, shape, F32))
        ut, vt = sb("ut", [P, 2, D]), sb("vt", [P, 2, D])
        ga, gw = sb("ga", [P, 2, T]), sb("gw", [P, 2, T])
        f = gates[:, 0:TT * D // T, :].rearrange("p a b -> p (a b)").rearrange("p (t n) -> p t n", t=TT)
        a_ps = [ctx.enter_context(psum(nc, f"a_ps{i}", [P, 512], F32)) for i in range(2)]
        out = [[ctx.enter_context(psum(nc, f"out{t}{i}", [P, 512], F32)) for i in range(2)] for t in range(TT)]
        with stage(nc, "u_in0", "u_in1", "v_in0", "v_in1", "scored", "gelued", "gated", "used") as (
                block, u_in0, u_in1, v_in0, v_in1, scored, gelued, gated, used):
            u_in, v_in = (u_in0, u_in1), (v_in0, v_in1)

            @block.sync
            def _(sp):
                for s in range(2):
                    sp.dma_start(ut[:, s, :], u[s]).then_inc(u_in[s], 16)
                    sp.dma_start(vt[:, s, :], v[s]).then_inc(v_in[s], 16)
                with sp.Fori(1, C // 2) as i:
                    for s in range(2):
                        sp.wait_ge(scored, 2 * i + (s - 1))
                        sp.dma_start(ut[:, s, :], u[2 * i + s]).then_inc(u_in[s], 16)
                        sp.wait_ge(used, 2 * i + (s + 1))
                        sp.dma_start(vt[:, s, :], v[2 * i + s]).then_inc(v_in[s], 16)

            @block.tensor
            def _(pe):
                def score(s, turn):
                    pe.wait_ge(u_in[s], turn)
                    for c in range(DC):
                        last = pe.matmul(a_ps[s][:, 0:T], ut[:, s, c * P:(c + 1) * P], h[:, c, :],
                                         start=(c == 0), stop=(c == DC - 1))
                    last.then_inc(scored, 1)

                def gather(s, turn, n, first=False, last_one=False):
                    pe.wait_ge(v_in[s], turn)
                    pe.wait_ge(gated, n + 2)
                    for t in range(TT):
                        for i in range(2):
                            last = pe.matmul(out[t][i][:], gw[:, s, t * P:(t + 1) * P], vt[:, s, i * 512:(i + 1) * 512],
                                             start=first, stop=last_one)
                    last.then_inc(used, 1)

                pe.sem_inc(used, 2)
                score(0, 16)
                score(1, 16)
                gather(0, 16, 1, first=True)
                with pe.Fori(1, C // 2) as i:
                    pe.wait_ge(gelued, 2 * i - 1)
                    score(0, 16 * i + 16)
                    gather(1, 16 * i, 2 * i)
                    pe.wait_ge(gelued, 2 * i)
                    score(1, 16 * i + 16)
                    gather(0, 16 * i + 16, 2 * i + 1)
                gather(1, 8 * C, C, last_one=True)

            @block.scalar
            def _(act):
                with act.Fori(0, C // 2) as i:
                    for s in range(2):
                        act.wait_ge(scored, 2 * i + (s + 1))
                        act.wait_ge(gated, 2 * i + (s + 1))
                        act.activation(ga[:, s, :], a_ps[s][:, 0:T], ACT.Gelu).then_inc(gelued, 1)

            @block.vector
            def _(dve):
                dve.sem_inc(gated, 2)
                with dve.Fori(0, C // 2) as i:
                    for s in range(2):
                        dve.wait_ge(gelued, 2 * i + (s + 1))
                        dve.wait_ge(used, 2 * i + (s + 1))
                        dve.tensor_tensor(gw[:, s, :], ga[:, s, :], gates[:, 2 * i + s, :],
                                          ALU.mult).then_inc(gated, 1)
                dve.wait_ge(used, C + 2)
                for t in range(TT):
                    for i in range(2):
                        dve.tensor_copy(f[:, t, i * 512:(i + 1) * 512], out[t][i][:])
        with stage(nc, "flipped", "added") as (block, flipped, added):
            @block.tensor
            def _(pe):
                for n in range(2 * TT):
                    t, half = divmod(n, 2)
                    for j in range(4):
                        c = 4 * half + j
                        last = pe.transpose(out[t][half][:, j * P:(j + 1) * P], f[:, t, c * P:(c + 1) * P], k.ident)
                    last.then_inc(flipped, 1)

            @block.vector
            def _(dve):
                for n in range(2 * TT):
                    t, half = divmod(n, 2)
                    dve.wait_ge(flipped, n + 1)
                    for j in range(4):
                        c = 4 * half + j
                        xs = x[:, c, t * P:(t + 1) * P]
                        dve.scalar_tensor_tensor(xs, out[t][half][:, j * P:(j + 1) * P], gain[:, c:c + 1], xs,
                                                 ALU.mult, ALU.add)


def peer(nc, k, h, x, gain, layer, d):
    with ExitStack() as ctx:
        route = ctx.enter_context(sbuf(nc, "route", [P, 3, T], F32))
        peer_route(nc, k, h, d.keys[layer], d.wq[layer], route)
        gates = ctx.enter_context(sbuf(nc, "gates", [P, PEER_NKEYS, T], F32))
        peer_gates(nc, k, route, gates)
        peer_experts(nc, k, h, d.u[layer], d.v[layer], gates, x, gain)


def second_block(nc, k, x, ctx_x, d):
    with ExitStack() as ctx:
        sb = lambda name, shape: ctx.enter_context(sbuf(nc, name, shape, F32))
        cols = sb("cols2", [P, N_COLS2])
        h, sc = sb("h2", [P, DC, 2 * T]), sb("sc", [P, DC, 2])
        mod, gains = sb("mod", [P, 2, 48]), sb("gains", [P, 2, 2, DC])
        load_stage(nc, [(cols[:], d.cols2)])
        a = COL2["c"][0]
        with stage(nc, "own") as (block, own):
            @block.scalar
            def _(act):
                act.activation(sc[:].rearrange("p c t -> p (c t)"), cols[:, a:a + 2 * DC], ACT.Silu)
        hx, hc = h[:, :, 0:T], h[:, :, T:2 * T]
        for layer in range(DEPTH):
            modulation(nc, k, sc, d.w_mod[layer], cols, layer, mod, gains)
            norm_stage(nc, k, x, gains[:, 0, 0], hx, mod[:, 0, 0:DC])
            norm_stage(nc, k, ctx_x, gains[:, 0, 1], hc, mod[:, 1, 0:DC])
            if layer == 0:
                even_mixer(nc, k, h, x, ctx_x, cols, mod, d)
            else:
                odd_mixer(nc, k, h, x, cols, mod, d)
            for kind, res in enumerate((x, ctx_x) if layer == 0 else (x,)):
                norm_stage(nc, k, res, gains[:, 1, kind], hx, mod[:, kind, 3 * DC:4 * DC])
                peer(nc, k, hx, res, mod[:, kind, 5 * DC:6 * DC], layer, d)


class Data:
    pass


def fm(w):
    *lead, k, n = w.shape
    w = w.reshape(*lead, k // P, P, n // P, P)
    r = len(lead)
    w = w.transpose(*range(r), r + 2, r + 1, r, r + 3)
    return np.ascontiguousarray(w).reshape(*lead, n // P, P, k)


def by_part(v):
    v = v.reshape(*v.shape[:-1], -1, P)
    return np.ascontiguousarray(np.swapaxes(v, -1, -2))


def constants():
    i, j = np.arange(P)[:, None], np.arange(P)[None, :]
    out = np.zeros((P, N_CST), np.float32)

    def put(name, v):
        a, n = CST[name]
        out[:, a:a + n] = v.reshape(P, n)

    put("ident", i == j)
    put("ones", np.ones((P, P)))
    put("halves", i // HEAD == j // HEAD)
    put("tri_incl", i <= j)
    put("tri_strict", i < j)
    s = np.arange(2 * P - HEAD - 1)[None, :]
    put("slide", s == (HEAD - 1) + HEAD * (i // HEAD))
    put("iota", np.broadcast_to(j, (P, P)))
    q = HEAD // 4
    rot = np.zeros((P, P))
    for m in range(P):
        if (m // q) % 2 == 0:
            rot[m + q, m] = -1.0
        else:
            rot[m - q, m] = 1.0
    put("rot", rot)
    t = np.arange(T)
    half = HEAD // 2
    inv = ROPE_THETA ** (-np.arange(0, half, 2, dtype=np.float32) / half)
    ar, ac = (t // GRID_W)[:, None] * inv, (t % GRID_W)[:, None] * inv
    ang = np.concatenate([ar, ar, ac, ac], axis=-1).astype(np.float32)
    put("cos", np.tile(np.cos(ang).T, (2, 1)))
    put("sin", np.tile(np.sin(ang).T, (2, 1)))
    qq, kk = np.arange(T).reshape(TT, P).T[:, :, None], np.arange(T)[None, None, :]
    put("band", np.where(np.abs(qq - kk) <= SWA_WINDOW, 0.0, NEG))
    level = np.stack([(i // (2 << m) == j // (2 << m)) & ((i >> m) % 2 == 1) & ((j >> m) % 2 == 0)
                      for m in range(7)])
    put("level", level.transpose(1, 0, 2))
    put("level_t", level.transpose(2, 0, 1))
    return out


def packed(parts, at, n, lead):
    out = np.zeros((*lead, P, n), np.float32)
    for name, v in parts.items():
        a, w = at[name]
        out[..., a:a + w] = v.reshape(*lead, P, w)
    return out


def first_arrays(v):
    w = v["w_in"]
    gd = slice(1024 + 2048, 1024 + 2048 + 8)
    main = np.concatenate([w[:, :, :gd.start], w[:, :, gd.stop:]], axis=2)
    rows = lambda a: np.broadcast_to(a[:, None, :], (DEPTH, P, a.shape[-1]))
    taps = lambda a: np.ascontiguousarray(a.reshape(DEPTH, CONV_W, -1, P).transpose(0, 3, 2, 1))
    cols = packed({
        "norm_ffn1": by_part(v["norm_ffn1"]), "norm_mix": by_part(v["norm_mix"]),
        "norm_ffn2": by_part(v["norm_ffn2"]), "hg_norm": np.tile(v["hg_norm_w"], (1, 2))[:, :, None],
        "gd_norm": v["gd_norm_w"][:, :, None], "gd_conv": taps(v["gd_conv_w"]),
        "rg_conv": taps(v["rg_conv_w"]), "rg_conv_b": by_part(v["rg_conv_b"]),
        "rg_br": by_part(v["rg_br"]), "rg_bi": by_part(v["rg_bi"]), "rg_lambda": by_part(v["rg_lambda"]),
        "gd_a_log": rows(v["gd_a_log"]), "gd_dt_bias": rows(v["gd_dt_bias"]),
    }, COL, N_COLS, (DEPTH,))
    wrg = np.zeros((DEPTH, P, 2, 2, P), np.float32)
    for m, name in enumerate(("rg_wr", "rg_wi")):
        for blk in range(4):
            c, o = blk // 2, 64 * (blk % 2)
            wrg[:, o:o + 64, m, c, o:o + 64] = v[name][:, blk]
    wd = lambda a: fm(a)
    return {
        "x": np.ascontiguousarray(v["x"][0].reshape(T, DC, P).transpose(2, 1, 0)),
        "cst": constants(), "cols": cols, "hg_lb": np.ascontiguousarray(v["hg_lb"].reshape(DEPTH, 2, P).transpose(2, 0, 1)),
        "wg0": fm(v["ffn1_gate"]), "wu0": fm(v["ffn1_up"]), "wd0": wd(v["ffn1_down"]),
        "wg1": fm(v["ffn2_gate"]), "wu1": fm(v["ffn2_up"]), "wd1": wd(v["ffn2_down"]),
        "w_in": fm(main), "w_out": fm(v["w_out"]),
        "wba": np.ascontiguousarray(w[:, :, gd].reshape(DEPTH, DC, P, 8).transpose(0, 2, 1, 3)),
        "wrg": wrg,
    }


def second_arrays(v):
    g = lambda n: v[n + "_2"]
    rows = lambda a: np.broadcast_to(a.reshape(1, -1), (P, a.size))
    layers = lambda a: by_part(a).transpose(1, 0, 2)
    both = np.stack([g("c")[0], g("c_ctx")])
    cols2 = packed({
        "norm1": layers(g("norm1_g")), "norm2": layers(g("norm2_g")), "b_mod": layers(g("b_mod")),
        "c": by_part(both).transpose(1, 2, 0), "final": by_part(g("final_g")),
        "norm_last": by_part(v["norm_final"]), "subln": g("diff_subln_g")[0],
        "lambda": rows(g("diff_lambda")), "sink": rows(g("swa_sink")),
    }, COL2, N_COLS2, ())
    rpb = g("na_rpb")[0]
    tok = np.arange(T)
    r, c = tok // GRID_W, tok % GRID_W
    start = np.clip(c - NA_WIN_W // 2, 0, GRID_W - NA_WIN_W)
    inside = (c[None, :] >= start[:, None]) & (c[None, :] < start[:, None] + NA_WIN_W)
    dr = r[None, :] - r[:, None] + NA_WIN_H - 1
    dc = np.clip(c[None, :] - c[:, None] + NA_WIN_W - 1, 0, 2 * NA_WIN_W - 2)
    bias = np.where(inside[None], rpb[:, dr, dc], np.float32(NEG))
    bias = bias.reshape(4, 2, TT, P, T).transpose(0, 3, 1, 2, 4)
    odd = g("w_in_odd")[0]
    nq = SWA_Q_HEADS * HEAD
    kv = odd[:, nq:].reshape(D, 2 * SWA_KV_HEADS, 1, HEAD)
    kv = np.broadcast_to(kv, (D, 2 * SWA_KV_HEADS, 2, HEAD)).reshape(D, -1)
    return {
        "cols2": cols2, "bias": np.ascontiguousarray(bias),
        "ctx": np.ascontiguousarray(g("ctx")[0].reshape(T, DC, P).transpose(2, 1, 0)),
        "w_mod": fm(g("w_mod")), "w_even": fm(g("w_in_even")[0]), "w_out_even": fm(g("w_out_even")[0]),
        "w_odd": fm(np.concatenate([odd[:, :nq], kv], axis=1)), "w_out_odd": fm(g("w_out_odd")[0]),
        "wq": fm(g("peer_wq")),
        "keys": np.ascontiguousarray(g("peer_keys").reshape(DEPTH, 16, PEER_NKEYS, P).transpose(0, 3, 1, 2)),
        "u": fm(g("peer_u").transpose(0, 2, 1)),
        "v": g("peer_v").reshape(DEPTH, PEER_NKEYS, PEER_NKEYS, D),
    }


def build(nc, d, out):
    _names.clear()
    with ExitStack() as ctx:
        sb = lambda name, shape: ctx.enter_context(sbuf(nc, name, shape, F32))
        x, ctx_x, cst, last = sb("x_fm", [P, DC, T]), sb("ctx_fm", [P, DC, T]), sb("cst_sb", [P, N_CST]), sb("last_cols", [P, 2 * DC])
        k = Constants(cst)
        a = COL2["final"][0]
        load_stage(nc, [(x[:], d.x), (ctx_x[:], d.ctx), (cst[:], d.cst), (last[:], d.cols2[:, a:a + 2 * DC])])
        first_block(nc, k, x, d)
        norm_stage(nc, k, x, last[:, DC:2 * DC], x)
        second_block(nc, k, x, ctx_x, d)
        norm_stage(nc, k, x, last[:, 0:DC], x)
        with stage(nc, "stored") as (block, stored):
            @block.sync
            def _(sp):
                sp.dma_start(out, x[:]).then_inc(stored, 16)
                sp.wait_ge(stored, 16)


def kernel(**inputs):
    import concourse.bacc as bacc
    from concourse.bass_utils import run_bass_kernel_spmd

    v = {n: np.asarray(a) for n, a in inputs.items()}
    arrays = {**first_arrays(v), **second_arrays(v)}
    nc = bacc.Bacc("TRN2", target_bir_lowering=False, num_devices=1)
    d = Data()
    for name, a in arrays.items():
        d.__dict__[name] = nc.dram_tensor(f"in_{name}", a.shape, F32, kind="ExternalInput").ap()
    out = nc.dram_tensor("out", (P, DC, T), F32, kind="ExternalOutput").ap()
    build(nc, d, out)
    r = run_bass_kernel_spmd(nc, [{f"in_{n}": np.ascontiguousarray(a) for n, a in arrays.items()}], core_ids=[0])
    y = np.asarray(r.results[0]["out"])
    return np.ascontiguousarray(y.transpose(2, 1, 0)).reshape(1, T, D)
```

```python
from contextlib import ExitStack, contextmanager

import numpy as np

import concourse.bass as bass
from concourse import mybir

F32 = mybir.dt.float32
U32 = mybir.dt.uint32
F32R = mybir.dt.float32r
ALU = mybir.AluOpType
ACT = mybir.ActivationFunctionType
AX = mybir.AxisListType.X

P = 128
D = 1024
DC = D // P
T = 256
TT = T // P
DEPTH = 2
D_FF = 2816
FC = D_FF // P
EPS = 1e-6

HG_DK = 64
HG_PAIRS = 2
GD_HEADS = 4
RG_C = 8.0
CONV_W = 4
N_PROJ = 28
PAD = CONV_W - 1
TPAD = T + 4
HG_Q, HG_F, HG_I, HG_G, GD_Q, GD_K, GD_V, GD_Z, RG_X, RG_GATE = 0, 2, 4, 6, 8, 12, 16, 20, 24, 26

HEAD = 64
GRID_W = 64
NA_WIN_H, NA_WIN_W, NA_HEADS = 8, 16, 8
DIFF_HEADS = 4
SWA_Q_HEADS, SWA_KV_HEADS, SWA_WINDOW = 16, 4, 128
ROPE_THETA = 10000.0
NEG = -1e30
LAM_INIT = 0.8 - 0.6
PEER_HEADS, PEER_NKEYS, PEER_TOPK = 8, 128, 16
SLOTS = PEER_HEADS * PEER_TOPK

COL, _at = {}, 0
for _name, _n in (("norm_ffn1", DC), ("norm_mix", DC), ("norm_ffn2", DC), ("hg_norm", 1),
                  ("gd_norm", 1), ("gd_conv", 12 * CONV_W), ("rg_conv", 2 * CONV_W), ("rg_conv_b", 2),
                  ("rg_br", 2), ("rg_bi", 2), ("rg_lambda", 2), ("gd_a_log", 4), ("gd_dt_bias", 4)):
    COL[_name] = (_at, _n)
    _at += _n
N_COLS = _at

COL2, _at = {}, 0
for _name, _n in (("norm1", 2 * DC), ("norm2", 2 * DC), ("b_mod", 2 * 48), ("c", 2 * DC), ("final", DC),
                  ("norm_last", DC), ("subln", 1), ("lambda", 4 * HEAD), ("sink", SWA_Q_HEADS)):
    COL2[_name] = (_at, _n)
    _at += _n
N_COLS2 = _at

CST, _at = {}, 0
for _name, _n in (("ident", P), ("ones", P), ("halves", P), ("tri_incl", P), ("tri_strict", P),
                  ("slide", 2 * P - HEAD - 1), ("iota", P)):
    CST[_name] = (_at, _n)
    _at += _n
N_CST = _at

CST2, _at = {}, 0
for _name, _n in (("rot", P), ("cos", T), ("sin", T), ("band", TT * T)):
    CST2[_name] = (_at, _n)
    _at += _n
N_CST2 = _at


_names = {}


def unique(name):
    _names[name] = _names.get(name, -1) + 1
    return f"{name}_{_names[name]}"


def sbuf(nc, name, shape, dtype):
    return nc.sbuf_tensor(unique(name), shape, dtype)


def psum(nc, name, shape, dtype):
    return nc.psum_tensor(unique(name), shape, dtype)


@contextmanager
def stage(nc, *names):
    def take():
        held = [nc.semaphore(n) for n in names]
        return held, [s.__enter__() for s in held]

    def give(held):
        for s in held:
            s.__exit__(None, None, None)

    held, sems = take()
    if sems[-1].num - sems[0].num != len(sems) - 1:
        give(held)
        held, sems = take()
    first = sems[0].num
    assert [s.num for s in sems] == list(range(first, first + len(sems)))
    with nc.Block() as block:
        yield (block, *sems)
    nc.all_engine_barrier(sems_to_clear=range(first, first + len(sems)))
    give(held)


class Order:

    def __init__(self, engine, sem):
        self.engine, self.sem, self.n = engine, sem, 0

    def __call__(self, ins):
        ins.then_inc(self.sem, 1)
        self.n += 1
        self.engine.wait_ge(self.sem, self.n)


def product(pe, out, w, x, first, last):
    (wh, wl), (xh, xl) = w, x
    pe.matmul(out, wh, xh, start=first, stop=False)
    pe.matmul(out, wh, xl, start=False, stop=False)
    return pe.matmul(out, wl, xh, start=False, stop=last)


class Buffers:
    pass


class Constants:

    def __init__(self, tile):
        part = lambda name: tile[:, CST[name][0]:CST[name][0] + CST[name][1]]
        self.ident, self.ones, self.halves = part("ident"), part("ones"), part("halves")
        self.tri_incl, self.tri_strict = part("tri_incl"), part("tri_strict")
        self.slide, self.iota = part("slide"), part("iota")

    def attention(self, tile):
        part = lambda name: tile[:, CST2[name][0]:CST2[name][0] + CST2[name][1]]
        self.rot, self.cos, self.sin, self.band = part("rot"), part("cos"), part("sin"), part("band")


def load_stage(nc, pairs):
    with stage(nc, "loaded") as (block, loaded):
        @block.sync
        def _(sp):
            for dst, src in pairs:
                sp.dma_start(dst, src).then_inc(loaded, 16)
            sp.wait_ge(loaded, 16 * len(pairs))


def norm_stage(nc, k, src, gain, dst, shift=None, split=None):
    HALF = DC // 2
    with ExitStack() as ctx:
        sq = ctx.enter_context(sbuf(nc, "sq", [P, DC, T], F32))
        rstd = ctx.enter_context(sbuf(nc, "rstd", [P, T], F32))
        mean = ctx.enter_context(psum(nc, "mean", [P, 512], F32))
        with stage(nc, "squared", "summed", "inverse", "rooted", "scaled", "shifted", "rounded", "own") as (
                block, squared, summed, inverse, rooted, scaled, shifted, rounded, own):
            @block.scalar
            def _(act):
                for h in range(2):
                    half = slice(h * HALF, (h + 1) * HALF)
                    act.activation(sq[:, half, :], src[:, half, :], ACT.Square).then_inc(squared, 1)
                act.wait_ge(inverse, 1)
                act.activation(rstd[:], rstd[:], ACT.Sqrt).then_inc(rooted, 1)
                if shift is not None:
                    for c in range(DC):
                        act.wait_ge(scaled, c + 1)
                        act.activation(dst[:, c, :], dst[:, c, :], ACT.Identity,
                                       bias=shift[:, c:c + 1]).then_inc(shifted, 1)
                if split is not None:
                    for h in range(2):
                        half = slice(h * HALF, (h + 1) * HALF)
                        act.wait_ge(scaled if shift is None else shifted, (h + 1) * HALF)
                        act.activation(split[0][:, half, :], dst[:, half, :], ACT.Copy).then_inc(rounded, 1)

            @block.tensor
            def _(pe):
                for c in range(DC):
                    if c % HALF == 0:
                        pe.wait_ge(squared, c // HALF + 1)
                    last = pe.matmul(mean[:, 0:T], k.ones, sq[:, c, :], start=(c == 0), stop=(c == DC - 1))
                last.then_inc(summed, 1)

            @block.vector
            def _(dve):
                order = Order(dve, own)
                dve.wait_ge(summed, 1)
                order(dve.tensor_scalar(rstd[:], mean[:, 0:T], 1.0 / D, EPS, ALU.mult, ALU.add))
                dve.reciprocal(rstd[:], rstd[:]).then_inc(inverse, 1)
                dve.wait_ge(rooted, 1)
                for c in range(DC):
                    dve.scalar_tensor_tensor(dst[:, c, :], src[:, c, :], gain[:, c:c + 1], rstd[:],
                                             ALU.mult, ALU.mult).then_inc(scaled, 1)
                if split is not None:
                    for h in range(2):
                        half = slice(h * HALF, (h + 1) * HALF)
                        dve.wait_ge(rounded, h + 1)
                        dve.tensor_tensor(split[1][:, half, :], dst[:, half, :],
                                          split[0][:, half, :].bitcast(F32), ALU.subtract)


def ffn_stage(nc, k, h, x, wg, wu, wd):
    FH = FC // 2
    (hh, hl) = h
    with ExitStack() as ctx:
        raw = ctx.enter_context(sbuf(nc, "raw", [P, 2, 2, D], F32))
        wh = ctx.enter_context(sbuf(nc, "wh", [P, 2, 2, D], F32R))
        wl = ctx.enter_context(sbuf(nc, "wl", [P, 2, 2, D], F32R))
        draw = ctx.enter_context(sbuf(nc, "draw", [P, 2, FH * P], F32))
        dh = ctx.enter_context(sbuf(nc, "dh", [P, 2, FH * P], F32R))
        dl = ctx.enter_context(sbuf(nc, "dl", [P, 2, FH * P], F32R))
        sg = ctx.enter_context(sbuf(nc, "sg", [P, 2, T], F32))
        full = ctx.enter_context(sbuf(nc, "full", [P, 2, T], F32))
        guh = ctx.enter_context(sbuf(nc, "guh", [P, FC, T], F32R))
        gul = ctx.enter_context(sbuf(nc, "gul", [P, FC, T], F32R))
        gate_up = [[ctx.enter_context(psum(nc, f"{n}{i}", [P, 512], F32)) for n in ("gate", "up")]
                   for i in range(2)]
        down = [ctx.enter_context(psum(nc, f"down{i}", [P, 512], F32)) for i in range(2)]
        with stage(nc, "w_in0", "w_in1", "rounded", "split", "gate_done", "w_used", "gated", "gu_free",
                   "multiplied", "d_in0", "d_in1", "d_rounded", "d_split", "d_used", "down_free") as (
                block, w_in0, w_in1, rounded, split, gate_done, w_used, gated, gu_free, multiplied,
                d_in0, d_in1, d_rounded, d_split, d_used, down_free):
            w_in, d_in = (w_in0, w_in1), (d_in0, d_in1)

            @block.sync
            def _(sp):
                def load(n, s):
                    sp.dma_start(raw[:, s, 0, :], wg[n]).then_inc(w_in[s], 16)
                    sp.dma_start(raw[:, s, 1, :], wu[n]).then_inc(w_in[s], 16)

                for s in range(2):
                    load(s, s)
                for s in range(2):
                    sp.dma_start(draw[:, s, :], wd[s]).then_inc(d_in[s], 16)
                with sp.Fori(1, FC // 2) as i:
                    for s in range(2):
                        sp.wait_ge(split, 2 * i + (s - 1))
                        load(2 * i + s, s)
                with sp.Fori(1, DC) as i:
                    for s in range(2):
                        sp.wait_ge(d_split, 2 * i + (s - 1))
                        sp.dma_start(draw[:, s, :], wd[2 * i + s]).then_inc(d_in[s], 16)

            @block.tensor
            def _(pe):
                with pe.Fori(0, FC // 2) as i:
                    for s in range(2):
                        pe.wait_ge(split, 2 * i + (s + 1))
                        pe.wait_ge(gu_free, 2 * i + (s + 1))
                        for m in range(2):
                            for c in range(DC):
                                w = slice(c * P, (c + 1) * P)
                                last = product(pe, gate_up[s][m][:, 0:T], (wh[:, s, m, w], wl[:, s, m, w]),
                                               (hh[:, c, :], hl[:, c, :]), c == 0, c == DC - 1)
                            last.then_inc(w_used if m else gate_done, 1)
                pe.wait_ge(gu_free, FC + 2)
                with pe.Fori(0, DC // 2) as i:
                    for o in range(2):
                        pe.wait_ge(down_free, 2 * i + (o + 1))
                        for s in range(2):
                            pe.wait_ge(d_split, 4 * i + (2 * o + s + 1))
                            for f in range(FH):
                                w = slice(f * P, (f + 1) * P)
                                g = s * FH + f
                                last = product(pe, down[o][:, 0:T], (dh[:, s, w], dl[:, s, w]),
                                               (guh[:, g, :], gul[:, g, :]), g == 0, g == FC - 1)
                            last.then_inc(d_used, 1)

            @block.scalar
            def _(act):
                def high(n, s, turn):
                    act.wait_ge(w_in[s], turn)
                    act.activation(wh[:, s], raw[:, s], ACT.Copy).then_inc(rounded, 1)

                def gate(n, s):
                    act.wait_ge(gate_done, n + 1)
                    act.wait_ge(gu_free, n + 1)
                    act.activation(sg[:, s, :], gate_up[s][0][:, 0:T], ACT.Silu).then_inc(gated, 1)

                def d_high(s, turn):
                    act.wait_ge(d_in[s], turn)
                    act.activation(dh[:, s], draw[:, s], ACT.Copy).then_inc(d_rounded, 1)

                high(0, 0, 32)
                high(1, 1, 32)
                with act.Fori(0, FC // 2 - 1) as i:
                    for s in range(2):
                        gate(2 * i + s, s)
                        act.wait_ge(w_used, 2 * i + (s + 1))
                        high(2 * i + (s + 2), s, 32 * i + 64)
                for s in range(2):
                    d_high(s, 16)
                    gate(FC - 2 + s, s)
                with act.Fori(0, DC - 1) as i:
                    for s in range(2):
                        act.wait_ge(d_used, 2 * i + (s + 1))
                        d_high(s, 16 * i + 32)

            @block.vector
            def _(dve):
                def low(n, s):
                    dve.wait_ge(rounded, n + 1)
                    dve.tensor_tensor(wl[:, s], raw[:, s], wh[:, s].bitcast(F32), ALU.subtract).then_inc(split, 1)

                def gate(n, s):
                    dve.wait_ge(gated, n + 1)
                    dve.wait_ge(w_used, n + 1)
                    up = gate_up[s][1][:, 0:T]
                    dve.tensor_tensor(guh[:, n, :], sg[:, s, :], up, ALU.mult).then_inc(multiplied, 1)
                    dve.tensor_tensor(full[:, s, :], sg[:, s, :], up, ALU.mult).then_inc(multiplied, 1)
                    dve.wait_ge(multiplied, 2 * n + 2)
                    dve.tensor_tensor(gul[:, n, :], full[:, s, :], guh[:, n, :].bitcast(F32),
                                      ALU.subtract).then_inc(gu_free, 1)

                def d_low(n, s):
                    dve.wait_ge(d_rounded, n + 1)
                    dve.tensor_tensor(dl[:, s], draw[:, s], dh[:, s].bitcast(F32), ALU.subtract).then_inc(d_split, 1)

                def residual(n, o):
                    dve.wait_ge(d_used, 2 * n + 2)
                    dve.scalar_tensor_tensor(x[:, n, :], down[o][:, 0:T], 0.5, x[:, n, :],
                                             ALU.mult, ALU.add).then_inc(down_free, 1)

                dve.sem_inc(gu_free, 2)
                dve.sem_inc(down_free, 2)
                low(0, 0)
                low(1, 1)
                with dve.Fori(0, FC // 2 - 1) as i:
                    for s in range(2):
                        gate(2 * i + s, s)
                        low(2 * i + (s + 2), s)
                for s in range(2):
                    d_low(s, s)
                    gate(FC - 2 + s, s)
                with dve.Fori(0, DC // 2 - 1) as i:
                    for o in range(2):
                        for s in range(2):
                            d_low(4 * i + (2 * o + s + 2), s)
                        residual(2 * i + o, o)
                for s in range(2):
                    d_low(2 * DC - 2 + s, s)
                for o in range(2):
                    residual(DC - 2 + o, o)


def project_stage(nc, w, n, h, write):
    (hh, hl) = h
    tokens = hh.shape[2]
    with ExitStack() as ctx:
        raw = ctx.enter_context(sbuf(nc, "raw", [P, 2, D], F32))
        wh = ctx.enter_context(sbuf(nc, "wh", [P, 2, D], F32R))
        wl = ctx.enter_context(sbuf(nc, "wl", [P, 2, D], F32R))
        ps = [ctx.enter_context(psum(nc, f"ps{i}", [P, 512], F32)) for i in range(2)]
        with stage(nc, "w_in0", "w_in1", "rounded", "split", "projected", "written") as (
                block, w_in0, w_in1, rounded, split, projected, written):
            w_in = (w_in0, w_in1)

            @block.sync
            def _(sp):
                for s in range(2):
                    sp.dma_start(raw[:, s, :], w[s]).then_inc(w_in[s], 16)
                with sp.Fori(1, n // 2) as i:
                    for s in range(2):
                        sp.wait_ge(split, 2 * i + (s - 1))
                        sp.dma_start(raw[:, s, :], w[2 * i + s]).then_inc(w_in[s], 16)

            @block.scalar
            def _(act):
                for s in range(2):
                    act.wait_ge(w_in[s], 16)
                    act.activation(wh[:, s], raw[:, s], ACT.Copy).then_inc(rounded, 1)
                with act.Fori(1, n // 2) as i:
                    for s in range(2):
                        act.wait_ge(w_in[s], 16 * i + 16)
                        act.wait_ge(projected, 2 * i + (s - 1))
                        act.activation(wh[:, s], raw[:, s], ACT.Copy).then_inc(rounded, 1)

            @block.tensor
            def _(pe):
                with pe.Fori(0, n // 2) as i:
                    for s in range(2):
                        pe.wait_ge(split, 2 * i + (s + 1))
                        pe.wait_ge(written, 2 * i + (s + 1))
                        for c in range(DC):
                            part = slice(c * P, (c + 1) * P)
                            last = product(pe, ps[s][:, 0:tokens], (wh[:, s, part], wl[:, s, part]),
                                           (hh[:, c, :], hl[:, c, :]), c == 0, c == DC - 1)
                        last.then_inc(projected, 1)

            @block.vector
            def _(dve):
                def low(m, s):
                    dve.wait_ge(rounded, m + 1)
                    dve.tensor_tensor(wl[:, s], raw[:, s], wh[:, s].bitcast(F32), ALU.subtract).then_inc(split, 1)

                def out(m, s):
                    dve.wait_ge(projected, m + 1)
                    write(dve, m, ps[s], written)

                dve.sem_inc(written, 2)
                low(0, 0)
                low(1, 1)
                with dve.Fori(0, n // 2 - 1) as i:
                    for s in range(2):
                        out(2 * i + s, s)
                        low(2 * i + (s + 2), s)
                for s in range(2):
                    out(n - 2 + s, s)


def split_stage(nc, src, high, low):
    with stage(nc, "rounded") as (block, rounded):
        half = DC // 2

        @block.scalar
        def _(act):
            for h in range(2):
                part = slice(h * half, (h + 1) * half)
                act.activation(high[:, part], src[:, part], ACT.Copy).then_inc(rounded, 1)

        @block.vector
        def _(dve):
            for h in range(2):
                part = slice(h * half, (h + 1) * half)
                dve.wait_ge(rounded, h + 1)
                dve.tensor_tensor(low[:, part], src[:, part], high[:, part].bitcast(F32), ALU.subtract)


def mixer_gates(nc, k, h, proj, cols, lb, wba, wrg, b):
    col = lambda name, i=0: cols[:, COL[name][0] + i:COL[name][0] + i + 1]
    with ExitStack() as ctx:
        ba = ctx.enter_context(psum(nc, "ba", [P, TT, T], F32))
        cum = ctx.enter_context(psum(nc, "cum", [P, TT, T], F32))
        tmp = ctx.enter_context(sbuf(nc, "tmp", [P, 6, TT, 4], F32))
        ea = ctx.enter_context(sbuf(nc, "ea", [P, 4], F32))
        with stage(nc, "projected", "prepared", "exped", "logged", "betad", "decayed", "summed", "own",
                   "ea_ready") as (
                block, projected, prepared, exped, logged, betad, decayed, summed, own, ea_ready):
            @block.tensor
            def _(pe):
                for t in range(TT):
                    for c in range(DC):
                        last = pe.matmul(ba[:, t, 0:8], h[:, c, t * P:(t + 1) * P], wba[:, c, :],
                                         start=(c == 0), stop=(c == DC - 1))
                last.then_inc(projected, 1)
                pe.wait_ge(decayed, 1)
                for t in range(TT):
                    last = pe.matmul(cum[:, t, 0:4], k.tri_incl, b.g[:, t, :], start=True, stop=True)
                last.then_inc(summed, 1)

            @block.vector
            def _(dve):
                order = Order(dve, own)
                dve.wait_ge(projected, 1)
                dt = cols[:, COL["gd_dt_bias"][0]:COL["gd_dt_bias"][0] + 4]
                for t in range(TT):
                    last = dve.tensor_tensor(tmp[:, 0, t, :], ba[:, t, 4:8], dt, ALU.add)
                order(last)
                order(dve.tensor_scalar(tmp[:, 1], tmp[:, 0], -1.0, None, ALU.mult))
                dve.tensor_tensor(tmp[:, 2], tmp[:, 0], tmp[:, 1], ALU.min).then_inc(prepared, 1)
                dve.wait_ge(exped, 1)
                dve.wait_ge(logged, 1)
                order(dve.scalar_tensor_tensor(tmp[:, 4], tmp[:, 0], 0.0, tmp[:, 3], ALU.max, ALU.add))
                dve.wait_ge(ea_ready, 1)
                for t in range(TT):
                    last = dve.scalar_tensor_tensor(b.g[:, t, :], tmp[:, 4, t, :], -1.0, ea[:],
                                                    ALU.mult, ALU.mult)
                last.then_inc(decayed, 1)
                dve.wait_ge(summed, 1)
                dve.tensor_copy(b.cum[:], cum[:, :, 0:4])

            @block.scalar
            def _(act):
                act.activation(ea[:], cols[:, COL["gd_a_log"][0]:COL["gd_a_log"][0] + 4],
                               ACT.Exp).then_inc(ea_ready, 1)
                act.wait_ge(prepared, 1)
                act.activation(tmp[:, 3], tmp[:, 2], ACT.Exp).then_inc(exped, 1)
                act.wait_ge(exped, 1)
                act.activation(tmp[:, 3], tmp[:, 3], ACT.Ln, bias=1.0).then_inc(logged, 1)
                act.activation(b.beta[:], ba[:, :, 0:4], ACT.Sigmoid)

    with ExitStack() as ctx:
        conv = ctx.enter_context(sbuf(nc, "conv", [P, 14, T], F32))
        with stage(nc, "own") as (block, own):
            @block.vector
            def _(dve):
                n = 0
                chunks = [(GD_Q + c, c) for c in range(12)] + [(RG_X + c, 12 + c) for c in range(2)]
                for j in range(CONV_W):
                    for src, c in chunks:
                        base = COL["gd_conv"][0] if c < 12 else COL["rg_conv"][0] - 12 * CONV_W
                        w = cols[:, base + c * CONV_W + j:base + c * CONV_W + j + 1]
                        tap = proj[:, src, j:j + T]
                        if j == 0:
                            ins = dve.tensor_scalar(conv[:, c, :], tap, w, None, ALU.mult)
                        else:
                            dve.wait_ge(own, n - len(chunks) + 1)
                            ins = dve.scalar_tensor_tensor(conv[:, c, :], tap, w, conv[:, c, :],
                                                           ALU.mult, ALU.add)
                        ins.then_inc(own, 1)
                        n += 1

            @block.scalar
            def _(act):
                for c in range(12):
                    act.wait_ge(own, 14 * (CONV_W - 1) + c + 1)
                    act.activation(proj[:, GD_Q + c, PAD:PAD + T], conv[:, c, :], ACT.Silu)
                for c in range(2):
                    act.wait_ge(own, 14 * (CONV_W - 1) + 12 + c + 1)
                    act.activation(b.xc[:, c, :], conv[:, 12 + c, :], ACT.Identity, bias=col("rg_conv_b", c))
                for c in (HG_Q, HG_Q + 1, HG_G, HG_G + 1, GD_Z, GD_Z + 1, GD_Z + 2, GD_Z + 3):
                    act.activation(proj[:, c, PAD:PAD + T], proj[:, c, PAD:PAD + T], ACT.Silu)
                for c in range(2):
                    act.activation(b.f[:, c, :], proj[:, HG_F + c, PAD:PAD + T], ACT.Sigmoid)

    with ExitStack() as ctx:
        sq = ctx.enter_context(sbuf(nc, "sq", [P, 8, T], F32))
        inv = ctx.enter_context(sbuf(nc, "inv", [P, 8, T], F32))
        norm = [ctx.enter_context(psum(nc, f"norm{i}", [P, 2, T], F32)) for i in range(4)]
        with stage(nc, "squared", "summed", "inverse", "rooted", "own") as (
                block, squared, summed, inverse, rooted, own):
            qk = proj[:, GD_Q:GD_Q + 8, PAD:PAD + T]

            @block.scalar
            def _(act):
                act.activation(sq[:], qk, ACT.Square).then_inc(squared, 1)
                act.wait_ge(inverse, 1)
                act.activation(inv[:], inv[:], ACT.Sqrt).then_inc(rooted, 1)

            @block.tensor
            def _(pe):
                pe.wait_ge(squared, 1)
                for c in range(8):
                    last = pe.matmul(norm[c // 2][:, c % 2, :], k.ones, sq[:, c, :], start=True, stop=True)
                last.then_inc(summed, 1)

            @block.vector
            def _(dve):
                order = Order(dve, own)
                for c in range(2):
                    dve.tensor_scalar(b.f[:, c, :], b.f[:, c, :], lb[:, 2 + c:3 + c], lb[:, c:c + 1],
                                      ALU.mult, ALU.add).then_inc(own, 1)
                dve.wait_ge(own, 2)
                order.n = 2
                for c in range(2):
                    dve.tensor_scalar(b.k[:, c, :], b.f[:, c, :], -1.0, 1.0, ALU.mult, ALU.add)
                    dve.tensor_scalar(b.q[:, c, :], proj[:, HG_Q + c, PAD:PAD + T], HG_DK ** -0.5, None,
                                      ALU.mult)
                    for r in range(2):
                        dve.tensor_copy(b.f0[:, c, r, 1:T], b.f[:, c, 1:T])
                dve.memset(b.f0[:, :, :, 0:1], 0.0)
                dve.wait_ge(summed, 1)
                for c in range(4):
                    last = dve.tensor_scalar(inv[:, 2 * c:2 * c + 2, :], norm[c][:], EPS, None, ALU.add)
                order(last)
                dve.reciprocal(inv[:], inv[:]).then_inc(inverse, 1)
                dve.wait_ge(rooted, 1)
                dve.scalar_tensor_tensor(proj[:, GD_Q:GD_Q + 4, PAD:PAD + T], proj[:, GD_Q:GD_Q + 4, PAD:PAD + T],
                                         float(P) ** -0.5, inv[:, 0:4, :], ALU.mult, ALU.mult)
                dve.tensor_tensor(proj[:, GD_K:GD_K + 4, PAD:PAD + T], proj[:, GD_K:GD_K + 4, PAD:PAD + T],
                                  inv[:, 4:8, :], ALU.mult)


def picks_stage(nc, k, picks):
    with stage(nc, "made") as (block, made):
        @block.gpsimd
        def _(pool):
            for hh in range(2):
                pool.tensor_copy(picks[:, :, hh * HEAD:(hh + 1) * HEAD],
                                 k.ident[:, hh * HEAD:(hh + 1) * HEAD].unsqueeze(2).to_broadcast([P, HEAD, HEAD]))


def hgrn2_stage(nc, k, proj, b, picks, pair):
    V = HEAD
    B = 3
    with ExitStack() as ctx:
        sb = lambda name, shape, dt=F32: ctx.enter_context(sbuf(nc, name, shape, dt))
        kv, st, qs = sb("kv", [P, 2, 2, T]), sb("st", [P, B, 2, T]), sb("qs", [P, B, 2, T])
        vh, vl = sb("vh", [P, T], F32R), sb("vl", [P, T], F32R)
        rows = [ctx.enter_context(psum(nc, f"rows{i}", [P, 2, T], F32)) for i in range(B)]
        out = ctx.enter_context(psum(nc, "out", [P, 512], F32))
        steps = V // 2
        with stage(nc, "rounded", "split", "spread", "outer", "scanned", "read", "reduced") as (
                block, rounded, split, spread, outer, scanned, read, reduced):
            vv = proj[:, HG_I + pair, PAD:PAD + T]

            @block.scalar
            def _(act):
                act.activation(vh[:], vv, ACT.Copy).then_inc(rounded, 1)

            @block.tensor
            def _(pe):
                def spread_rows(n):
                    if n >= B:
                        pe.wait_ge(outer, n - B + 1)
                    for j in range(2):
                        pick = picks[:, 2 * n + j, :]
                        pe.matmul(rows[n % B][:, j, :], pick, vh[:], start=True, stop=False)
                        last = pe.matmul(rows[n % B][:, j, :], pick, vl[:], start=False, stop=True)
                    last.then_inc(spread, 1)

                pe.wait_ge(split, 1)
                spread_rows(0)
                spread_rows(1)
                for n in range(steps):
                    if n + 2 < steps:
                        spread_rows(n + 2)
                    pe.wait_ge(read, n + 1)
                    for j in range(2):
                        v = 2 * n + j
                        last = pe.matmul(out[:, 0:T], k.slide[:, V - 1 - v:V - 1 - v + P], qs[:, n % B, j, :],
                                         start=(v == 0), stop=(v == V - 1))
                    last.then_inc(reduced, 1)

            @block.vector
            def _(dve):
                kk = b.k[:, pair, :].unsqueeze(1).to_broadcast([P, 2, T])
                f0 = b.f0[:, pair, :, :].rearrange("p r t -> p (r t)")

                def outer_step(n):
                    dve.wait_ge(spread, n + 1)
                    if n >= 2:
                        dve.wait_ge(scanned, n - 1)
                    dve.tensor_tensor(kv[:, n % 2], rows[n % B][:], kk, ALU.mult).then_inc(outer, 1)

                dve.wait_ge(rounded, 1)
                dve.tensor_tensor(vl[:], vv, vh[:].bitcast(F32), ALU.subtract).then_inc(split, 1)
                outer_step(0)
                for n in range(steps):
                    if n + 1 < steps:
                        outer_step(n + 1)
                    dve.wait_ge(outer, n + 1)
                    if n >= B:
                        dve.wait_ge(read, n - B + 1)
                    dve.tensor_tensor_scan(st[:, n % B].rearrange("p r t -> p (r t)"), f0,
                                           kv[:, n % 2].rearrange("p r t -> p (r t)"), 0.0,
                                           ALU.mult, ALU.add).then_inc(scanned, 1)
                dve.wait_ge(reduced, steps)
                dve.tensor_copy(b.o[:, pair, :], out[:, 0:T])

            @block.gpsimd
            def _(pool):
                qq = b.q[:, pair, :].unsqueeze(1).to_broadcast([P, 2, T])
                for n in range(steps):
                    pool.wait_ge(scanned, n + 1)
                    if n >= B:
                        pool.wait_ge(reduced, n - B + 1)
                    pool.tensor_tensor(qs[:, n % B], st[:, n % B], qq, ALU.mult).then_inc(read, 1)


def head_norm_stage(nc, k, o, n, summing, width, weight, proj, gate, y):
    with ExitStack() as ctx:
        sq = ctx.enter_context(sbuf(nc, "sq", [P, n, T], F32))
        ms = [ctx.enter_context(psum(nc, f"ms{i}", [P, 2, T], F32)) for i in range(n // 2)]
        with stage(nc, "squared", "summed", "inverse", "rooted", "own") as (
                block, squared, summed, inverse, rooted, own):
            @block.scalar
            def _(act):
                act.activation(sq[:], o[:, 0:n, :], ACT.Square).then_inc(squared, 1)
                act.wait_ge(inverse, 1)
                act.activation(sq[:], sq[:], ACT.Sqrt).then_inc(rooted, 1)

            @block.tensor
            def _(pe):
                pe.wait_ge(squared, 1)
                for c in range(n):
                    last = pe.matmul(ms[c // 2][:, c % 2, :], summing, sq[:, c, :], start=True, stop=True)
                last.then_inc(summed, 1)

            @block.vector
            def _(dve):
                order = Order(dve, own)
                dve.wait_ge(summed, 1)
                for c in range(n // 2):
                    last = dve.tensor_scalar(sq[:, 2 * c:2 * c + 2, :], ms[c][:], 1.0 / width, EPS,
                                             ALU.mult, ALU.add)
                order(last)
                dve.reciprocal(sq[:], sq[:]).then_inc(inverse, 1)
                dve.wait_ge(rooted, 1)
                order(dve.scalar_tensor_tensor(y, o[:, 0:n, :], weight, sq[:], ALU.mult, ALU.mult))
                dve.tensor_tensor(y, y, proj[:, gate:gate + n, PAD:PAD + T], ALU.mult)


def delta_stages(nc, k, proj, b):
    H = GD_HEADS
    with ExitStack() as ctx:
        sb = lambda name, shape: ctx.enter_context(sbuf(nc, name, shape, F32))
        ktok, vtok = sb("ktok", [P, TT, H, P]), sb("vtok", [P, TT, H, P])
        crow, brow = sb("crow", [P, TT, H, P]), sb("brow", [P, TT, H, P])
        decay, sct = sb("decay", [P, TT, H, P]), sb("sct", [P, TT, H, P])
        low, lowt = sb("low", [P, TT, H, P]), sb("lowt", [P, TT, H, P])
        pst = [ctx.enter_context(psum(nc, f"pst{i}", [P, H, P], F32)) for i in range(8)]
        with stage(nc, "moved") as (block, moved):
            jobs = [(ktok, "k"), (vtok, "v"), (crow, "cum"), (brow, "beta")]

            @block.tensor
            def _(pe):
                for n, (_dst, what) in enumerate(jobs):
                    for t in range(TT):
                        tok = slice(PAD + t * P, PAD + (t + 1) * P)
                        for hh in range(H):
                            o = pst[2 * n + t][:, hh, :]
                            if what == "k":
                                last = pe.transpose(o, proj[:, GD_K + hh, tok], k.ident)
                            elif what == "v":
                                last = pe.transpose(o, proj[:, GD_V + hh, tok], k.ident)
                            elif what == "cum":
                                last = pe.matmul(o, b.g[:, t, hh:hh + 1].to_broadcast([P, P]), k.tri_incl,
                                                 start=True, stop=True)
                            else:
                                last = pe.matmul(o, b.beta[:, t, hh:hh + 1].to_broadcast([P, P]), k.ident,
                                                 start=True, stop=True)
                        last.then_inc(moved, 1)

            @block.vector
            def _(dve):
                for n in (0, 2):
                    for t in range(TT):
                        dve.wait_ge(moved, 2 * n + t + 1)
                        dve.tensor_copy(jobs[n][0][:, t], pst[2 * n + t][:])

            @block.scalar
            def _(act):
                for n in (1, 3):
                    for t in range(TT):
                        act.wait_ge(moved, 2 * n + t + 1)
                        act.activation(jobs[n][0][:, t], pst[2 * n + t][:], ACT.Copy)

        with stage(nc, "products", "differenced", "exped", "masked", "own", "lowered", "flipped") as (
                block, products, differenced, exped, masked, own, lowered, flipped):
            @block.tensor
            def _(pe):
                for t in range(TT):
                    tok = slice(PAD + t * P, PAD + (t + 1) * P)
                    for hh in range(H):
                        pe.matmul(pst[2 * t][:, hh, :], proj[:, GD_K + hh, tok], proj[:, GD_K + hh, tok],
                                  start=True, stop=True)
                    for hh in range(H):
                        last = pe.matmul(pst[2 * t + 1][:, hh, :], proj[:, GD_K + hh, tok],
                                         proj[:, GD_Q + hh, tok], start=True, stop=True)
                    last.then_inc(products, 1)
                for t in range(TT):
                    pe.wait_ge(lowered, t + 1)
                    for hh in range(H):
                        last = pe.transpose(pst[4 + t][:, hh, :], lowt[:, t, hh, :], k.ident)
                    last.then_inc(flipped, 1)

            @block.vector
            def _(dve):
                order = Order(dve, own)
                for t in range(TT):
                    for hh in range(H):
                        last = dve.tensor_scalar(decay[:, t, hh, :], crow[:, t, hh, :], b.cum[:, t, hh:hh + 1], 0.0,
                                                 ALU.subtract, ALU.min)
                    last.then_inc(differenced, 1)
                for t in range(TT):
                    incl = k.tri_incl.unsqueeze(1).to_broadcast([P, H, P])
                    strict = k.tri_strict.unsqueeze(1).to_broadcast([P, H, P])
                    dve.wait_ge(exped, t + 1)
                    order(dve.tensor_tensor(decay[:, t], decay[:, t], incl, ALU.mult))
                    dve.wait_ge(products, t + 1)
                    dve.tensor_tensor(sct[:, t], pst[2 * t + 1][:], decay[:, t], ALU.mult)
                    order(dve.tensor_tensor(lowt[:, t], pst[2 * t][:], brow[:, t], ALU.mult))
                    order(dve.tensor_tensor(lowt[:, t], lowt[:, t], decay[:, t], ALU.mult))
                    dve.tensor_tensor(lowt[:, t], lowt[:, t], strict, ALU.mult).then_inc(lowered, 1)

            @block.scalar
            def _(act):
                for t in range(TT):
                    act.wait_ge(differenced, t + 1)
                    act.activation(decay[:, t], decay[:, t], ACT.Exp).then_inc(exped, 1)
                for t in range(TT):
                    act.wait_ge(flipped, t + 1)
                    act.activation(low[:, t], pst[4 + t][:], ACT.Copy)

        xi, xit, yy = sb("xi", [P, TT, H, P]), sb("xit", [P, TT, H, P]), sb("yy", [P, TT, H, P])
        bm, bmt = sb("bm", [P, TT, H, P]), sb("bmt", [P, TT, H, P])
        LEVELS = 7
        wide = lambda ap: ap.unsqueeze(1).to_broadcast([P, H, P])
        with stage(nc, "cut", "ydone", "ycopied", "zdone", "updated", "own") as (
                block, cut, ydone, ycopied, zdone, updated, own):
            @block.vector
            def _(dve):
                order = Order(dve, own)
                for t in range(TT):
                    order(dve.tensor_tensor(bm[:, t], low[:, t], wide(k.level(0)), ALU.mult))
                    order(dve.tensor_tensor(bmt[:, t], lowt[:, t], wide(k.level_t(0)), ALU.mult))
                    dve.tensor_tensor(xi[:, t], wide(k.ident), bm[:, t], ALU.subtract).then_inc(updated, 1)
                    dve.tensor_tensor(xit[:, t], wide(k.ident), bmt[:, t], ALU.subtract).then_inc(updated, 1)
                dve.wait_ge(updated, 2 * TT)
                for lev in range(1, LEVELS):
                    for t in range(TT):
                        if lev > 1:
                            dve.wait_ge(ydone, (lev - 2) * TT + t + 1)
                        dve.tensor_tensor(bmt[:, t], lowt[:, t], wide(k.level_t(lev)), ALU.mult).then_inc(cut, 1)
                    for t in range(TT):
                        n = (lev - 1) * TT + t
                        dve.wait_ge(zdone, n + 1)
                        dve.tensor_tensor(xi[:, t], xi[:, t], pst[4 * t + 1][:], ALU.subtract).then_inc(updated, 1)
                        dve.tensor_tensor(xit[:, t], xit[:, t], pst[4 * t + 2][:],
                                          ALU.subtract).then_inc(updated, 1)

            @block.tensor
            def _(pe):
                for lev in range(1, LEVELS):
                    for t in range(TT):
                        n = (lev - 1) * TT + t
                        pe.wait_ge(cut, n + 1)
                        pe.wait_ge(updated, 2 * n + 2)
                        for hh in range(H):
                            last = pe.matmul(pst[4 * t][:, hh, :], bmt[:, t, hh, :], xi[:, t, hh, :],
                                             start=True, stop=True)
                        last.then_inc(ydone, 1)
                    for t in range(TT):
                        n = (lev - 1) * TT + t
                        pe.wait_ge(ycopied, n + 1)
                        for hh in range(H):
                            pe.matmul(pst[4 * t + 1][:, hh, :], xit[:, t, hh, :], yy[:, t, hh, :],
                                      start=True, stop=True)
                        for hh in range(H):
                            last = pe.matmul(pst[4 * t + 2][:, hh, :], yy[:, t, hh, :], xit[:, t, hh, :],
                                             start=True, stop=True)
                        last.then_inc(zdone, 1)

            @block.scalar
            def _(act):
                for lev in range(1, LEVELS):
                    for t in range(TT):
                        n = (lev - 1) * TT + t
                        act.wait_ge(ydone, n + 1)
                        if lev > 1:
                            act.wait_ge(zdone, n - TT + 1)
                        act.activation(yy[:, t], pst[4 * t][:], ACT.Copy).then_inc(ycopied, 1)

        qe, vb, kbe, kl = bm, bmt, yy, low
        erow = crow
        ecol, lcol = sb("ecol", [P, TT, H]), sb("lcol", [P, TT, H])
        with stage(nc, "exped", "last", "own") as (block, exped, lasts, own):
            @block.vector
            def _(dve):
                order = Order(dve, own)
                for t in range(TT):
                    order(dve.tensor_tensor(lcol[:, t], crow[:, t, :, P - 1], b.cum[:, t], ALU.subtract))
                lasts_ready = dve.tensor_copy(b.last[:], crow[:, :, :, P - 1])
                lasts_ready.then_inc(lasts, 1)
                dve.wait_ge(exped, 1)
                order(dve.tensor_tensor(qe[:], erow[:], proj_q(proj), ALU.mult))
                for t in range(TT):
                    order(dve.tensor_tensor(ecol[:, t], ecol[:, t], b.beta[:, t], ALU.mult))
                    for hh in range(H):
                        dve.tensor_scalar(vb[:, t, hh, :], vtok[:, t, hh, :], b.beta[:, t, hh:hh + 1], None, ALU.mult)
                        dve.tensor_scalar(kbe[:, t, hh, :], ktok[:, t, hh, :], ecol[:, t, hh:hh + 1], None, ALU.mult)
                        dve.tensor_scalar(kl[:, t, hh, :], ktok[:, t, hh, :], lcol[:, t, hh:hh + 1], None, ALU.mult)

            @block.scalar
            def _(act):
                act.wait_ge(lasts, 1)
                act.activation(erow[:], crow[:], ACT.Exp)
                act.activation(ecol[:], b.cum[:], ACT.Exp)
                act.activation(lcol[:], lcol[:], ACT.Exp)
                act.activation(b.last[:], b.last[:], ACT.Exp).then_inc(exped, 1)

        wt, vn, state = decay, vtok, ktok[:, 0]
        with stage(nc, "w_done", "w_copied", "v_done", "v_copied", "o_done", "s_done", "s_copied") as (
                block, w_done, w_copied, v_done, v_copied, o_done, s_done, s_copied):
            @block.tensor
            def _(pe):
                for t in range(TT):
                    for hh in range(H):
                        last = pe.matmul(pst[t][:, hh, :], kbe[:, t, hh, :], xit[:, t, hh, :], start=True, stop=True)
                    last.then_inc(w_done, 1)
                for t in range(TT):
                    if t:
                        pe.wait_ge(w_copied, t + 1)
                        pe.wait_ge(s_copied, t)
                    for hh in range(H):
                        last = pe.matmul(pst[2 + t][:, hh, :], xit[:, t, hh, :], vb[:, t, hh, :],
                                         start=True, stop=(t == 0))
                        if t:
                            last = pe.matmul(pst[2 + t][:, hh, :], wt[:, t, hh, :], state[:, hh, :],
                                             start=False, stop=True)
                    last.then_inc(v_done, 1)
                    pe.wait_ge(v_copied, t + 1)
                    if t + 1 < TT:
                        for hh in range(H):
                            last = pe.matmul(pst[6 + t][:, hh, :], kl[:, t, hh, :], vn[:, t, hh, :],
                                             start=True, stop=True)
                        last.then_inc(s_done, 1)
                    for hh in range(H):
                        last = pe.matmul(pst[4 + t][:, hh, :], vn[:, t, hh, :], sct[:, t, hh, :],
                                         start=True, stop=(t == 0))
                        if t:
                            last = pe.matmul(pst[4 + t][:, hh, :], state[:, hh, :], qe[:, t, hh, :],
                                             start=False, stop=True)
                    last.then_inc(o_done, 1)

            @block.scalar
            def _(act):
                for t in range(TT):
                    act.wait_ge(w_done, t + 1)
                    act.activation(wt[:, t], pst[t][:], ACT.Copy, scale=-1.0).then_inc(w_copied, 1)
                for t in range(TT):
                    act.wait_ge(o_done, t + 1)
                    act.activation(b.ogd[:, :, t * P:(t + 1) * P], pst[4 + t][:], ACT.Copy)

            @block.vector
            def _(dve):
                for t in range(TT):
                    dve.wait_ge(v_done, t + 1)
                    dve.tensor_copy(vn[:, t], pst[2 + t][:]).then_inc(v_copied, 1)
                    if t + 1 < TT:
                        dve.wait_ge(s_done, t + 1)
                        dve.tensor_copy(state, pst[6 + t][:]).then_inc(s_copied, 1)


def proj_q(proj):
    return proj[:, GD_Q:GD_Q + GD_HEADS, PAD:PAD + T].rearrange("p h (t c) -> p t h c", t=TT)


def rg_stage(nc, k, proj, cols, b, wrg, y):
    at = lambda name: COL[name][0]
    with ExitStack() as ctx:
        sb = lambda name, shape: ctx.enter_context(sbuf(nc, name, shape, F32))
        gates = sb("gates", [P, 2, 2, T])
        sp_ = sb("softplus", [P, 4, 2])
        la, a, th, bx = sb("la", [P, 2, T]), sb("a", [P, 2, T]), sb("th", [P, 2, T]), sb("bx", [P, 2, T])
        ge = sb("ge", [P, 2, T])
        ps = [ctx.enter_context(psum(nc, f"ps{i}", [P, 2, T], F32)) for i in range(2)]
        with stage(nc, "multiplied", "absed", "logged", "sigmoided", "coefficient", "exped", "ready",
                   "rooted", "own", "gelued", "aown") as (
                block, multiplied, absed, logged, sigmoided, coefficient, exped, ready, rooted, own,
                gelued, aown):
            @block.tensor
            def _(pe):
                for m in range(2):
                    for c in range(2):
                        last = pe.matmul(ps[m][:, c, :], wrg[:, m, c, :], b.xc[:, c, :], start=True, stop=True)
                last.then_inc(multiplied, 1)

            @block.vector
            def _(dve):
                order = Order(dve, own)
                lam = cols[:, at("rg_lambda"):at("rg_lambda") + 2]
                order(dve.tensor_scalar(sp_[:, 0], lam, -1.0, None, ALU.mult))
                dve.tensor_tensor(sp_[:, 1], sp_[:, 0], lam, ALU.min).then_inc(absed, 1)
                dve.wait_ge(logged, 1)
                order(dve.scalar_tensor_tensor(sp_[:, 3], sp_[:, 0], 0.0, sp_[:, 2], ALU.max, ALU.add))
                order(dve.tensor_scalar(sp_[:, 3], sp_[:, 3], -RG_C, None, ALU.mult))
                dve.wait_ge(sigmoided, 1)
                for c in range(2):
                    last = dve.tensor_scalar(la[:, c, :], gates[:, 0, c, :], sp_[:, 3, c:c + 1], None, ALU.mult)
                last.then_inc(coefficient, 1)
                order(dve.tensor_tensor(bx[:], gates[:, 1], b.xc[:], ALU.mult))
                dve.wait_ge(exped, 1)
                order(dve.tensor_tensor(la[:], a[:], a[:], ALU.mult))
                order(dve.tensor_scalar(la[:], la[:], 1.0, None, ALU.add))
                dve.scalar_tensor_tensor(th[:], th[:], -1.0, la[:], ALU.mult, ALU.mult).then_inc(ready, 1)
                dve.wait_ge(rooted, 1)
                order(dve.tensor_tensor(bx[:], bx[:], th[:], ALU.mult))
                for c in range(2):
                    last = dve.tensor_tensor_scan(la[:, c, :], a[:, c, :], bx[:, c, :], 0.0, ALU.mult, ALU.add)
                order(last)
                dve.wait_ge(gelued, 1)
                dve.tensor_tensor(y, la[:], ge[:], ALU.mult)

            @block.scalar
            def _(act):
                order = Order(act, aown)
                act.wait_ge(absed, 1)
                order(act.activation(sp_[:, 2], sp_[:, 1], ACT.Exp))
                act.activation(sp_[:, 2], sp_[:, 2], ACT.Ln, bias=1.0).then_inc(logged, 1)
                act.wait_ge(multiplied, 1)
                for m, name in enumerate(("rg_br", "rg_bi")):
                    for c in range(2):
                        last = act.activation(gates[:, m, c, :], ps[m][:, c, :], ACT.Sigmoid,
                                              bias=cols[:, at(name) + c:at(name) + c + 1])
                last.then_inc(sigmoided, 1)
                act.wait_ge(coefficient, 1)
                act.activation(a[:], la[:], ACT.Exp)
                act.activation(th[:], la[:], ACT.Tanh).then_inc(exped, 1)
                act.activation(ge[:], proj[:, RG_GATE:RG_GATE + 2, PAD:PAD + T], ACT.Gelu_apprx_tanh).then_inc(gelued, 1)
                act.wait_ge(ready, 1)
                act.activation(th[:], th[:], ACT.Sqrt).then_inc(rooted, 1)


def lower_bounds(nc, raw, lb):
    with ExitStack() as ctx:
        t = ctx.enter_context(sbuf(nc, "lbt", [P, 6, 2], F32))
        with stage(nc, "centred", "exped", "own") as (block, centred, exped, own):
            @block.vector
            def _(dve):
                order = Order(dve, own)
                order(dve.tensor_tensor(t[:, 0], raw[:, 0], raw[:, 1], ALU.max))
                order(dve.tensor_tensor(t[:, 1], raw[:, 0], t[:, 0], ALU.subtract))
                dve.tensor_tensor(t[:, 2], raw[:, 1], t[:, 0], ALU.subtract).then_inc(centred, 1)
                dve.wait_ge(exped, 1)
                order(dve.tensor_tensor(t[:, 0], t[:, 3], t[:, 4], ALU.add))
                order(dve.reciprocal(t[:, 0], t[:, 0]))
                order(dve.memset(lb[:, 0, 0:2], 0.0))
                order(dve.memset(lb[:, 0, 2:4], 1.0))
                order(dve.tensor_tensor(lb[:, 1, 0:2], t[:, 4], t[:, 0], ALU.mult))
                dve.tensor_scalar(lb[:, 1, 2:4], lb[:, 1, 0:2], -1.0, 1.0, ALU.mult, ALU.add)

            @block.scalar
            def _(act):
                act.wait_ge(centred, 1)
                act.activation(t[:, 3:5], t[:, 1:3], ACT.Exp).then_inc(exped, 1)


def first_block(nc, k, x, d):
    with ExitStack() as ctx:
        sb = lambda name, shape: ctx.enter_context(sbuf(nc, name, shape, F32))
        h = sb("h", [P, DC, T])
        hs = [ctx.enter_context(sbuf(nc, n, [P, DC, T], F32R)) for n in ("h_high", "h_low")]
        cols, lb, lbl, raw = sb("cols", [P, N_COLS]), sb("lb", [P, DEPTH, 4]), sb("lbl", [P, 4]), sb("raw", [P, DEPTH, 2])
        k.picks = ctx.enter_context(sbuf(nc, "picks", [P, HEAD, P], F32R))
        load_stage(nc, [(raw[:], d.hg_lb)])
        picks_stage(nc, k, k.picks)
        lower_bounds(nc, raw, lb)
        with nc.Fori(0, DEPTH) as layer:
            with stage(nc, "loaded") as (block, loaded):
                @block.sync
                def _(sp):
                    sp.dma_start(cols[:], d.cols[layer]).then_inc(loaded, 16)
                    sp.wait_ge(loaded, 16)

                @block.vector
                def _(dve):
                    dve.tensor_copy(lbl[:], lb[:, layer, :])
            gain = lambda name: cols[:, COL[name][0]:COL[name][0] + DC]
            norm_stage(nc, k, x, gain("norm_ffn1"), h, split=hs)
            ffn_stage(nc, k, hs, x, d.wg0[layer], d.wu0[layer], d.wd0[layer])
            norm_stage(nc, k, x, gain("norm_mix"), h, split=hs)
            mixer(nc, k, h, hs, x, cols, lbl, layer, d)
            norm_stage(nc, k, x, gain("norm_ffn2"), h, split=hs)
            ffn_stage(nc, k, hs, x, d.wg1[layer], d.wu1[layer], d.wd1[layer])


def mixer(nc, k, h, hs, x, cols, lb, layer, d):
    with ExitStack() as ctx:
        sb = lambda name, shape: ctx.enter_context(sbuf(nc, name, shape, F32))
        proj = sb("proj", [P, N_PROJ, TPAD])
        wba, wrg = sb("wba", [P, DC, 8]), sb("wrg", [P, 2, 2, P])
        b = Buffers()
        b.g, b.cum, b.beta, b.last = (sb(n, [P, TT, 4]) for n in ("g", "cumt", "beta", "last"))
        b.xc, b.f, b.k, b.q, b.o = (sb(n, [P, 2, T]) for n in ("xc", "fg", "kg", "qg", "o_hg"))
        levels = sb("levels", [P, 2, 7, P])
        k.level, k.level_t = (lambda m: levels[:, 0, m, :]), (lambda m: levels[:, 1, m, :])
        b.f0, b.ogd = sb("f0", [P, 2, 2, T]), sb("ogd", [P, GD_HEADS, T])
        with stage(nc, "loaded") as (block, loaded):
            @block.sync
            def _(sp):
                sp.dma_start(wba[:], d.wba[layer]).then_inc(loaded, 16)
                sp.dma_start(wrg[:], d.wrg[layer]).then_inc(loaded, 16)
                sp.dma_start(levels[:], d.levels).then_inc(loaded, 16)
                sp.wait_ge(loaded, 48)

            @block.vector
            def _(dve):
                dve.memset(proj[:, :, 0:PAD], 0.0)
        project_stage(nc, d.w_in[layer], N_PROJ, hs,
                      lambda dve, n, ps, done: dve.tensor_copy(proj[:, n, PAD:PAD + T], ps[:, 0:T]).then_inc(done, 1))
        mixer_gates(nc, k, h, proj, cols, lb, wba, wrg, b)
        y = h
        rg_stage(nc, k, proj, cols, b, wrg, y[:, 6:8, :])
        delta_stages(nc, k, proj, b)
        for pair in range(HG_PAIRS):
            hgrn2_stage(nc, k, proj, b, k.picks, pair)
        head_norm_stage(nc, k, b.o, 2, k.halves, HG_DK, cols[:, COL["hg_norm"][0]:COL["hg_norm"][0] + 1],
                        proj, HG_G, y[:, 0:2, :])
        head_norm_stage(nc, k, b.ogd, 4, k.ones, P, cols[:, COL["gd_norm"][0]:COL["gd_norm"][0] + 1],
                        proj, GD_Z, y[:, 2:6, :])
        split_stage(nc, y, *hs)
        project_stage(nc, d.w_out[layer], DC, hs,
                      lambda dve, n, ps, done: dve.tensor_tensor(x[:, n, :], ps[:, 0:T], x[:, n, :],
                                                                 ALU.add).then_inc(done, 1))


def modulation(nc, k, sc, w_mod, cols, layer, mod, gains):
    b_mod = COL2["b_mod"][0] + 48 * layer
    S, N = 4, 48
    with ExitStack() as ctx:
        wt = ctx.enter_context(sbuf(nc, "wt", [P, S, D], F32))
        ps = [ctx.enter_context(psum(nc, f"ps{i}", [P, 512], F32)) for i in range(S)]
        with stage(nc, "w_in0", "w_in1", "w_in2", "w_in3", "projected", "written") as (
                block, w_in0, w_in1, w_in2, w_in3, projected, written):
            w_in = (w_in0, w_in1, w_in2, w_in3)

            @block.sync
            def _(sp):
                for s in range(S):
                    sp.dma_start(wt[:, s, :], w_mod[s]).then_inc(w_in[s], 16)
                with sp.Fori(1, N // S) as i:
                    for s in range(S):
                        sp.wait_ge(projected, S * i + (s - S + 1))
                        sp.dma_start(wt[:, s, :], w_mod[S * i + s]).then_inc(w_in[s], 16)

            @block.tensor
            def _(pe):
                with pe.Fori(0, N // S) as i:
                    for s in range(S):
                        pe.wait_ge(w_in[s], 16 * i + 16)
                        pe.wait_ge(written, S * i + (s + 1))
                        for c in range(DC):
                            last = pe.matmul(ps[s][:, 0:2], wt[:, s, c * P:(c + 1) * P], sc[:, c, :],
                                             start=(c == 0), stop=(c == DC - 1))
                        last.then_inc(projected, 1)

            @block.vector
            def _(dve):
                dve.sem_inc(written, S)
                with dve.Fori(0, N // S) as i:
                    for s in range(S):
                        n = S * i + s
                        dve.wait_ge(projected, S * i + (s + 1))
                        dve.tensor_scalar(mod[:, :, n], ps[s][:, 0:2], cols[:, bass.ds(n + b_mod, 1)], None,
                                          ALU.add).then_inc(written, 1)
    with stage(nc, "own") as (block, own):
        @block.vector
        def _(dve):
            for m, name in enumerate(("norm1", "norm2")):
                a = COL2[name][0] + DC * layer
                g = cols[:, a:a + DC].unsqueeze(1).to_broadcast([P, 2, DC])
                dve.scalar_tensor_tensor(gains[:, m], mod[:, :, (3 * m + 1) * DC:(3 * m + 2) * DC], 1.0, g,
                                         ALU.add, ALU.mult)


def qkv_stage(nc, k, h, raw_w, nq, tq, rope, q, kt, v, extra=()):
    n = nq + 2
    (hh, hl) = h
    with ExitStack() as ctx:
        wh = ctx.enter_context(sbuf(nc, "wh", [P, n, D], F32R))
        wl = ctx.enter_context(sbuf(nc, "wl", [P, n, D], F32R))
        raw = ctx.enter_context(sbuf(nc, "raw", [P, nq + 1, T], F32))
        part = ctx.enter_context(sbuf(nc, "part", [P, nq + 1, 2, T], F32))
        ps = [ctx.enter_context(psum(nc, f"ps{i}", [P, 512], F32)) for i in range(n)]
        rot = [ctx.enter_context(psum(nc, f"rot{i}", [P, 512], F32)) for i in range(nq + 1)] if rope else None
        tk = 2 * T
        with stage(nc, "loaded", "rounded", "split", "projected", "raw_ready", "rotated", "own") as (
                block, loaded, rounded, split, projected, raw_ready, rotated, own):
            @block.sync
            def _(sp):
                for dst, src in extra:
                    sp.dma_start(dst, src).then_inc(loaded, 16)
                if extra:
                    sp.wait_ge(loaded, 16 * len(extra))

            @block.tensor
            def _(pe):
                for i in range(nq + 1):
                    tokens = tq if i < nq else tk
                    pe.wait_ge(split, i + 1)
                    for c in range(DC):
                        w = slice(c * P, (c + 1) * P)
                        last = product(pe, ps[i][:, 0:tokens], (wh[:, i, w], wl[:, i, w]),
                                       (hh[:, c, 0:tokens], hl[:, c, 0:tokens]), c == 0, c == DC - 1)
                    last.then_inc(projected, 1)
                pe.wait_ge(split, n)
                for t in range(tk // P):
                    tok = slice(t * P, (t + 1) * P)
                    for c in range(DC):
                        w = slice(c * P, (c + 1) * P)
                        last = product(pe, ps[nq + 1][:, tok], (hh[:, c, tok], hl[:, c, tok]),
                                       (wh[:, nq + 1, w], wl[:, nq + 1, w]), c == 0, c == DC - 1)
                last.then_inc(projected, 1)
                if rope:
                    for i in range(nq + 1):
                        pe.wait_ge(raw_ready, i + 1)
                        pe.matmul(rot[i][:, 0:T], k.rot, raw[:, i, :], start=True, stop=True).then_inc(rotated, 1)

            @block.scalar
            def _(act):
                for i in range(n):
                    act.activation(wh[:, i], raw_w[:, i], ACT.Copy).then_inc(rounded, 1)
                for i in range(nq + 1):
                    act.wait_ge(projected, i + 1)
                    scale = HEAD ** -0.5 if i < nq else 1.0
                    if rope:
                        act.activation(raw[:, i, :], ps[i][:, 0:T], ACT.Copy, scale=scale).then_inc(raw_ready, 1)
                    first = T if rope else 0
                    if i == nq:
                        act.activation(kt[:, first:tk], ps[i][:, first:tk], ACT.Copy)
                    elif tq > first:
                        for m in range(2):
                            rows = slice(m * HEAD, (m + 1) * HEAD)
                            act.activation(q[rows, 2 * i + m, first:tq], ps[i][rows, first:tq], ACT.Copy, scale=scale)
                act.wait_ge(projected, n)
                act.activation(v[:], ps[nq + 1][:].rearrange("p (t f) -> p t f", f=P), ACT.Copy)

            @block.vector
            def _(dve):
                for i in range(n):
                    dve.wait_ge(rounded, i + 1)
                    dve.tensor_tensor(wl[:, i], raw_w[:, i], wh[:, i].bitcast(F32), ALU.subtract).then_inc(split, 1)
                for i in range(nq + 1 if rope else 0):
                    dve.wait_ge(raw_ready, i + 1)
                    dve.tensor_tensor(part[:, i, 0, :], raw[:, i, :], k.cos, ALU.mult).then_inc(own, 1)
                    dve.wait_ge(rotated, i + 1)
                    dve.tensor_tensor(part[:, i, 1, :], rot[i][:, 0:T], k.sin, ALU.mult).then_inc(own, 1)
                    dve.wait_ge(own, 2 * i + 2)
                    if i == nq:
                        dve.tensor_tensor(kt[:, 0:T], part[:, i, 0, :], part[:, i, 1, :], ALU.add)
                    else:
                        for m in range(2):
                            rows = slice(m * HEAD, (m + 1) * HEAD)
                            dve.tensor_tensor(q[rows, 2 * i + m, 0:T], part[rows, i, 0, :],
                                              part[rows, i, 1, :], ALU.add)


def attend_stage(nc, k, groups, q, kt, v, width, out, ahead, bias=None, sink=None, lam=None):
    nm = len(groups[0][0])
    G = len(groups)
    K = 2 * T
    with ExitStack() as ctx:
        sb = lambda name, shape: ctx.enter_context(sbuf(nc, name, shape, F32))
        p = sb("p", [P, 2, nm, K])
        lg = sb("lg", [P, 2, K]) if bias is not None else None
        pts = sb("pts", [P, 2, K])
        neg, tot, inv, snk = (sb(n, [P, G * nm]) for n in ("neg", "tot", "inv", "snk"))
        s_ps = [ctx.enter_context(psum(nc, f"s_ps{i}", [P, 512], F32)) for i in range(2 * nm)]
        pt_ps = [ctx.enter_context(psum(nc, f"pt_ps{i}", [P, 512], F32)) for i in range(2)]
        o_ps = [ctx.enter_context(psum(nc, f"o_ps{i}", [P, 512], F32)) for i in range(2)]
        with stage(nc, "scored", "biased", "maxed", "exped", "weighted", "flipped", "flip_copied",
                   "gathered", "written", "own", "loaded") as (
                block, scored, biased, maxed, exped, weighted, flipped, flip_copied, gathered, written, own,
                loaded):
            @block.sync
            def _(sp):
                for dst, src in ahead:
                    sp.dma_start(dst, src).then_inc(loaded, 16)
                sp.wait_ge(loaded, 16 * len(ahead))

            @block.tensor
            def _(pe):
                for step in range(G + 2):
                    if step < G:
                        g = step
                        heads, qt, k0 = groups[g][:3]
                        if g >= 2:
                            pe.wait_ge(exped, (g - 1) * nm)
                        for m, head in enumerate(heads):
                            last = pe.matmul(s_ps[(g % 2) * nm + m][:, k0:K], q[:, head, qt * P:(qt + 1) * P],
                                             kt[:, k0:K], start=True, stop=True)
                        last.then_inc(scored, 1)
                    if 0 <= step - 1 < G:
                        g = step - 1
                        k0 = groups[g][2]
                        pe.wait_ge(weighted if nm == 2 else exped, g + 1)
                        if g >= 2:
                            pe.wait_ge(flip_copied, g - 1)
                        for t in range(k0 // P, K // P):
                            last = pe.transpose(pt_ps[g % 2][:, t * P:(t + 1) * P],
                                                p[:, g % 2, 0, t * P:(t + 1) * P], k.ident)
                        last.then_inc(flipped, 1)
                    if 0 <= step - 2:
                        g = step - 2
                        k0, v0 = groups[g][2:4]
                        pe.wait_ge(flip_copied, g + 1)
                        if g >= 2:
                            pe.wait_ge(written, g - 1)
                        for t in range(k0 // P, K // P):
                            last = pe.matmul(o_ps[g % 2][:, 0:width], pts[:, g % 2, t * P:(t + 1) * P],
                                             v[:, t, v0:v0 + width], start=(t == k0 // P), stop=(t == K // P - 1))
                        last.then_inc(gathered, 1)

            @block.scalar
            def _(act):
                for step in range(G + 1):
                    if step < G:
                        g = step
                        k0 = groups[g][2]
                        act.wait_ge(maxed, g + 1)
                        if g >= 2:
                            act.wait_ge(flipped, g - 1)
                        for m in range(nm):
                            i = g * nm + m
                            src = s_ps[(g % 2) * nm + m] if bias is None else lg[:, g % 2, :]
                            act.activation(p[:, g % 2, m, k0:K], src[:, k0:K], ACT.Exp, bias=neg[:, i:i + 1],
                                           accum_out=tot[:, i:i + 1]).then_inc(exped, 1)
                        if sink is not None:
                            col = groups[g][5]
                            act.activation(snk[:, g:g + 1], neg[:, g:g + 1], ACT.Exp, bias=sink[0][:, col:col + 1],
                                           ).then_inc(weighted, 1)
                    if step >= 1:
                        g = step - 1
                        k0 = groups[g][2]
                        act.wait_ge(flipped, g + 1)
                        if g >= 2:
                            act.wait_ge(gathered, g - 1)
                        act.activation(pts[:, g % 2, k0:K], pt_ps[g % 2][:, k0:K], ACT.Copy).then_inc(flip_copied, 1)

            @block.vector
            def _(dve):
                order = Order(dve, own)
                for step in range(G + 2):
                    if step < G:
                        g = step
                        _h, qt, k0, _v, bi, si = groups[g][:6]
                        dve.wait_ge(scored, g + 1)
                        if bias is not None:
                            if g >= 2:
                                dve.wait_ge(exped, g - 1)
                            s = s_ps[g % 2]
                            if k0 == 0:
                                dve.tensor_tensor(lg[:, g % 2, 0:T], s[:, 0:T], bias[bi], ALU.add)
                            order(dve.tensor_copy(lg[:, g % 2, T:K], s[:, T:K]))
                            order(dve.tensor_reduce(neg[:, g:g + 1], lg[:, g % 2, k0:K], AX, ALU.max, negate=True))
                            if sink is not None:
                                order(dve.tensor_tensor(neg[:, g:g + 1], neg[:, g:g + 1],
                                                        sink[1][:, si:si + 1], ALU.min))
                        else:
                            for m in range(nm):
                                i = g * nm + m
                                order(dve.tensor_reduce(neg[:, i:i + 1], s_ps[(g % 2) * nm + m][:, k0:K], AX,
                                                        ALU.max, negate=True))
                        dve.sem_inc(maxed, 1)
                    if 0 <= step - 1 < G:
                        g = step - 1
                        k0 = groups[g][2]
                        dve.wait_ge(exped, (g + 1) * nm)
                        one = slice(g * nm, (g + 1) * nm)
                        if sink is not None:
                            dve.wait_ge(weighted, g + 1)
                            order(dve.tensor_tensor(tot[:, one], tot[:, one], snk[:, one], ALU.add))
                        order(dve.reciprocal(inv[:, one], tot[:, one]))
                        if nm == 2:
                            order(dve.tensor_scalar(inv[:, 2 * g + 1:2 * g + 2], inv[:, 2 * g + 1:2 * g + 2], lam,
                                                    None, ALU.mult))
                            order(dve.tensor_scalar(p[:, g % 2, 0, k0:K], p[:, g % 2, 0, k0:K],
                                                    inv[:, 2 * g:2 * g + 1], None, ALU.mult))
                            dve.scalar_tensor_tensor(p[:, g % 2, 0, k0:K], p[:, g % 2, 1, k0:K],
                                                     inv[:, 2 * g + 1:2 * g + 2], p[:, g % 2, 0, k0:K],
                                                     ALU.mult, ALU.add).then_inc(weighted, 1)
                    if 0 <= step - 2:
                        g = step - 2
                        dve.wait_ge(gathered, g + 1)
                        if nm == 2:
                            dve.tensor_copy(out(groups[g][6]), o_ps[g % 2][:, 0:width]).then_inc(written, 1)
                        else:
                            dve.tensor_scalar(out(groups[g][6]), o_ps[g % 2][:, 0:width], inv[:, g:g + 1], None,
                                              ALU.mult).then_inc(written, 1)


def to_features_stage(nc, k, o, y, tiles):
    with ExitStack() as ctx:
        ps = [ctx.enter_context(psum(nc, f"ps{i}", [P, 4, P], F32)) for i in range(4)]
        n = tiles * DC // 4
        with stage(nc, "flipped", "copied") as (block, flipped, copied):
            @block.tensor
            def _(pe):
                for i in range(n):
                    if i >= 4:
                        pe.wait_ge(copied, i - 3)
                    for j in range(4):
                        t, c = divmod(4 * i + j, DC)
                        last = pe.transpose(ps[i % 4][:, j, :], o[:, t, c * P:(c + 1) * P], k.ident)
                    last.then_inc(flipped, 1)

            @block.vector
            def _(dve):
                for i in range(n):
                    t, c = divmod(4 * i, DC)
                    dve.wait_ge(flipped, i + 1)
                    dve.tensor_copy(y[:, c:c + 4, t * P:(t + 1) * P], ps[i % 4][:]).then_inc(copied, 1)


def diff_norm_stage(nc, o, tiles, weight, first):
    n = tiles * DIFF_HEADS
    with ExitStack() as ctx:
        sq = ctx.enter_context(sbuf(nc, "sq", [P, n, P], F32))
        ms = ctx.enter_context(sbuf(nc, "ms", [P, n], F32))
        with stage(nc, "own", "inverse", "rooted") as (block, own, inverse, rooted):
            part = lambda t: o[:, t, first:first + DIFF_HEADS * P].rearrange("p (h f) -> p h f", f=P)

            @block.vector
            def _(dve):
                order = Order(dve, own)
                for t in range(tiles):
                    last = dve.tensor_tensor(sq[:, t * 4:t * 4 + 4, :], part(t), part(t), ALU.mult)
                order(last)
                order(dve.tensor_reduce(ms[:], sq[:], AX, ALU.add))
                order(dve.tensor_scalar(ms[:], ms[:], 1.0 / P, EPS, ALU.mult, ALU.add))
                dve.reciprocal(ms[:], ms[:]).then_inc(inverse, 1)
                dve.wait_ge(rooted, 1)
                for t in range(tiles):
                    for hh in range(DIFF_HEADS):
                        i = t * 4 + hh
                        dve.tensor_scalar(part(t)[:, hh, :], part(t)[:, hh, :], ms[:, i:i + 1], 1.0 - LAM_INIT,
                                          ALU.mult, ALU.mult)

            @block.scalar
            def _(act):
                act.wait_ge(inverse, 1)
                act.activation(ms[:], ms[:], ACT.Sqrt).then_inc(rooted, 1)


def lambda_stage(nc, raw, lam):
    with ExitStack() as ctx:
        t = ctx.enter_context(sbuf(nc, "lam_t", [P, 2, HEAD], F32))
        s = ctx.enter_context(sbuf(nc, "lam_s", [P, 2], F32))
        with stage(nc, "own", "summed", "exped") as (block, own, summed, exped):
            @block.vector
            def _(dve):
                order = Order(dve, own)
                pairs = raw.rearrange("p (a b f) -> p a b f", a=2, b=2)
                order(dve.tensor_tensor(t[:], pairs[:, :, 0, :], pairs[:, :, 1, :], ALU.mult))
                dve.tensor_reduce(s[:], t[:], AX, ALU.add).then_inc(summed, 1)
                dve.wait_ge(exped, 1)
                order(dve.tensor_tensor(lam[:], s[:, 1:2], s[:, 0:1], ALU.subtract))
                dve.tensor_scalar(lam[:], lam[:], LAM_INIT, None, ALU.subtract)

            @block.scalar
            def _(act):
                act.wait_ge(summed, 1)
                act.activation(s[:], s[:], ACT.Exp).then_inc(exped, 1)


def clear_stage(nc, tile):
    with stage(nc, "cleared") as (block, _c):
        @block.vector
        def _(dve):
            dve.memset(tile[:], 0.0)


def even_mixer(nc, k, h, hs, x, ctx_x, cols, mod, d):
    with ExitStack() as ctx:
        sb = lambda name, shape: ctx.enter_context(sbuf(nc, name, shape, F32))
        o = sb("o", [P, 4, D])
        q, kt, v = sb("q", [P, 2, 2 * T]), sb("kt", [P, 2 * T]), sb("v", [P, 4, P])
        bias, lam = sb("bias", [P, 2, TT, T]), sb("lam", [P, 1])
        a = COL2["lambda"][0]
        lambda_stage(nc, cols[:, a:a + 4 * HEAD], lam)
        clear_stage(nc, q)
        w = d.w_even
        raw_w = sb("raw_w", [P, 3, D])
        turn = lambda a, c: [(raw_w[:, i], w[c + (a + 4 * i)]) for i in range(3)]
        load_stage(nc, turn(0, 0))
        with nc.Fori(0, 4) as c:
            qkv_stage(nc, k, hs, raw_w, 1, 2 * T, False, q, kt, v, [(bias[:], d.bias[c])])
            groups = [((m,), t, 0 if t < TT else T, m * HEAD, (m, t), None, (t, m * HEAD))
                      for t in range(4) for m in range(2)]
            attend_stage(nc, k, groups, q, kt, v, HEAD,
                         lambda at: o[:, at[0], bass.ds(c * P + at[1], HEAD)], turn(1, c),
                         bias={(m, t): bias[:, m, t, :] for m in range(2) for t in range(TT)} | {
                             (m, t): None for m in range(2) for t in (2, 3)})
        load_stage(nc, turn(12, 0))
        with nc.Fori(0, DIFF_HEADS) as c:
            qkv_stage(nc, k, hs, raw_w, 1, 2 * T, True, q, kt, v)
            groups = [((0, 1), t, 0 if t < TT else T, 0, None, None, t) for t in range(4)]
            attend_stage(nc, k, groups, q, kt, v, P,
                         lambda t: o[:, t, bass.ds(c * P + 4 * P, P)], turn(13, c), lam=lam[:])
        diff_norm_stage(nc, o, 4, None, 4 * P)
        to_features_stage(nc, k, o, h, 4)
        a = COL2["subln"][0]
        with stage(nc, "own") as (block, own):
            @block.vector
            def _(dve):
                dve.tensor_scalar(h[:, 4:8, :], h[:, 4:8, :], cols[:, a:a + 1], None, ALU.mult)

        def residual(dve, n, ps, done):
            dve.scalar_tensor_tensor(x[:, n, :], ps[:, 0:T], mod[:, 0, bass.ds(n + 2 * DC, 1)], x[:, n, :],
                                     ALU.mult, ALU.add)
            dve.scalar_tensor_tensor(ctx_x[:, n, :], ps[:, T:2 * T], mod[:, 1, bass.ds(n + 2 * DC, 1)],
                                     ctx_x[:, n, :], ALU.mult, ALU.add).then_inc(done, 1)

        split_stage(nc, h, *hs)
        project_stage(nc, d.w_out_even, DC, hs, residual)


def odd_mixer(nc, k, h, hs, x, cols, mod, d):
    with ExitStack() as ctx:
        sb = lambda name, shape: ctx.enter_context(sbuf(nc, name, shape, F32))
        o = sb("o", [P, TT, D])
        q, kt, v = sb("q", [P, 4, T]), sb("kt", [P, 2 * T]), sb("v", [P, 4, P])
        snk, nsnk = sb("snk4", [P, 4]), sb("nsnk4", [P, 4])
        clear_stage(nc, q)
        w = d.w_odd
        a = COL2["sink"][0]
        band = k.band.rearrange("p (t k) -> p t k", t=TT)
        raw_w = sb("raw_w", [P, 4, D])
        turn = lambda n: [(raw_w[:, i], w[4 * n + i]) for i in range(4)]
        load_stage(nc, turn(0))
        with nc.Fori(0, SWA_KV_HEADS) as n:
            qkv_stage(nc, k, hs, raw_w, 2, T, True, q, kt, v)
            with stage(nc, "own") as (block, own):
                @block.vector
                def _(dve):
                    dve.tensor_copy(snk[:], cols[:, bass.ds(4 * n + a, 4)])
                    dve.tensor_scalar(nsnk[:], cols[:, bass.ds(4 * n + a, 4)], -1.0, None, ALU.mult)
            groups = [((g,), t, 0, 0, t, g, (t, g * HEAD)) for t in range(TT) for g in range(4)]
            attend_stage(nc, k, groups, q, kt, v, HEAD,
                         lambda at: o[:, at[0], bass.ds(n * (4 * HEAD) + at[1], HEAD)], turn(n + 1),
                         bias=[band[:, t, :] for t in range(TT)], sink=(snk, nsnk))
        to_features_stage(nc, k, o, h, TT)
        ys = [a[:, :, 0:T] for a in hs]
        split_stage(nc, h[:, :, 0:T], *ys)
        project_stage(nc, d.w_out_odd, DC, ys,
                      lambda dve, n, ps, done: dve.scalar_tensor_tensor(
                          x[:, n, :], ps[:, 0:T], mod[:, 0, bass.ds(n + 2 * DC, 1)], x[:, n, :],
                          ALU.mult, ALU.add).then_inc(done, 1))


def peer_route(nc, k, h, keys_dram, wq, route):
    R = PEER_TOPK
    with ExitStack() as ctx:
        sb = lambda name, shape, dt=F32: ctx.enter_context(sbuf(nc, name, shape, dt))
        qp, keys = sb("qp", [P, 16, T]), sb("keys", [P, 16, P])
        load_stage(nc, [(keys[:], keys_dram)])
        project_stage(nc, wq, 16, h,
                      lambda dve, n, ps, done: dve.tensor_copy(qp[:, n, :], ps[:, 0:T]).then_inc(done, 1))
        s, s2 = sb("s", [P, 16, P]), sb("s2", [P, 16, P])
        sv, si, sif = sb("sv", [P, 16, R]), sb("si", [P, 16, R], U32), sb("sif", [P, 16, R])
        cand, cand2 = sb("cand", [P, 8, R, R]), sb("cand2", [P, 8, R * R])
        fv, fi = sb("fv", [P, 8, R]), sb("fi", [P, 8, R], U32)
        hi, hif = sb("hi", [P, 2, 8 * R], U32), sb("hif", [P, 2, 8 * R])
        eq, sm = sb("eq", [P, 8 * R, R]), sb("sm", [P, 8])
        res = sb("res", [P, 3, SLOTS])
        ps = [ctx.enter_context(psum(nc, f"ps{i}", [P, 4, P], F32)) for i in range(4)]
        pt = [ctx.enter_context(psum(nc, f"pt{i}", [P, P], F32)) for i in range(3)]
        for t in range(TT):
            with stage(nc, "scored", "own", "centred", "exped", "decoded", "flipped", "copied") as (
                    block, scored, own, centred, exped, decoded, flipped, copied):
                @block.tensor
                def _(pe):
                    for i in range(16):
                        last = pe.matmul(ps[i // 4][:, i % 4, :], qp[:, i, t * P:(t + 1) * P], keys[:, i, :],
                                         start=True, stop=True)
                        if i % 4 == 3:
                            last.then_inc(scored, 1)
                    pe.wait_ge(decoded, 1)
                    for i in range(3):
                        pe.transpose(pt[i][:], res[:, i, :], k.ident).then_inc(flipped, 1)

                @block.scalar
                def _(act):
                    for i in range(4):
                        act.wait_ge(scored, i + 1)
                        act.activation(s[:, 4 * i:4 * i + 4, :], ps[i][:], ACT.Copy).then_inc(copied, 1)
                    act.wait_ge(centred, 1)
                    act.activation(fv[:], fv[:], ACT.Exp).then_inc(exped, 1)
                    for i in range(3):
                        act.wait_ge(flipped, i + 1)
                        act.activation(route[:, i, t * P:(t + 1) * P], pt[i][:], ACT.Copy)

                @block.vector
                def _(dve):
                    order = Order(dve, own)

                    def top(values, rest, best, index, n):
                        for lo in (0, 8):
                            src = values if lo == 0 else rest
                            for i in range(n):
                                last = dve.max(best[:, i, lo:lo + 8], src[:, i, :])
                            order(last)
                            for i in range(n):
                                last = dve.max_index(index[:, i, lo:lo + 8], best[:, i, lo:lo + 8], src[:, i, :])
                                if lo == 0:
                                    last = dve.match_replace(rest[:, i, :], best[:, i, 0:8], values[:, i, :], -3e38)
                            order(last)

                    dve.wait_ge(copied, 4)
                    top(s, s2, sv, si, 16)
                    order(dve.tensor_copy(sif[:], si[:]))
                    pair = sv[:].rearrange("p (h two) r -> p h two r", two=2)
                    for hh in range(8):
                        last = dve.tensor_tensor(cand[:, hh], pair[:, hh, 0, :].unsqueeze(2).to_broadcast([P, R, R]),
                                                 pair[:, hh, 1, :].unsqueeze(1).to_broadcast([P, R, R]), ALU.add)
                    order(last)
                    flat = cand[:].rearrange("p h a b -> p h (a b)")
                    top(flat, cand2, fv, fi, 8)
                    fif = fi[:].rearrange("p h r -> p (h r)")
                    dve.tensor_scalar(hi[:, 0, :], fif, 4, None, ALU.logical_shift_right)
                    order(dve.tensor_scalar(hi[:, 1, :], fif, R - 1, None, ALU.bitwise_and))
                    order(dve.tensor_copy(hif[:], hi[:]))
                    dve.tensor_tensor(fv[:], fv[:], res_max(dve, order, sm, fv), ALU.subtract).then_inc(centred, 1)
                    sip = sif[:].rearrange("p (h two) r -> p h two r", two=2)
                    io = k.iota[:, 0:R].unsqueeze(1).to_broadcast([P, 8 * R, R])
                    for half in range(2):
                        order(dve.tensor_tensor(eq[:], hif[:, half, :].unsqueeze(2).to_broadcast([P, 8 * R, R]), io,
                                                ALU.is_equal))
                        for hh in range(8):
                            row = sip[:, hh, half, :].unsqueeze(1).to_broadcast([P, R, R])
                            e = eq[:, hh * R:(hh + 1) * R, :]
                            last = dve.tensor_tensor(e, e, row, ALU.mult)
                        order(last)
                        order(dve.tensor_reduce(res[:, half, :], eq[:], AX, ALU.add))
                    dve.wait_ge(exped, 1)
                    order(dve.tensor_reduce(sm[:], fv[:], AX, ALU.add))
                    order(dve.reciprocal(sm[:], sm[:]))
                    dve.tensor_tensor(res[:, 2, :].rearrange("p (h r) -> p h r", r=R), fv[:],
                                      sm[:].unsqueeze(2).to_broadcast([P, 8, R]), ALU.mult).then_inc(decoded, 1)


def res_max(dve, order, sm, fv):
    order(dve.tensor_copy(sm[:], fv[:, :, 0]))
    return sm[:].unsqueeze(2).to_broadcast([P, 8, PEER_TOPK])


def peer_gates(nc, k, route, gates):
    B = 4
    with ExitStack() as ctx:
        sb = lambda name, shape: ctx.enter_context(sbuf(nc, name, shape, F32))
        one, two = sb("one", [P, 2, B, P]), sb("two", [P, 2, B, P])
        ps = [ctx.enter_context(psum(nc, f"ps{i}", [P, B, P], F32)) for i in range(2)]
        with stage(nc, "spelled", "multiplied", "kept") as (block, spelled, multiplied, kept):
            @block.vector
            def _(dve):
                with dve.Fori(0, T // (2 * B)) as i:
                    for s in range(2):
                        dve.wait_ge(multiplied, 2 * i + (s + 1))
                        for j in range(B):
                            t = 2 * B * i + (s * B + j)
                            dve.tensor_scalar(one[:, s, j, :], k.iota, route[:, 0, bass.ds(t, 1)],
                                              route[:, 2, bass.ds(t, 1)], ALU.is_equal, ALU.mult)
                            last = dve.tensor_scalar(two[:, s, j, :], k.iota, route[:, 1, bass.ds(t, 1)], None,
                                                     ALU.is_equal)
                        last.then_inc(spelled, 1)

            @block.tensor
            def _(pe):
                pe.sem_inc(multiplied, 2)
                with pe.Fori(0, T // (2 * B)) as i:
                    for s in range(2):
                        pe.wait_ge(spelled, 2 * i + (s + 1))
                        pe.wait_ge(kept, 2 * i + (s + 1))
                        for j in range(B):
                            last = pe.matmul(ps[s][:, j, :], two[:, s, j, :], one[:, s, j, :], start=True, stop=True)
                        last.then_inc(multiplied, 1)

            @block.scalar
            def _(act):
                act.sem_inc(kept, 2)
                with act.Fori(0, T // (2 * B)) as i:
                    for s in range(2):
                        act.wait_ge(multiplied, 2 * i + (s + 3))
                        act.activation(gates[:, :, bass.ds(2 * B * i + s * B, B)],
                                       ps[s][:].rearrange("p t e -> p e t"), ACT.Copy).then_inc(kept, 1)


def peer_experts(nc, k, h, u, v, gates, room, x, gain):
    C = PEER_NKEYS
    (hh, hl) = h
    with ExitStack() as ctx:
        sb = lambda name, shape, dt=F32: ctx.enter_context(sbuf(nc, name, shape, dt))
        ur, vr = sb("ur", [P, 2, D]), sb("vr", [P, 2, D])
        uh, ul, vh, vl = (sb(n, [P, 2, D], F32R) for n in ("uh", "ul", "vh", "vl"))
        ga, full = room[:, 0:2, :], room[:, 2, :]
        gh, gl = sb("gh", [P, 2, T], F32R), sb("gl", [P, 2, T], F32R)
        f = gates[:, 0:TT * D // T, :].rearrange("p a b -> p (a b)").rearrange("p (t n) -> p t n", t=TT)
        a_ps = [ctx.enter_context(psum(nc, f"a_ps{i}", [P, 512], F32)) for i in range(2)]
        out = [[ctx.enter_context(psum(nc, f"out{t}{i}", [P, 512], F32)) for i in range(2)] for t in range(TT)]
        with stage(nc, "u_in0", "u_in1", "v_in0", "v_in1", "u_rounded", "u_split", "v_rounded", "v_split",
                   "scored", "gelued", "weighted", "gated", "used") as (
                block, u_in0, u_in1, v_in0, v_in1, u_rounded, u_split, v_rounded, v_split, scored,
                gelued, weighted, gated, used):
            u_in, v_in = (u_in0, u_in1), (v_in0, v_in1)

            @block.sync
            def _(sp):
                for s in range(2):
                    sp.dma_start(ur[:, s, :], u[s]).then_inc(u_in[s], 16)
                    sp.dma_start(vr[:, s, :], v[s]).then_inc(v_in[s], 16)
                with sp.Fori(1, C // 2) as i:
                    for s in range(2):
                        sp.wait_ge(u_split, 2 * i + (s - 1))
                        sp.dma_start(ur[:, s, :], u[2 * i + s]).then_inc(u_in[s], 16)
                        sp.wait_ge(v_split, 2 * i + (s - 1))
                        sp.dma_start(vr[:, s, :], v[2 * i + s]).then_inc(v_in[s], 16)

            @block.tensor
            def _(pe):
                def score(n, s):
                    pe.wait_ge(u_split, n + 1)
                    for c in range(DC):
                        w = slice(c * P, (c + 1) * P)
                        last = product(pe, a_ps[s][:, 0:T], (uh[:, s, w], ul[:, s, w]), (hh[:, c, :], hl[:, c, :]),
                                       c == 0, c == DC - 1)
                    last.then_inc(scored, 1)

                def gather(n, s, first=False, last_one=False):
                    pe.wait_ge(v_split, n + 1)
                    pe.wait_ge(gated, n + 3)
                    for t in range(TT):
                        tok = slice(t * P, (t + 1) * P)
                        for i in range(2):
                            part = slice(i * 512, (i + 1) * 512)
                            last = product(pe, out[t][i][:], (gh[:, s, tok], gl[:, s, tok]),
                                           (vh[:, s, part], vl[:, s, part]), first, last_one)
                    last.then_inc(used, 1)

                pe.sem_inc(used, 2)
                score(0, 0)
                score(1, 1)
                gather(0, 0, first=True)
                with pe.Fori(1, C // 2) as i:
                    pe.wait_ge(gelued, 2 * i - 1)
                    score(2 * i, 0)
                    gather(2 * i - 1, 1)
                    pe.wait_ge(gelued, 2 * i)
                    score(2 * i + 1, 1)
                    gather(2 * i, 0)
                gather(C - 1, 1, last_one=True)

            @block.scalar
            def _(act):
                def gelu(n, s):
                    act.wait_ge(scored, n + 1)
                    act.wait_ge(gated, n + 1)
                    act.activation(ga[:, s, :], a_ps[s][:, 0:T], ACT.Gelu).then_inc(gelued, 1)

                def u_high(s, turn):
                    act.wait_ge(u_in[s], turn)
                    act.activation(uh[:, s], ur[:, s], ACT.Copy).then_inc(u_rounded, 1)

                def v_high(n, s, turn):
                    act.wait_ge(v_in[s], turn)
                    act.wait_ge(used, n + 1)
                    act.activation(vh[:, s], vr[:, s], ACT.Copy).then_inc(v_rounded, 1)

                u_high(0, 16)
                u_high(1, 16)
                v_high(0, 0, 16)
                with act.Fori(0, C // 2 - 1) as i:
                    for s in range(2):
                        gelu(2 * i + s, s)
                        u_high(s, 16 * i + 32)
                        v_high(2 * i + (s + 1), 1 - s, 16 * i + (16 + 16 * s))
                gelu(C - 2, 0)
                v_high(C - 1, 1, 8 * C)
                gelu(C - 1, 1)

            @block.vector
            def _(dve):
                def gate(n, s):
                    dve.wait_ge(gelued, n + 1)
                    dve.wait_ge(used, n + 1)
                    g = gates[:, n, :]
                    dve.tensor_tensor(gh[:, s, :], ga[:, s, :], g, ALU.mult).then_inc(weighted, 1)
                    dve.tensor_tensor(full, ga[:, s, :], g, ALU.mult).then_inc(weighted, 1)
                    dve.wait_ge(weighted, 2 * n + 2)
                    dve.tensor_tensor(gl[:, s, :], full, gh[:, s, :].bitcast(F32), ALU.subtract).then_inc(gated, 1)

                def u_low(n, s):
                    dve.wait_ge(u_rounded, n + 1)
                    dve.tensor_tensor(ul[:, s], ur[:, s], uh[:, s].bitcast(F32), ALU.subtract).then_inc(u_split, 1)

                def v_low(n, s):
                    dve.wait_ge(v_rounded, n + 1)
                    dve.tensor_tensor(vl[:, s], vr[:, s], vh[:, s].bitcast(F32), ALU.subtract).then_inc(v_split, 1)

                dve.sem_inc(gated, 2)
                u_low(0, 0)
                u_low(1, 1)
                v_low(0, 0)
                with dve.Fori(0, C // 2 - 1) as i:
                    for s in range(2):
                        gate(2 * i + s, s)
                        dve.wait_ge(gated, 2 * i + (s + 3))
                        u_low(2 * i + (s + 2), s)
                        v_low(2 * i + (s + 1), 1 - s)
                gate(C - 2, 0)
                dve.wait_ge(gated, C + 1)
                v_low(C - 1, 1)
                gate(C - 1, 1)
                dve.wait_ge(used, C + 2)
                for t in range(TT):
                    for i in range(2):
                        dve.tensor_copy(f[:, t, i * 512:(i + 1) * 512], out[t][i][:])
        with stage(nc, "flipped", "added") as (block, flipped, added):
            @block.tensor
            def _(pe):
                for n in range(2 * TT):
                    t, half = divmod(n, 2)
                    for j in range(4):
                        c = 4 * half + j
                        last = pe.transpose(out[t][half][:, j * P:(j + 1) * P], f[:, t, c * P:(c + 1) * P], k.ident)
                    last.then_inc(flipped, 1)

            @block.vector
            def _(dve):
                for n in range(2 * TT):
                    t, half = divmod(n, 2)
                    dve.wait_ge(flipped, n + 1)
                    for j in range(4):
                        c = 4 * half + j
                        xs = x[:, c, t * P:(t + 1) * P]
                        dve.scalar_tensor_tensor(xs, out[t][half][:, j * P:(j + 1) * P], gain[:, c:c + 1], xs,
                                                 ALU.mult, ALU.add)


def peer(nc, k, h, x, gain, layer, d):
    with ExitStack() as ctx:
        route = ctx.enter_context(sbuf(nc, "route", [P, 3, T], F32))
        peer_route(nc, k, h, d.keys[layer], d.wq[layer], route)
        gates = ctx.enter_context(sbuf(nc, "gates", [P, PEER_NKEYS, T], F32))
        peer_gates(nc, k, route, gates)
        peer_experts(nc, k, h, d.u[layer], d.v[layer], gates, route, x, gain)


def second_block(nc, k, x, d):
    with ExitStack() as ctx:
        sb = lambda name, shape, dt=F32: ctx.enter_context(sbuf(nc, name, shape, dt))
        cols, sc = sb("cols2", [P, N_COLS2]), sb("sc", [P, DC, 2])
        mod, gains = sb("mod", [P, 2, 48]), sb("gains", [P, 2, 2, DC])
        ctx_x = sb("ctx_fm", [P, DC, T])
        load_stage(nc, [(cols[:], d.cols2), (ctx_x[:], d.ctx)])
        a = COL2["c"][0]
        with stage(nc, "own") as (block, own):
            @block.scalar
            def _(act):
                act.activation(sc[:].rearrange("p c t -> p (c t)"), cols[:, a:a + 2 * DC], ACT.Silu)
        for layer in range(DEPTH):
            modulation(nc, k, sc, d.w_mod[layer], cols, layer, mod, gains)
            with ExitStack() as part:
                h = part.enter_context(sbuf(nc, "h2", [P, DC, 2 * T], F32))
                hs = [part.enter_context(sbuf(nc, n, [P, DC, 2 * T], F32R)) for n in ("h2_high", "h2_low")]
                cst2 = part.enter_context(sbuf(nc, "cst2_sb", [P, N_CST2], F32))
                k.attention(cst2)
                load_stage(nc, [(cst2[:], d.cst2)])
                for kind, res in enumerate((x, ctx_x)):
                    tok = slice(kind * T, (kind + 1) * T)
                    norm_stage(nc, k, res, gains[:, 0, kind], h[:, :, tok], mod[:, kind, 0:DC],
                               [a[:, :, tok] for a in hs])
                if layer == 0:
                    even_mixer(nc, k, h, hs, x, ctx_x, cols, mod, d)
                else:
                    odd_mixer(nc, k, h, hs, x, cols, mod, d)
            for kind, res in enumerate((x, ctx_x) if layer == 0 else (x,)):
                with ExitStack() as part:
                    hs = [part.enter_context(sbuf(nc, n, [P, DC, T], F32R)) for n in ("h3_high", "h3_low")]
                    with ExitStack() as own:
                        h = own.enter_context(sbuf(nc, "h3", [P, DC, T], F32))
                        norm_stage(nc, k, res, gains[:, 1, kind], h, mod[:, kind, 3 * DC:4 * DC], hs)
                    peer(nc, k, hs, res, mod[:, kind, 5 * DC:6 * DC], layer, d)


class Data:
    pass


def fm(w):
    *lead, k, n = w.shape
    w = w.reshape(*lead, k // P, P, n // P, P)
    r = len(lead)
    w = w.transpose(*range(r), r + 2, r + 1, r, r + 3)
    return np.ascontiguousarray(w).reshape(*lead, n // P, P, k)


def by_part(v):
    v = v.reshape(*v.shape[:-1], -1, P)
    return np.ascontiguousarray(np.swapaxes(v, -1, -2))


def constants():
    i, j = np.arange(P)[:, None], np.arange(P)[None, :]
    out, out2 = np.zeros((P, N_CST), np.float32), np.zeros((P, N_CST2), np.float32)

    def put(name, v):
        to, (a, n) = (out, CST[name]) if name in CST else (out2, CST2[name])
        to[:, a:a + n] = v.reshape(P, n)

    put("ident", i == j)
    put("ones", np.ones((P, P)))
    put("halves", i // HEAD == j // HEAD)
    put("tri_incl", i <= j)
    put("tri_strict", i < j)
    s = np.arange(2 * P - HEAD - 1)[None, :]
    put("slide", s == (HEAD - 1) + HEAD * (i // HEAD))
    put("iota", np.broadcast_to(j, (P, P)))
    q = HEAD // 4
    rot = np.zeros((P, P))
    for m in range(P):
        if (m // q) % 2 == 0:
            rot[m + q, m] = -1.0
        else:
            rot[m - q, m] = 1.0
    put("rot", rot)
    t = np.arange(T)
    half = HEAD // 2
    inv = ROPE_THETA ** (-np.arange(0, half, 2, dtype=np.float32) / half)
    ar, ac = (t // GRID_W)[:, None] * inv, (t % GRID_W)[:, None] * inv
    ang = np.concatenate([ar, ar, ac, ac], axis=-1).astype(np.float32)
    put("cos", np.tile(np.cos(ang).T, (2, 1)))
    put("sin", np.tile(np.sin(ang).T, (2, 1)))
    qq, kk = np.arange(T).reshape(TT, P).T[:, :, None], np.arange(T)[None, None, :]
    put("band", np.where(np.abs(qq - kk) <= SWA_WINDOW, 0.0, NEG))
    return out, out2


def join_masks():
    i, j = np.arange(P)[:, None], np.arange(P)[None, :]
    level = np.stack([(i // (2 << m) == j // (2 << m)) & ((i >> m) % 2 == 1) & ((j >> m) % 2 == 0)
                      for m in range(7)])
    return np.stack([level.transpose(1, 0, 2), level.transpose(2, 0, 1)], axis=1).astype(np.float32)


def packed(parts, at, n, lead):
    out = np.zeros((*lead, P, n), np.float32)
    for name, v in parts.items():
        a, w = at[name]
        out[..., a:a + w] = v.reshape(*lead, P, w)
    return out


def first_arrays(v):
    w = v["w_in"]
    gd = slice(1024 + 2048, 1024 + 2048 + 8)
    main = np.concatenate([w[:, :, :gd.start], w[:, :, gd.stop:]], axis=2)
    rows = lambda a: np.broadcast_to(a[:, None, :], (DEPTH, P, a.shape[-1]))
    taps = lambda a: np.ascontiguousarray(a.reshape(DEPTH, CONV_W, -1, P).transpose(0, 3, 2, 1))
    cols = packed({
        "norm_ffn1": by_part(v["norm_ffn1"]), "norm_mix": by_part(v["norm_mix"]),
        "norm_ffn2": by_part(v["norm_ffn2"]), "hg_norm": np.tile(v["hg_norm_w"], (1, 2))[:, :, None],
        "gd_norm": v["gd_norm_w"][:, :, None], "gd_conv": taps(v["gd_conv_w"]),
        "rg_conv": taps(v["rg_conv_w"]), "rg_conv_b": by_part(v["rg_conv_b"]),
        "rg_br": by_part(v["rg_br"]), "rg_bi": by_part(v["rg_bi"]), "rg_lambda": by_part(v["rg_lambda"]),
        "gd_a_log": rows(v["gd_a_log"]), "gd_dt_bias": rows(v["gd_dt_bias"]),
    }, COL, N_COLS, (DEPTH,))
    wrg = np.zeros((DEPTH, P, 2, 2, P), np.float32)
    for m, name in enumerate(("rg_wr", "rg_wi")):
        for blk in range(4):
            c, o = blk // 2, 64 * (blk % 2)
            wrg[:, o:o + 64, m, c, o:o + 64] = v[name][:, blk]
    wd = lambda a: fm(a).reshape(DEPTH, DC, P, 2, D_FF // 2).transpose(0, 1, 3, 2, 4).reshape(DEPTH, 2 * DC, P, D_FF // 2)
    return {
        "x": np.ascontiguousarray(v["x"][0].reshape(T, DC, P).transpose(2, 1, 0)),
        "cst": constants()[0], "cst2": constants()[1], "levels": join_masks(), "cols": cols, "hg_lb": np.ascontiguousarray(v["hg_lb"].reshape(DEPTH, 2, P).transpose(2, 0, 1)),
        "wg0": fm(v["ffn1_gate"]), "wu0": fm(v["ffn1_up"]), "wd0": wd(v["ffn1_down"]),
        "wg1": fm(v["ffn2_gate"]), "wu1": fm(v["ffn2_up"]), "wd1": wd(v["ffn2_down"]),
        "w_in": fm(main), "w_out": fm(v["w_out"]),
        "wba": np.ascontiguousarray(w[:, :, gd].reshape(DEPTH, DC, P, 8).transpose(0, 2, 1, 3)),
        "wrg": wrg,
    }


def second_arrays(v):
    g = lambda n: v[n + "_2"]
    rows = lambda a: np.broadcast_to(a.reshape(1, -1), (P, a.size))
    layers = lambda a: by_part(a).transpose(1, 0, 2)
    both = np.stack([g("c")[0], g("c_ctx")])
    cols2 = packed({
        "norm1": layers(g("norm1_g")), "norm2": layers(g("norm2_g")), "b_mod": layers(g("b_mod")),
        "c": by_part(both).transpose(1, 2, 0), "final": by_part(g("final_g")),
        "norm_last": by_part(v["norm_final"]), "subln": g("diff_subln_g")[0],
        "lambda": rows(g("diff_lambda")), "sink": rows(g("swa_sink")),
    }, COL2, N_COLS2, ())
    rpb = g("na_rpb")[0]
    tok = np.arange(T)
    r, c = tok // GRID_W, tok % GRID_W
    start = np.clip(c - NA_WIN_W // 2, 0, GRID_W - NA_WIN_W)
    inside = (c[None, :] >= start[:, None]) & (c[None, :] < start[:, None] + NA_WIN_W)
    dr = r[None, :] - r[:, None] + NA_WIN_H - 1
    dc = np.clip(c[None, :] - c[:, None] + NA_WIN_W - 1, 0, 2 * NA_WIN_W - 2)
    bias = np.where(inside[None], rpb[:, dr, dc], np.float32(NEG))
    bias = bias.reshape(4, 2, TT, P, T).transpose(0, 3, 1, 2, 4)
    odd = g("w_in_odd")[0]
    nq = SWA_Q_HEADS * HEAD
    kv = odd[:, nq:].reshape(D, 2 * SWA_KV_HEADS, 1, HEAD)
    kv = np.broadcast_to(kv, (D, 2 * SWA_KV_HEADS, 2, HEAD)).reshape(D, -1)
    odd = fm(np.concatenate([odd[:, :nq], kv], axis=1))
    order = [c for n in range(SWA_KV_HEADS) for c in (2 * n, 2 * n + 1, 8 + n, 12 + n)]
    behind = lambda w, n: np.concatenate([w, np.zeros((n, P, D), w.dtype)])
    return {
        "cols2": cols2, "bias": np.ascontiguousarray(bias),
        "ctx": np.ascontiguousarray(g("ctx")[0].reshape(T, DC, P).transpose(2, 1, 0)),
        "w_mod": fm(g("w_mod")), "w_even": behind(fm(g("w_in_even")[0]), 1), "w_out_even": fm(g("w_out_even")[0]),
        "w_odd": behind(odd[order], 4), "w_out_odd": fm(g("w_out_odd")[0]),
        "wq": fm(g("peer_wq")),
        "keys": np.ascontiguousarray(g("peer_keys").reshape(DEPTH, 16, PEER_NKEYS, P).transpose(0, 3, 1, 2)),
        "u": fm(g("peer_u").transpose(0, 2, 1)),
        "v": g("peer_v").reshape(DEPTH, PEER_NKEYS, PEER_NKEYS, D),
    }


def build(nc, d, out):
    _names.clear()
    with ExitStack() as ctx:
        sb = lambda name, shape: ctx.enter_context(sbuf(nc, name, shape, F32))
        x, cst, last = sb("x_fm", [P, DC, T]), sb("cst_sb", [P, N_CST]), sb("last_cols", [P, 2 * DC])
        k = Constants(cst)
        a = COL2["final"][0]
        load_stage(nc, [(x[:], d.x), (cst[:], d.cst), (last[:], d.cols2[:, a:a + 2 * DC])])
        first_block(nc, k, x, d)
        norm_stage(nc, k, x, last[:, DC:2 * DC], x)
        second_block(nc, k, x, d)
        norm_stage(nc, k, x, last[:, 0:DC], x)
        with stage(nc, "stored") as (block, stored):
            @block.sync
            def _(sp):
                sp.dma_start(out, x[:]).then_inc(stored, 16)
                sp.wait_ge(stored, 16)


def kernel(**inputs):
    import concourse.bacc as bacc
    from concourse.bass_utils import run_bass_kernel_spmd

    v = {n: np.asarray(a) for n, a in inputs.items()}
    arrays = {**first_arrays(v), **second_arrays(v)}
    nc = bacc.Bacc("TRN2", target_bir_lowering=False, num_devices=1,
                   dynamic_dma_scratch_size=1024)
    d = Data()
    for name, a in arrays.items():
        d.__dict__[name] = nc.dram_tensor(f"in_{name}", a.shape, F32, kind="ExternalInput").ap()
    out = nc.dram_tensor("out", (P, DC, T), F32, kind="ExternalOutput").ap()
    build(nc, d, out)
    r = run_bass_kernel_spmd(nc, [{f"in_{n}": np.ascontiguousarray(a) for n, a in arrays.items()}], core_ids=[0])
    y = np.asarray(r.results[0]["out"])
    return np.ascontiguousarray(y.transpose(2, 1, 0)).reshape(1, T, D)
```

```python
from contextlib import ExitStack, contextmanager

import numpy as np

import concourse.bass as bass
from concourse import mybir

F32 = mybir.dt.float32
U32 = mybir.dt.uint32
F32R = mybir.dt.float32r
ALU = mybir.AluOpType
ACT = mybir.ActivationFunctionType
AX = mybir.AxisListType.X

P = 128
D = 1024
DC = D // P
T = 256
TT = T // P
DEPTH = 2
D_FF = 2816
FC = D_FF // P
EPS = 1e-6

HG_DK = 64
HG_PAIRS = 2
GD_HEADS = 4
RG_C = 8.0
CONV_W = 4
N_PROJ = 28
PAD = CONV_W - 1
TPAD = T + 4
HG_Q, HG_F, HG_I, HG_G, GD_Q, GD_K, GD_V, GD_Z, RG_X, RG_GATE = 0, 2, 4, 6, 8, 12, 16, 20, 24, 26

HEAD = 64
GRID_W = 64
NA_WIN_H, NA_WIN_W, NA_HEADS = 8, 16, 8
DIFF_HEADS = 4
SWA_Q_HEADS, SWA_KV_HEADS, SWA_WINDOW = 16, 4, 128
ROPE_THETA = 10000.0
NEG = -1e30
LAM_INIT = 0.8 - 0.6
PEER_HEADS, PEER_NKEYS, PEER_TOPK = 8, 128, 16
SLOTS = PEER_HEADS * PEER_TOPK
MOD_W = 512

COL, _at = {}, 0
for _name, _n in (("norm_ffn1", DC), ("norm_mix", DC), ("norm_ffn2", DC), ("hg_norm", 1),
                  ("gd_norm", 1), ("gd_conv", 12 * CONV_W), ("rg_conv", 2 * CONV_W), ("rg_conv_b", 2),
                  ("rg_br", 2), ("rg_bi", 2), ("rg_lambda", 2), ("gd_a_log", 4), ("gd_dt_bias", 4)):
    COL[_name] = (_at, _n)
    _at += _n
N_COLS = _at

COL2, _at = {}, 0
for _name, _n in (("norm1", 2 * DC), ("norm2", 2 * DC), ("b_mod", 2 * 48), ("c", 2 * DC), ("final", DC),
                  ("norm_last", DC), ("subln", 1), ("lambda", 4 * HEAD), ("sink", SWA_Q_HEADS)):
    COL2[_name] = (_at, _n)
    _at += _n
N_COLS2 = _at

CST, _at = {}, 0
for _name, _n in (("ident", P), ("ones", P), ("halves", P), ("tri_incl", P), ("tri_strict", P),
                  ("slide", 2 * P - HEAD - 1), ("iota", P)):
    CST[_name] = (_at, _n)
    _at += _n
N_CST = _at

CST2, _at = {}, 0
for _name, _n in (("rot", P), ("cos", T), ("sin", T), ("band", TT * T)):
    CST2[_name] = (_at, _n)
    _at += _n
N_CST2 = _at


_names = {}


def unique(name):
    _names[name] = _names.get(name, -1) + 1
    return f"{name}_{_names[name]}"


def sbuf(nc, name, shape, dtype):
    return nc.sbuf_tensor(unique(name), shape, dtype)


def psum(nc, name, shape, dtype):
    return nc.psum_tensor(unique(name), shape, dtype)


@contextmanager
def stage(nc, *names):
    def take():
        held = [nc.semaphore(n) for n in names]
        return held, [s.__enter__() for s in held]

    def give(held):
        for s in held:
            s.__exit__(None, None, None)

    held, sems = take()
    if sems[-1].num - sems[0].num != len(sems) - 1:
        give(held)
        held, sems = take()
    first = sems[0].num
    assert [s.num for s in sems] == list(range(first, first + len(sems)))
    with nc.Block() as block:
        yield (block, *sems)
    nc.all_engine_barrier(sems_to_clear=range(first, first + len(sems)))
    give(held)


class Order:

    def __init__(self, engine, sem):
        self.engine, self.sem, self.n = engine, sem, 0

    def __call__(self, ins):
        ins.then_inc(self.sem, 1)
        self.n += 1
        self.engine.wait_ge(self.sem, self.n)


def product(pe, out, w, x, first, last):
    (wh, wl), (xh, xl) = w, x
    pe.matmul(out, wh, xh, start=first, stop=False)
    pe.matmul(out, wh, xl, start=False, stop=False)
    return pe.matmul(out, wl, xh, start=False, stop=last)


class Buffers:
    pass


class Constants:

    def __init__(self, tile):
        part = lambda name: tile[:, CST[name][0]:CST[name][0] + CST[name][1]]
        self.ident, self.ones, self.halves = part("ident"), part("ones"), part("halves")
        self.tri_incl, self.tri_strict = part("tri_incl"), part("tri_strict")
        self.slide, self.iota = part("slide"), part("iota")

    def attention(self, tile):
        part = lambda name: tile[:, CST2[name][0]:CST2[name][0] + CST2[name][1]]
        self.rot, self.cos, self.sin, self.band = part("rot"), part("cos"), part("sin"), part("band")


def load_stage(nc, pairs):
    with stage(nc, "loaded") as (block, loaded):
        @block.sync
        def _(sp):
            for dst, src in pairs:
                sp.dma_start(dst, src).then_inc(loaded, 16)
            sp.wait_ge(loaded, 16 * len(pairs))


def norm_stage(nc, k, src, gain, dst, shift=None, split=None, loads=()):
    HALF = DC // 2
    with ExitStack() as ctx:
        sq = ctx.enter_context(sbuf(nc, "sq", [P, DC, T], F32))
        rstd = ctx.enter_context(sbuf(nc, "rstd", [P, T], F32))
        mean = ctx.enter_context(psum(nc, "mean", [P, 512], F32))
        with stage(nc, "squared", "summed", "inverse", "rooted", "scaled", "shifted", "rounded", "own",
                   "loaded") as (
                block, squared, summed, inverse, rooted, scaled, shifted, rounded, own, loaded):
            if loads:
                @block.sync
                def _(sp):
                    for a, b in loads:
                        sp.dma_start(a, b).then_inc(loaded, 16)
                    sp.wait_ge(loaded, 16 * len(loads))

            @block.scalar
            def _(act):
                for h in range(2):
                    half = slice(h * HALF, (h + 1) * HALF)
                    act.activation(sq[:, half, :], src[:, half, :], ACT.Square).then_inc(squared, 1)
                act.wait_ge(inverse, 1)
                act.activation(rstd[:], rstd[:], ACT.Sqrt).then_inc(rooted, 1)
                if shift is not None:
                    for c in range(DC):
                        act.wait_ge(scaled, c + 1)
                        act.activation(dst[:, c, :], dst[:, c, :], ACT.Identity,
                                       bias=shift[:, c:c + 1]).then_inc(shifted, 1)
                if split is not None:
                    for h in range(2):
                        half = slice(h * HALF, (h + 1) * HALF)
                        act.wait_ge(scaled if shift is None else shifted, (h + 1) * HALF)
                        act.activation(split[0][:, half, :], dst[:, half, :], ACT.Copy).then_inc(rounded, 1)

            @block.tensor
            def _(pe):
                for c in range(DC):
                    if c % HALF == 0:
                        pe.wait_ge(squared, c // HALF + 1)
                    last = pe.matmul(mean[:, 0:T], k.ones, sq[:, c, :], start=(c == 0), stop=(c == DC - 1))
                last.then_inc(summed, 1)

            @block.vector
            def _(dve):
                order = Order(dve, own)
                dve.wait_ge(summed, 1)
                order(dve.tensor_scalar(rstd[:], mean[:, 0:T], 1.0 / D, EPS, ALU.mult, ALU.add))
                dve.reciprocal(rstd[:], rstd[:]).then_inc(inverse, 1)
                dve.wait_ge(rooted, 1)
                for c in range(DC):
                    dve.scalar_tensor_tensor(dst[:, c, :], src[:, c, :], gain[:, c:c + 1], rstd[:],
                                             ALU.mult, ALU.mult).then_inc(scaled, 1)
                if split is not None:
                    for h in range(2):
                        half = slice(h * HALF, (h + 1) * HALF)
                        dve.wait_ge(rounded, h + 1)
                        dve.tensor_tensor(split[1][:, half, :], dst[:, half, :],
                                          split[0][:, half, :].bitcast(F32), ALU.subtract)


def ffn_stage(nc, k, h, x, wg, wu, wd):
    FH = FC // 2
    (hh, hl) = h
    with ExitStack() as ctx:
        raw = ctx.enter_context(sbuf(nc, "raw", [P, 2, 2, D], F32))
        wh = ctx.enter_context(sbuf(nc, "wh", [P, 2, 2, D], F32R))
        wl = ctx.enter_context(sbuf(nc, "wl", [P, 2, 2, D], F32R))
        draw = ctx.enter_context(sbuf(nc, "draw", [P, 2, FH * P], F32))
        dh = ctx.enter_context(sbuf(nc, "dh", [P, 2, FH * P], F32R))
        dl = ctx.enter_context(sbuf(nc, "dl", [P, 2, FH * P], F32R))
        sg = ctx.enter_context(sbuf(nc, "sg", [P, 2, T], F32))
        full = ctx.enter_context(sbuf(nc, "full", [P, 2, T], F32))
        guh = ctx.enter_context(sbuf(nc, "guh", [P, FC, T], F32R))
        gul = ctx.enter_context(sbuf(nc, "gul", [P, FC, T], F32R))
        gate_up = [[ctx.enter_context(psum(nc, f"{n}{i}", [P, 512], F32)) for n in ("gate", "up")]
                   for i in range(2)]
        down = [ctx.enter_context(psum(nc, f"down{i}", [P, 512], F32)) for i in range(2)]
        with stage(nc, "w_in0", "w_in1", "rounded", "split", "gate_done", "w_used", "gated", "gu_free",
                   "multiplied", "d_in0", "d_in1", "d_rounded", "d_split", "d_used", "down_free") as (
                block, w_in0, w_in1, rounded, split, gate_done, w_used, gated, gu_free, multiplied,
                d_in0, d_in1, d_rounded, d_split, d_used, down_free):
            w_in, d_in = (w_in0, w_in1), (d_in0, d_in1)

            @block.sync
            def _(sp):
                def load(n, s):
                    sp.dma_start(raw[:, s, 0, :], wg[n]).then_inc(w_in[s], 16)
                    sp.dma_start(raw[:, s, 1, :], wu[n]).then_inc(w_in[s], 16)

                for s in range(2):
                    load(s, s)
                for s in range(2):
                    sp.dma_start(draw[:, s, :], wd[s]).then_inc(d_in[s], 16)
                with sp.Fori(1, FC // 2) as i:
                    for s in range(2):
                        sp.wait_ge(split, 2 * i + (s - 1))
                        load(2 * i + s, s)
                with sp.Fori(1, DC) as i:
                    for s in range(2):
                        sp.wait_ge(d_split, 2 * i + (s - 1))
                        sp.dma_start(draw[:, s, :], wd[2 * i + s]).then_inc(d_in[s], 16)

            @block.tensor
            def _(pe):
                with pe.Fori(0, FC // 2) as i:
                    for s in range(2):
                        pe.wait_ge(split, 2 * i + (s + 1))
                        pe.wait_ge(gu_free, 2 * i + (s + 1))
                        for m in range(2):
                            for c in range(DC):
                                w = slice(c * P, (c + 1) * P)
                                last = product(pe, gate_up[s][m][:, 0:T], (wh[:, s, m, w], wl[:, s, m, w]),
                                               (hh[:, c, :], hl[:, c, :]), c == 0, c == DC - 1)
                            last.then_inc(w_used if m else gate_done, 1)
                pe.wait_ge(gu_free, FC + 2)
                with pe.Fori(0, DC // 2) as i:
                    for o in range(2):
                        pe.wait_ge(down_free, 2 * i + (o + 1))
                        for s in range(2):
                            pe.wait_ge(d_split, 4 * i + (2 * o + s + 1))
                            for f in range(FH):
                                w = slice(f * P, (f + 1) * P)
                                g = s * FH + f
                                last = product(pe, down[o][:, 0:T], (dh[:, s, w], dl[:, s, w]),
                                               (guh[:, g, :], gul[:, g, :]), g == 0, g == FC - 1)
                            last.then_inc(d_used, 1)

            @block.scalar
            def _(act):
                def high(n, s, turn):
                    act.wait_ge(w_in[s], turn)
                    act.activation(wh[:, s], raw[:, s], ACT.Copy).then_inc(rounded, 1)

                def gate(n, s):
                    act.wait_ge(gate_done, n + 1)
                    act.wait_ge(gu_free, n + 1)
                    act.activation(sg[:, s, :], gate_up[s][0][:, 0:T], ACT.Silu).then_inc(gated, 1)

                def d_high(s, turn):
                    act.wait_ge(d_in[s], turn)
                    act.activation(dh[:, s], draw[:, s], ACT.Copy).then_inc(d_rounded, 1)

                high(0, 0, 32)
                high(1, 1, 32)
                with act.Fori(0, FC // 2 - 1) as i:
                    for s in range(2):
                        gate(2 * i + s, s)
                        act.wait_ge(w_used, 2 * i + (s + 1))
                        high(2 * i + (s + 2), s, 32 * i + 64)
                for s in range(2):
                    d_high(s, 16)
                    gate(FC - 2 + s, s)
                with act.Fori(0, DC - 1) as i:
                    for s in range(2):
                        act.wait_ge(d_used, 2 * i + (s + 1))
                        d_high(s, 16 * i + 32)

            @block.vector
            def _(dve):
                def low(n, s):
                    dve.wait_ge(rounded, n + 1)
                    dve.tensor_tensor(wl[:, s], raw[:, s], wh[:, s].bitcast(F32), ALU.subtract).then_inc(split, 1)

                def gate(n, s):
                    dve.wait_ge(gated, n + 1)
                    dve.wait_ge(w_used, n + 1)
                    up = gate_up[s][1][:, 0:T]
                    dve.tensor_tensor(guh[:, n, :], sg[:, s, :], up, ALU.mult).then_inc(multiplied, 1)
                    dve.tensor_tensor(full[:, s, :], sg[:, s, :], up, ALU.mult).then_inc(multiplied, 1)
                    dve.wait_ge(multiplied, 2 * n + 2)
                    dve.tensor_tensor(gul[:, n, :], full[:, s, :], guh[:, n, :].bitcast(F32),
                                      ALU.subtract).then_inc(gu_free, 1)

                def d_low(n, s):
                    dve.wait_ge(d_rounded, n + 1)
                    dve.tensor_tensor(dl[:, s], draw[:, s], dh[:, s].bitcast(F32), ALU.subtract).then_inc(d_split, 1)

                def residual(n, o):
                    dve.wait_ge(d_used, 2 * n + 2)
                    dve.scalar_tensor_tensor(x[:, n, :], down[o][:, 0:T], 0.5, x[:, n, :],
                                             ALU.mult, ALU.add).then_inc(down_free, 1)

                dve.sem_inc(gu_free, 2)
                dve.sem_inc(down_free, 2)
                low(0, 0)
                low(1, 1)
                with dve.Fori(0, FC // 2 - 1) as i:
                    for s in range(2):
                        gate(2 * i + s, s)
                        low(2 * i + (s + 2), s)
                for s in range(2):
                    d_low(s, s)
                    gate(FC - 2 + s, s)
                with dve.Fori(0, DC // 2 - 1) as i:
                    for o in range(2):
                        for s in range(2):
                            d_low(4 * i + (2 * o + s + 2), s)
                        residual(2 * i + o, o)
                for s in range(2):
                    d_low(2 * DC - 2 + s, s)
                for o in range(2):
                    residual(DC - 2 + o, o)


def project_stage(nc, w, n, h, write, loads=()):
    (hh, hl) = h
    tokens = hh.shape[2]
    G = 2
    turn = 2 * G
    with ExitStack() as ctx:
        raw = ctx.enter_context(sbuf(nc, "raw", [P, 2, G, D], F32))
        wh = ctx.enter_context(sbuf(nc, "wh", [P, 2, D], F32R))
        wl = ctx.enter_context(sbuf(nc, "wl", [P, 2, D], F32R))
        ps = [ctx.enter_context(psum(nc, f"ps{i}", [P, 512], F32)) for i in range(2)]
        with stage(nc, "w_in0", "w_in1", "rounded", "split", "projected", "written", "loaded") as (
                block, w_in0, w_in1, rounded, split, projected, written, loaded):
            w_in = (w_in0, w_in1)

            @block.sync
            def _(sp):
                def load(first, s):
                    sp.dma_start(raw[:, s], w[bass.ds(first, G)].rearrange("n p m -> p n m")).then_inc(w_in[s], 16)

                load(0, 0)
                load(G, 1)
                for dst, src in loads:
                    sp.dma_start(dst, src).then_inc(loaded, 16)
                with sp.Fori(1, n // turn) as i:
                    for s in range(2):
                        sp.wait_ge(split, turn * i + (G * (s + 1) - turn))
                        load(turn * i + G * s, s)
                if loads:
                    sp.wait_ge(loaded, 16 * len(loads))

            @block.scalar
            def _(act):
                def high(s, j):
                    act.activation(wh[:, j], raw[:, s, j], ACT.Copy).then_inc(rounded, 1)

                with act.Fori(0, n // turn) as i:
                    for s in range(2):
                        act.wait_ge(w_in[s], 16 * i + 16)
                        for j in range(G):
                            act.wait_ge(projected, turn * i + (G * s + j + 1))
                            high(s, j)

            @block.tensor
            def _(pe):
                pe.sem_inc(projected, 2)
                with pe.Fori(0, n // 2) as i:
                    for s in range(2):
                        pe.wait_ge(split, 2 * i + (s + 1))
                        pe.wait_ge(written, 2 * i + (s + 1))
                        for c in range(DC):
                            part = slice(c * P, (c + 1) * P)
                            last = product(pe, ps[s][:, 0:tokens], (wh[:, s, part], wl[:, s, part]),
                                           (hh[:, c, :], hl[:, c, :]), c == 0, c == DC - 1)
                        last.then_inc(projected, 1)

            @block.vector
            def _(dve):
                def low(m, s, j):
                    dve.wait_ge(rounded, m + 1)
                    dve.tensor_tensor(wl[:, j], raw[:, s, j], wh[:, j].bitcast(F32), ALU.subtract).then_inc(split, 1)

                def out(m, j):
                    dve.wait_ge(projected, m + 3)
                    write(dve, m, ps[j], written)

                dve.sem_inc(written, 2)
                low(0, 0, 0)
                low(1, 0, 1)
                with dve.Fori(0, n // turn - 1) as i:
                    for m in range(turn):
                        out(turn * i + m, m % G)
                        low(turn * i + (m + 2), (m // G + 1) % 2, m % G)
                for m in range(turn):
                    out(n - turn + m, m % G)
                    if m + 2 < turn:
                        low(n - turn + m + 2, 1, m % G)


def split_stage(nc, src, high, low):
    with stage(nc, "rounded") as (block, rounded):
        half = DC // 2

        @block.scalar
        def _(act):
            for h in range(2):
                part = slice(h * half, (h + 1) * half)
                act.activation(high[:, part], src[:, part], ACT.Copy).then_inc(rounded, 1)

        @block.vector
        def _(dve):
            for h in range(2):
                part = slice(h * half, (h + 1) * half)
                dve.wait_ge(rounded, h + 1)
                dve.tensor_tensor(low[:, part], src[:, part], high[:, part].bitcast(F32), ALU.subtract)


def mixer_gates(nc, k, h, proj, cols, lb, wba, wrg, b):
    col = lambda name, i=0: cols[:, COL[name][0] + i:COL[name][0] + i + 1]
    with ExitStack() as ctx:
        ba = ctx.enter_context(psum(nc, "ba", [P, TT, T], F32))
        cum = ctx.enter_context(psum(nc, "cum", [P, TT, T], F32))
        tmp = ctx.enter_context(sbuf(nc, "tmp", [P, 6, TT, 4], F32))
        ea = ctx.enter_context(sbuf(nc, "ea", [P, 4], F32))
        with stage(nc, "projected", "prepared", "exped", "logged", "betad", "decayed", "summed", "own",
                   "ea_ready") as (
                block, projected, prepared, exped, logged, betad, decayed, summed, own, ea_ready):
            @block.tensor
            def _(pe):
                for t in range(TT):
                    for c in range(DC):
                        last = pe.matmul(ba[:, t, 0:8], h[:, c, t * P:(t + 1) * P], wba[:, c, :],
                                         start=(c == 0), stop=(c == DC - 1))
                last.then_inc(projected, 1)
                pe.wait_ge(decayed, 1)
                for t in range(TT):
                    last = pe.matmul(cum[:, t, 0:4], k.tri_incl, b.g[:, t, :], start=True, stop=True)
                last.then_inc(summed, 1)

            @block.vector
            def _(dve):
                order = Order(dve, own)
                dve.wait_ge(projected, 1)
                dt = cols[:, COL["gd_dt_bias"][0]:COL["gd_dt_bias"][0] + 4]
                for t in range(TT):
                    last = dve.tensor_tensor(tmp[:, 0, t, :], ba[:, t, 4:8], dt, ALU.add)
                order(last)
                order(dve.tensor_scalar(tmp[:, 1], tmp[:, 0], -1.0, None, ALU.mult))
                dve.tensor_tensor(tmp[:, 2], tmp[:, 0], tmp[:, 1], ALU.min).then_inc(prepared, 1)
                dve.wait_ge(exped, 1)
                dve.wait_ge(logged, 1)
                order(dve.scalar_tensor_tensor(tmp[:, 4], tmp[:, 0], 0.0, tmp[:, 3], ALU.max, ALU.add))
                dve.wait_ge(ea_ready, 1)
                for t in range(TT):
                    last = dve.scalar_tensor_tensor(b.g[:, t, :], tmp[:, 4, t, :], -1.0, ea[:],
                                                    ALU.mult, ALU.mult)
                last.then_inc(decayed, 1)
                dve.wait_ge(summed, 1)
                dve.tensor_copy(b.cum[:], cum[:, :, 0:4])

            @block.scalar
            def _(act):
                act.activation(ea[:], cols[:, COL["gd_a_log"][0]:COL["gd_a_log"][0] + 4],
                               ACT.Exp).then_inc(ea_ready, 1)
                act.wait_ge(prepared, 1)
                act.activation(tmp[:, 3], tmp[:, 2], ACT.Exp).then_inc(exped, 1)
                act.wait_ge(exped, 1)
                act.activation(tmp[:, 3], tmp[:, 3], ACT.Ln, bias=1.0).then_inc(logged, 1)
                act.activation(b.beta[:], ba[:, :, 0:4], ACT.Sigmoid)

    with ExitStack() as ctx:
        conv = ctx.enter_context(sbuf(nc, "conv", [P, 14, T], F32))
        with stage(nc, "own") as (block, own):
            @block.vector
            def _(dve):
                n = 0
                chunks = [(GD_Q + c, c) for c in range(12)] + [(RG_X + c, 12 + c) for c in range(2)]
                for j in range(CONV_W):
                    for src, c in chunks:
                        base = COL["gd_conv"][0] if c < 12 else COL["rg_conv"][0] - 12 * CONV_W
                        w = cols[:, base + c * CONV_W + j:base + c * CONV_W + j + 1]
                        tap = proj[:, src, j:j + T]
                        if j == 0:
                            ins = dve.tensor_scalar(conv[:, c, :], tap, w, None, ALU.mult)
                        else:
                            dve.wait_ge(own, n - len(chunks) + 1)
                            ins = dve.scalar_tensor_tensor(conv[:, c, :], tap, w, conv[:, c, :],
                                                           ALU.mult, ALU.add)
                        ins.then_inc(own, 1)
                        n += 1

            @block.scalar
            def _(act):
                for c in range(12):
                    act.wait_ge(own, 14 * (CONV_W - 1) + c + 1)
                    act.activation(proj[:, GD_Q + c, PAD:PAD + T], conv[:, c, :], ACT.Silu)
                for c in range(2):
                    act.wait_ge(own, 14 * (CONV_W - 1) + 12 + c + 1)
                    act.activation(b.xc[:, c, :], conv[:, 12 + c, :], ACT.Identity, bias=col("rg_conv_b", c))
                for c in (HG_Q, HG_Q + 1, HG_G, HG_G + 1, GD_Z, GD_Z + 1, GD_Z + 2, GD_Z + 3):
                    act.activation(proj[:, c, PAD:PAD + T], proj[:, c, PAD:PAD + T], ACT.Silu)
                for c in range(2):
                    act.activation(b.f[:, c, :], proj[:, HG_F + c, PAD:PAD + T], ACT.Sigmoid)

    with ExitStack() as ctx:
        sq = ctx.enter_context(sbuf(nc, "sq", [P, 8, T], F32))
        inv = ctx.enter_context(sbuf(nc, "inv", [P, 8, T], F32))
        norm = [ctx.enter_context(psum(nc, f"norm{i}", [P, 2, T], F32)) for i in range(4)]
        with stage(nc, "squared", "summed", "inverse", "rooted", "own") as (
                block, squared, summed, inverse, rooted, own):
            qk = proj[:, GD_Q:GD_Q + 8, PAD:PAD + T]

            @block.scalar
            def _(act):
                act.activation(sq[:], qk, ACT.Square).then_inc(squared, 1)
                act.wait_ge(inverse, 1)
                act.activation(inv[:], inv[:], ACT.Sqrt).then_inc(rooted, 1)

            @block.tensor
            def _(pe):
                pe.wait_ge(squared, 1)
                for c in range(8):
                    last = pe.matmul(norm[c // 2][:, c % 2, :], k.ones, sq[:, c, :], start=True, stop=True)
                last.then_inc(summed, 1)

            @block.vector
            def _(dve):
                order = Order(dve, own)
                for c in range(2):
                    dve.tensor_scalar(b.f[:, c, :], b.f[:, c, :], lb[:, 2 + c:3 + c], lb[:, c:c + 1],
                                      ALU.mult, ALU.add).then_inc(own, 1)
                dve.wait_ge(own, 2)
                order.n = 2
                for c in range(2):
                    dve.tensor_scalar(b.k[:, c, :], b.f[:, c, :], -1.0, 1.0, ALU.mult, ALU.add)
                    dve.tensor_scalar(b.q[:, c, :], proj[:, HG_Q + c, PAD:PAD + T], HG_DK ** -0.5, None,
                                      ALU.mult)
                    for r in range(2):
                        dve.tensor_copy(b.f0[:, c, r, 1:T], b.f[:, c, 1:T])
                dve.memset(b.f0[:, :, :, 0:1], 0.0)
                dve.wait_ge(summed, 1)
                for c in range(4):
                    last = dve.tensor_scalar(inv[:, 2 * c:2 * c + 2, :], norm[c][:], EPS, None, ALU.add)
                order(last)
                dve.reciprocal(inv[:], inv[:]).then_inc(inverse, 1)
                dve.wait_ge(rooted, 1)
                dve.scalar_tensor_tensor(proj[:, GD_Q:GD_Q + 4, PAD:PAD + T], proj[:, GD_Q:GD_Q + 4, PAD:PAD + T],
                                         float(P) ** -0.5, inv[:, 0:4, :], ALU.mult, ALU.mult)
                dve.tensor_tensor(proj[:, GD_K:GD_K + 4, PAD:PAD + T], proj[:, GD_K:GD_K + 4, PAD:PAD + T],
                                  inv[:, 4:8, :], ALU.mult)


def picks_stage(nc, k, picks):
    def spread(hh, first, last):
        columns = slice(hh * HEAD + first, hh * HEAD + last)
        return (picks[:, first:last, hh * HEAD:(hh + 1) * HEAD],
                k.ident[:, columns].unsqueeze(2).to_broadcast([P, last - first, HEAD]))

    half = HEAD // 2
    with stage(nc, "made") as (block, made):
        @block.vector
        def _(dve):
            dve.tensor_copy(*spread(0, 0, HEAD))

        @block.scalar
        def _(act):
            dst, src = spread(1, 0, half)
            act.activation(dst, src, ACT.Copy)

        @block.gpsimd
        def _(pool):
            pool.tensor_copy(*spread(1, half, HEAD))


def hgrn2_stage(nc, k, proj, b, picks, pair):
    V = HEAD
    R, AHEAD, K, B = 6, 4, 3, 4
    with ExitStack() as ctx:
        sb = lambda name, shape, dt=F32: ctx.enter_context(sbuf(nc, name, shape, dt))
        kv, st, qs = sb("kv", [P, K, 2, T]), sb("st", [P, B, 2, T]), sb("qs", [P, B, 2, T])
        vh, vl = sb("vh", [P, T], F32R), sb("vl", [P, T], F32R)
        rows = [ctx.enter_context(psum(nc, f"rows{i}", [P, 2, T], F32)) for i in range(R)]
        out = ctx.enter_context(psum(nc, "out", [P, 512], F32))
        steps = V // 2
        with stage(nc, "rounded", "split", "spread", "outer", "scanned", "read", "reduced") as (
                block, rounded, split, spread, outer, scanned, read, reduced):
            vv = proj[:, HG_I + pair, PAD:PAD + T]

            @block.scalar
            def _(act):
                act.activation(vh[:], vv, ACT.Copy).then_inc(rounded, 1)

            @block.tensor
            def _(pe):
                def spread_rows(n):
                    if n >= R:
                        pe.wait_ge(outer, n - R + 1)
                    for j in range(2):
                        pick = picks[:, 2 * n + j, :]
                        pe.matmul(rows[n % R][:, j, :], pick, vh[:], start=True, stop=False)
                        last = pe.matmul(rows[n % R][:, j, :], pick, vl[:], start=False, stop=True)
                    last.then_inc(spread, 1)

                pe.wait_ge(split, 1)
                for n in range(AHEAD):
                    spread_rows(n)
                for n in range(steps):
                    if n + AHEAD < steps:
                        spread_rows(n + AHEAD)
                    pe.wait_ge(read, n + 1)
                    for j in range(2):
                        v = 2 * n + j
                        last = pe.matmul(out[:, 0:T], k.slide[:, V - 1 - v:V - 1 - v + P], qs[:, n % B, j, :],
                                         start=(v == 0), stop=(v == V - 1))
                    last.then_inc(reduced, 1)

            @block.vector
            def _(dve):
                kk = b.k[:, pair, :].unsqueeze(1).to_broadcast([P, 2, T])
                f0 = b.f0[:, pair, :, :].rearrange("p r t -> p (r t)")

                def outer_step(n):
                    dve.wait_ge(spread, n + 1)
                    if n >= K:
                        dve.wait_ge(scanned, n - K + 1)
                    dve.tensor_tensor(kv[:, n % K], rows[n % R][:], kk, ALU.mult).then_inc(outer, 1)

                dve.wait_ge(rounded, 1)
                dve.tensor_tensor(vl[:], vv, vh[:].bitcast(F32), ALU.subtract).then_inc(split, 1)
                outer_step(0)
                for n in range(steps):
                    if n + 1 < steps:
                        outer_step(n + 1)
                    dve.wait_ge(outer, n + 1)
                    if n >= B:
                        dve.wait_ge(read, n - B + 1)
                    dve.tensor_tensor_scan(st[:, n % B].rearrange("p r t -> p (r t)"), f0,
                                           kv[:, n % K].rearrange("p r t -> p (r t)"), 0.0,
                                           ALU.mult, ALU.add).then_inc(scanned, 1)
                dve.wait_ge(reduced, steps)
                dve.tensor_copy(b.o[:, pair, :], out[:, 0:T])

            @block.gpsimd
            def _(pool):
                qq = b.q[:, pair, :].unsqueeze(1).to_broadcast([P, 2, T])
                for n in range(steps):
                    pool.wait_ge(scanned, n + 1)
                    if n >= B:
                        pool.wait_ge(reduced, n - B + 1)
                    pool.tensor_tensor(qs[:, n % B], st[:, n % B], qq, ALU.mult).then_inc(read, 1)


def head_norm_stage(nc, k, o, n, summing, width, weight, proj, gate, y):
    with ExitStack() as ctx:
        sq = ctx.enter_context(sbuf(nc, "sq", [P, n, T], F32))
        ms = [ctx.enter_context(psum(nc, f"ms{i}", [P, 2, T], F32)) for i in range(n // 2)]
        with stage(nc, "squared", "summed", "inverse", "rooted", "own") as (
                block, squared, summed, inverse, rooted, own):
            @block.scalar
            def _(act):
                act.activation(sq[:], o[:, 0:n, :], ACT.Square).then_inc(squared, 1)
                act.wait_ge(inverse, 1)
                act.activation(sq[:], sq[:], ACT.Sqrt).then_inc(rooted, 1)

            @block.tensor
            def _(pe):
                pe.wait_ge(squared, 1)
                for c in range(n):
                    last = pe.matmul(ms[c // 2][:, c % 2, :], summing, sq[:, c, :], start=True, stop=True)
                last.then_inc(summed, 1)

            @block.vector
            def _(dve):
                order = Order(dve, own)
                dve.wait_ge(summed, 1)
                for c in range(n // 2):
                    last = dve.tensor_scalar(sq[:, 2 * c:2 * c + 2, :], ms[c][:], 1.0 / width, EPS,
                                             ALU.mult, ALU.add)
                order(last)
                dve.reciprocal(sq[:], sq[:]).then_inc(inverse, 1)
                dve.wait_ge(rooted, 1)
                order(dve.scalar_tensor_tensor(y, o[:, 0:n, :], weight, sq[:], ALU.mult, ALU.mult))
                dve.tensor_tensor(y, y, proj[:, gate:gate + n, PAD:PAD + T], ALU.mult)


def delta_stages(nc, k, proj, b):
    H = GD_HEADS
    with ExitStack() as ctx:
        sb = lambda name, shape: ctx.enter_context(sbuf(nc, name, shape, F32))
        ktok, vtok = sb("ktok", [P, TT, H, P]), sb("vtok", [P, TT, H, P])
        crow, brow = sb("crow", [P, TT, H, P]), sb("brow", [P, TT, H, P])
        decay, sct = sb("decay", [P, TT, H, P]), sb("sct", [P, TT, H, P])
        low, lowt = sb("low", [P, TT, H, P]), sb("lowt", [P, TT, H, P])
        pst = [ctx.enter_context(psum(nc, f"pst{i}", [P, H, P], F32)) for i in range(8)]
        with stage(nc, "moved") as (block, moved):
            jobs = [(ktok, "k"), (vtok, "v"), (crow, "cum"), (brow, "beta")]

            @block.tensor
            def _(pe):
                for n, (_dst, what) in enumerate(jobs):
                    for t in range(TT):
                        tok = slice(PAD + t * P, PAD + (t + 1) * P)
                        for hh in range(H):
                            o = pst[2 * n + t][:, hh, :]
                            if what == "k":
                                last = pe.transpose(o, proj[:, GD_K + hh, tok], k.ident)
                            elif what == "v":
                                last = pe.transpose(o, proj[:, GD_V + hh, tok], k.ident)
                            elif what == "cum":
                                last = pe.matmul(o, b.g[:, t, hh:hh + 1].to_broadcast([P, P]), k.tri_incl,
                                                 start=True, stop=True)
                            else:
                                last = pe.matmul(o, b.beta[:, t, hh:hh + 1].to_broadcast([P, P]), k.ident,
                                                 start=True, stop=True)
                        last.then_inc(moved, 1)

            @block.vector
            def _(dve):
                for n in (0, 2):
                    for t in range(TT):
                        dve.wait_ge(moved, 2 * n + t + 1)
                        dve.tensor_copy(jobs[n][0][:, t], pst[2 * n + t][:])

            @block.scalar
            def _(act):
                for n in (1, 3):
                    for t in range(TT):
                        act.wait_ge(moved, 2 * n + t + 1)
                        act.activation(jobs[n][0][:, t], pst[2 * n + t][:], ACT.Copy)

        with stage(nc, "products", "differenced", "exped", "masked", "own", "lowered", "flipped") as (
                block, products, differenced, exped, masked, own, lowered, flipped):
            @block.tensor
            def _(pe):
                for t in range(TT):
                    tok = slice(PAD + t * P, PAD + (t + 1) * P)
                    for hh in range(H):
                        pe.matmul(pst[2 * t][:, hh, :], proj[:, GD_K + hh, tok], proj[:, GD_K + hh, tok],
                                  start=True, stop=True)
                    for hh in range(H):
                        last = pe.matmul(pst[2 * t + 1][:, hh, :], proj[:, GD_K + hh, tok],
                                         proj[:, GD_Q + hh, tok], start=True, stop=True)
                    last.then_inc(products, 1)
                for t in range(TT):
                    pe.wait_ge(lowered, t + 1)
                    for hh in range(H):
                        last = pe.transpose(pst[4 + t][:, hh, :], lowt[:, t, hh, :], k.ident)
                    last.then_inc(flipped, 1)

            @block.vector
            def _(dve):
                order = Order(dve, own)
                for t in range(TT):
                    for hh in range(H):
                        last = dve.tensor_scalar(decay[:, t, hh, :], crow[:, t, hh, :], b.cum[:, t, hh:hh + 1], 0.0,
                                                 ALU.subtract, ALU.min)
                    last.then_inc(differenced, 1)
                for t in range(TT):
                    incl = k.tri_incl.unsqueeze(1).to_broadcast([P, H, P])
                    strict = k.tri_strict.unsqueeze(1).to_broadcast([P, H, P])
                    dve.wait_ge(exped, t + 1)
                    order(dve.tensor_tensor(decay[:, t], decay[:, t], incl, ALU.mult))
                    dve.wait_ge(products, t + 1)
                    dve.tensor_tensor(sct[:, t], pst[2 * t + 1][:], decay[:, t], ALU.mult)
                    order(dve.tensor_tensor(lowt[:, t], pst[2 * t][:], brow[:, t], ALU.mult))
                    order(dve.tensor_tensor(lowt[:, t], lowt[:, t], decay[:, t], ALU.mult))
                    dve.tensor_tensor(lowt[:, t], lowt[:, t], strict, ALU.mult).then_inc(lowered, 1)

            @block.scalar
            def _(act):
                for t in range(TT):
                    act.wait_ge(differenced, t + 1)
                    act.activation(decay[:, t], decay[:, t], ACT.Exp).then_inc(exped, 1)
                for t in range(TT):
                    act.wait_ge(flipped, t + 1)
                    act.activation(low[:, t], pst[4 + t][:], ACT.Copy)

        xi, xit, yy = sb("xi", [P, TT, H, P]), sb("xit", [P, TT, H, P]), sb("yy", [P, TT, H, P])
        bm, bmt = sb("bm", [P, TT, H, P]), sb("bmt", [P, TT, H, P])
        LEVELS = 7
        wide = lambda ap: ap.unsqueeze(1).to_broadcast([P, H, P])
        with stage(nc, "cut", "ydone", "ycopied", "zdone", "updated", "own") as (
                block, cut, ydone, ycopied, zdone, updated, own):
            @block.vector
            def _(dve):
                order = Order(dve, own)
                for t in range(TT):
                    order(dve.tensor_tensor(bm[:, t], low[:, t], wide(k.level(0)), ALU.mult))
                    order(dve.tensor_tensor(bmt[:, t], lowt[:, t], wide(k.level_t(0)), ALU.mult))
                    dve.tensor_tensor(xi[:, t], wide(k.ident), bm[:, t], ALU.subtract).then_inc(updated, 1)
                    dve.tensor_tensor(xit[:, t], wide(k.ident), bmt[:, t], ALU.subtract).then_inc(updated, 1)
                dve.wait_ge(updated, 2 * TT)
                for lev in range(1, LEVELS):
                    for t in range(TT):
                        if lev > 1:
                            dve.wait_ge(ydone, (lev - 2) * TT + t + 1)
                        dve.tensor_tensor(bmt[:, t], lowt[:, t], wide(k.level_t(lev)), ALU.mult).then_inc(cut, 1)
                    for t in range(TT):
                        n = (lev - 1) * TT + t
                        dve.wait_ge(zdone, n + 1)
                        dve.tensor_tensor(xi[:, t], xi[:, t], pst[4 * t + 1][:], ALU.subtract).then_inc(updated, 1)
                        dve.tensor_tensor(xit[:, t], xit[:, t], pst[4 * t + 2][:],
                                          ALU.subtract).then_inc(updated, 1)

            @block.tensor
            def _(pe):
                for lev in range(1, LEVELS):
                    for t in range(TT):
                        n = (lev - 1) * TT + t
                        pe.wait_ge(cut, n + 1)
                        pe.wait_ge(updated, 2 * n + 2)
                        for hh in range(H):
                            last = pe.matmul(pst[4 * t][:, hh, :], bmt[:, t, hh, :], xi[:, t, hh, :],
                                             start=True, stop=True)
                        last.then_inc(ydone, 1)
                    for t in range(TT):
                        n = (lev - 1) * TT + t
                        pe.wait_ge(ycopied, n + 1)
                        for hh in range(H):
                            pe.matmul(pst[4 * t + 1][:, hh, :], xit[:, t, hh, :], yy[:, t, hh, :],
                                      start=True, stop=True)
                        for hh in range(H):
                            last = pe.matmul(pst[4 * t + 2][:, hh, :], yy[:, t, hh, :], xit[:, t, hh, :],
                                             start=True, stop=True)
                        last.then_inc(zdone, 1)

            @block.scalar
            def _(act):
                for lev in range(1, LEVELS):
                    for t in range(TT):
                        n = (lev - 1) * TT + t
                        act.wait_ge(ydone, n + 1)
                        if lev > 1:
                            act.wait_ge(zdone, n - TT + 1)
                        act.activation(yy[:, t], pst[4 * t][:], ACT.Copy).then_inc(ycopied, 1)

        qe, vb, kbe, kl = bm, bmt, yy, low
        erow = crow
        ecol, lcol = sb("ecol", [P, TT, H]), sb("lcol", [P, TT, H])
        with stage(nc, "exped", "last", "own") as (block, exped, lasts, own):
            @block.vector
            def _(dve):
                order = Order(dve, own)
                for t in range(TT):
                    order(dve.tensor_tensor(lcol[:, t], crow[:, t, :, P - 1], b.cum[:, t], ALU.subtract))
                lasts_ready = dve.tensor_copy(b.last[:], crow[:, :, :, P - 1])
                lasts_ready.then_inc(lasts, 1)
                dve.wait_ge(exped, 1)
                order(dve.tensor_tensor(qe[:], erow[:], proj_q(proj), ALU.mult))
                for t in range(TT):
                    order(dve.tensor_tensor(ecol[:, t], ecol[:, t], b.beta[:, t], ALU.mult))
                    for hh in range(H):
                        dve.tensor_scalar(vb[:, t, hh, :], vtok[:, t, hh, :], b.beta[:, t, hh:hh + 1], None, ALU.mult)
                        dve.tensor_scalar(kbe[:, t, hh, :], ktok[:, t, hh, :], ecol[:, t, hh:hh + 1], None, ALU.mult)
                        dve.tensor_scalar(kl[:, t, hh, :], ktok[:, t, hh, :], lcol[:, t, hh:hh + 1], None, ALU.mult)

            @block.scalar
            def _(act):
                act.wait_ge(lasts, 1)
                act.activation(erow[:], crow[:], ACT.Exp)
                act.activation(ecol[:], b.cum[:], ACT.Exp)
                act.activation(lcol[:], lcol[:], ACT.Exp)
                act.activation(b.last[:], b.last[:], ACT.Exp).then_inc(exped, 1)

        wt, vn, state = decay, vtok, ktok[:, 0]
        with stage(nc, "w_done", "w_copied", "v_done", "v_copied", "o_done", "s_done", "s_copied") as (
                block, w_done, w_copied, v_done, v_copied, o_done, s_done, s_copied):
            @block.tensor
            def _(pe):
                for t in range(TT):
                    for hh in range(H):
                        last = pe.matmul(pst[t][:, hh, :], kbe[:, t, hh, :], xit[:, t, hh, :], start=True, stop=True)
                    last.then_inc(w_done, 1)
                for t in range(TT):
                    if t:
                        pe.wait_ge(w_copied, t + 1)
                        pe.wait_ge(s_copied, t)
                    for hh in range(H):
                        last = pe.matmul(pst[2 + t][:, hh, :], xit[:, t, hh, :], vb[:, t, hh, :],
                                         start=True, stop=(t == 0))
                        if t:
                            last = pe.matmul(pst[2 + t][:, hh, :], wt[:, t, hh, :], state[:, hh, :],
                                             start=False, stop=True)
                    last.then_inc(v_done, 1)
                    pe.wait_ge(v_copied, t + 1)
                    if t + 1 < TT:
                        for hh in range(H):
                            last = pe.matmul(pst[6 + t][:, hh, :], kl[:, t, hh, :], vn[:, t, hh, :],
                                             start=True, stop=True)
                        last.then_inc(s_done, 1)
                    for hh in range(H):
                        last = pe.matmul(pst[4 + t][:, hh, :], vn[:, t, hh, :], sct[:, t, hh, :],
                                         start=True, stop=(t == 0))
                        if t:
                            last = pe.matmul(pst[4 + t][:, hh, :], state[:, hh, :], qe[:, t, hh, :],
                                             start=False, stop=True)
                    last.then_inc(o_done, 1)

            @block.scalar
            def _(act):
                for t in range(TT):
                    act.wait_ge(w_done, t + 1)
                    act.activation(wt[:, t], pst[t][:], ACT.Copy, scale=-1.0).then_inc(w_copied, 1)
                for t in range(TT):
                    act.wait_ge(o_done, t + 1)
                    act.activation(b.ogd[:, :, t * P:(t + 1) * P], pst[4 + t][:], ACT.Copy)

            @block.vector
            def _(dve):
                for t in range(TT):
                    dve.wait_ge(v_done, t + 1)
                    dve.tensor_copy(vn[:, t], pst[2 + t][:]).then_inc(v_copied, 1)
                    if t + 1 < TT:
                        dve.wait_ge(s_done, t + 1)
                        dve.tensor_copy(state, pst[6 + t][:]).then_inc(s_copied, 1)


def proj_q(proj):
    return proj[:, GD_Q:GD_Q + GD_HEADS, PAD:PAD + T].rearrange("p h (t c) -> p t h c", t=TT)


def rg_stage(nc, k, proj, cols, b, wrg, y):
    at = lambda name: COL[name][0]
    with ExitStack() as ctx:
        sb = lambda name, shape: ctx.enter_context(sbuf(nc, name, shape, F32))
        gates = sb("gates", [P, 2, 2, T])
        sp_ = sb("softplus", [P, 4, 2])
        la, a, th, bx = sb("la", [P, 2, T]), sb("a", [P, 2, T]), sb("th", [P, 2, T]), sb("bx", [P, 2, T])
        ge = sb("ge", [P, 2, T])
        ps = [ctx.enter_context(psum(nc, f"ps{i}", [P, 2, T], F32)) for i in range(2)]
        with stage(nc, "multiplied", "absed", "logged", "sigmoided", "coefficient", "exped", "ready",
                   "rooted", "own", "gelued", "aown") as (
                block, multiplied, absed, logged, sigmoided, coefficient, exped, ready, rooted, own,
                gelued, aown):
            @block.tensor
            def _(pe):
                for m in range(2):
                    for c in range(2):
                        last = pe.matmul(ps[m][:, c, :], wrg[:, m, c, :], b.xc[:, c, :], start=True, stop=True)
                last.then_inc(multiplied, 1)

            @block.vector
            def _(dve):
                order = Order(dve, own)
                lam = cols[:, at("rg_lambda"):at("rg_lambda") + 2]
                order(dve.tensor_scalar(sp_[:, 0], lam, -1.0, None, ALU.mult))
                dve.tensor_tensor(sp_[:, 1], sp_[:, 0], lam, ALU.min).then_inc(absed, 1)
                dve.wait_ge(logged, 1)
                order(dve.scalar_tensor_tensor(sp_[:, 3], sp_[:, 0], 0.0, sp_[:, 2], ALU.max, ALU.add))
                order(dve.tensor_scalar(sp_[:, 3], sp_[:, 3], -RG_C, None, ALU.mult))
                dve.wait_ge(sigmoided, 1)
                for c in range(2):
                    last = dve.tensor_scalar(la[:, c, :], gates[:, 0, c, :], sp_[:, 3, c:c + 1], None, ALU.mult)
                last.then_inc(coefficient, 1)
                order(dve.tensor_tensor(bx[:], gates[:, 1], b.xc[:], ALU.mult))
                dve.wait_ge(exped, 1)
                order(dve.tensor_tensor(la[:], a[:], a[:], ALU.mult))
                order(dve.tensor_scalar(la[:], la[:], 1.0, None, ALU.add))
                dve.scalar_tensor_tensor(th[:], th[:], -1.0, la[:], ALU.mult, ALU.mult).then_inc(ready, 1)
                dve.wait_ge(rooted, 1)
                order(dve.tensor_tensor(bx[:], bx[:], th[:], ALU.mult))
                for c in range(2):
                    last = dve.tensor_tensor_scan(la[:, c, :], a[:, c, :], bx[:, c, :], 0.0, ALU.mult, ALU.add)
                order(last)
                dve.wait_ge(gelued, 1)
                dve.tensor_tensor(y, la[:], ge[:], ALU.mult)

            @block.scalar
            def _(act):
                order = Order(act, aown)
                act.wait_ge(absed, 1)
                order(act.activation(sp_[:, 2], sp_[:, 1], ACT.Exp))
                act.activation(sp_[:, 2], sp_[:, 2], ACT.Ln, bias=1.0).then_inc(logged, 1)
                act.wait_ge(multiplied, 1)
                for m, name in enumerate(("rg_br", "rg_bi")):
                    for c in range(2):
                        last = act.activation(gates[:, m, c, :], ps[m][:, c, :], ACT.Sigmoid,
                                              bias=cols[:, at(name) + c:at(name) + c + 1])
                last.then_inc(sigmoided, 1)
                act.wait_ge(coefficient, 1)
                act.activation(a[:], la[:], ACT.Exp)
                act.activation(th[:], la[:], ACT.Tanh).then_inc(exped, 1)
                act.activation(ge[:], proj[:, RG_GATE:RG_GATE + 2, PAD:PAD + T], ACT.Gelu_apprx_tanh).then_inc(gelued, 1)
                act.wait_ge(ready, 1)
                act.activation(th[:], th[:], ACT.Sqrt).then_inc(rooted, 1)


def lower_bounds(nc, raw, lb):
    with ExitStack() as ctx:
        t = ctx.enter_context(sbuf(nc, "lbt", [P, 6, 2], F32))
        with stage(nc, "centred", "exped", "own") as (block, centred, exped, own):
            @block.vector
            def _(dve):
                order = Order(dve, own)
                order(dve.tensor_tensor(t[:, 0], raw[:, 0], raw[:, 1], ALU.max))
                order(dve.tensor_tensor(t[:, 1], raw[:, 0], t[:, 0], ALU.subtract))
                dve.tensor_tensor(t[:, 2], raw[:, 1], t[:, 0], ALU.subtract).then_inc(centred, 1)
                dve.wait_ge(exped, 1)
                order(dve.tensor_tensor(t[:, 0], t[:, 3], t[:, 4], ALU.add))
                order(dve.reciprocal(t[:, 0], t[:, 0]))
                order(dve.memset(lb[:, 0, 0:2], 0.0))
                order(dve.memset(lb[:, 0, 2:4], 1.0))
                order(dve.tensor_tensor(lb[:, 1, 0:2], t[:, 4], t[:, 0], ALU.mult))
                dve.tensor_scalar(lb[:, 1, 2:4], lb[:, 1, 0:2], -1.0, 1.0, ALU.mult, ALU.add)

            @block.scalar
            def _(act):
                act.wait_ge(centred, 1)
                act.activation(t[:, 3:5], t[:, 1:3], ACT.Exp).then_inc(exped, 1)


def first_block(nc, k, x, d):
    with ExitStack() as ctx:
        sb = lambda name, shape: ctx.enter_context(sbuf(nc, name, shape, F32))
        h = sb("h", [P, DC, T])
        hs = [ctx.enter_context(sbuf(nc, n, [P, DC, T], F32R)) for n in ("h_high", "h_low")]
        cols, lb, lbl, raw = sb("cols", [P, N_COLS]), sb("lb", [P, DEPTH, 4]), sb("lbl", [P, 4]), sb("raw", [P, DEPTH, 2])
        k.picks = ctx.enter_context(sbuf(nc, "picks", [P, HEAD, P], F32R))
        load_stage(nc, [(raw[:], d.hg_lb)])
        picks_stage(nc, k, k.picks)
        lower_bounds(nc, raw, lb)
        with nc.Fori(0, DEPTH) as layer:
            with stage(nc, "loaded") as (block, loaded):
                @block.sync
                def _(sp):
                    sp.dma_start(cols[:], d.cols[layer]).then_inc(loaded, 16)
                    sp.wait_ge(loaded, 16)

                @block.vector
                def _(dve):
                    dve.tensor_copy(lbl[:], lb[:, layer, :])
            gain = lambda name: cols[:, COL[name][0]:COL[name][0] + DC]
            norm_stage(nc, k, x, gain("norm_ffn1"), h, split=hs)
            ffn_stage(nc, k, hs, x, d.wg0[layer], d.wu0[layer], d.wd0[layer])
            norm_stage(nc, k, x, gain("norm_mix"), h, split=hs)
            mixer(nc, k, h, hs, x, cols, lbl, layer, d)
            norm_stage(nc, k, x, gain("norm_ffn2"), h, split=hs)
            ffn_stage(nc, k, hs, x, d.wg1[layer], d.wu1[layer], d.wd1[layer])


def mixer(nc, k, h, hs, x, cols, lb, layer, d):
    with ExitStack() as ctx:
        sb = lambda name, shape: ctx.enter_context(sbuf(nc, name, shape, F32))
        proj = sb("proj", [P, N_PROJ, TPAD])
        wba, wrg = sb("wba", [P, DC, 8]), sb("wrg", [P, 2, 2, P])
        b = Buffers()
        b.g, b.cum, b.beta, b.last = (sb(n, [P, TT, 4]) for n in ("g", "cumt", "beta", "last"))
        b.xc, b.f, b.k, b.q, b.o = (sb(n, [P, 2, T]) for n in ("xc", "fg", "kg", "qg", "o_hg"))
        levels = sb("levels", [P, 2, 7, P])
        k.level, k.level_t = (lambda m: levels[:, 0, m, :]), (lambda m: levels[:, 1, m, :])
        b.f0, b.ogd = sb("f0", [P, 2, 2, T]), sb("ogd", [P, GD_HEADS, T])
        with stage(nc, "cleared") as (block, _c):
            @block.vector
            def _(dve):
                dve.memset(proj[:, :, 0:PAD], 0.0)
        project_stage(nc, d.w_in[layer], N_PROJ, hs,
                      lambda dve, n, ps, done: dve.tensor_copy(proj[:, n, PAD:PAD + T], ps[:, 0:T]).then_inc(done, 1),
                      [(wba[:], d.wba[layer]), (wrg[:], d.wrg[layer]), (levels[:], d.levels)])
        mixer_gates(nc, k, h, proj, cols, lb, wba, wrg, b)
        y = h
        rg_stage(nc, k, proj, cols, b, wrg, y[:, 6:8, :])
        delta_stages(nc, k, proj, b)
        for pair in range(HG_PAIRS):
            hgrn2_stage(nc, k, proj, b, k.picks, pair)
        head_norm_stage(nc, k, b.o, 2, k.halves, HG_DK, cols[:, COL["hg_norm"][0]:COL["hg_norm"][0] + 1],
                        proj, HG_G, y[:, 0:2, :])
        head_norm_stage(nc, k, b.ogd, 4, k.ones, P, cols[:, COL["gd_norm"][0]:COL["gd_norm"][0] + 1],
                        proj, GD_Z, y[:, 2:6, :])
        split_stage(nc, y, *hs)
        project_stage(nc, d.w_out[layer], DC, hs,
                      lambda dve, n, ps, done: dve.tensor_tensor(x[:, n, :], ps[:, 0:T], x[:, n, :],
                                                                 ALU.add).then_inc(done, 1))


def modulation(nc, k, sc, w_mod, cols, layer, mod, gains):
    b_mod = COL2["b_mod"][0] + 48 * layer
    N, W, S = 48 * P // MOD_W, MOD_W, 4
    G = W // P
    with ExitStack() as ctx:
        wt = ctx.enter_context(sbuf(nc, "wt", [P, S, DC, W], F32))
        row = ctx.enter_context(sbuf(nc, "row", [P, 2, W], F32))
        ps = [ctx.enter_context(psum(nc, f"ps{i}", [P, W], F32)) for i in range(2)]
        pt = [ctx.enter_context(psum(nc, f"pt{i}", [P, G, 2], F32)) for i in range(2)]
        clear_stage(nc, row)
        with stage(nc, "w_in0", "w_in1", "w_in2", "w_in3", "projected", "copied", "flipped", "written") as (
                block, w_in0, w_in1, w_in2, w_in3, projected, copied, flipped, written):
            w_in = (w_in0, w_in1, w_in2, w_in3)

            def load(engine, n, s):
                engine.wait_ge(projected, n + 1)
                engine.dma_start(wt[:, s].rearrange("p c m -> p (c m)"), w_mod[n]).then_inc(w_in[s], 16)

            @block.sync
            def _(sp):
                with sp.Fori(0, N // S) as i:
                    for s in (0, 2):
                        load(sp, S * i + s, s)

            @block.scalar
            def _(act):
                def copy(n, s):
                    act.wait_ge(projected, n + (S + 1))
                    act.wait_ge(flipped, n + 1)
                    act.activation(row[0:2, s % 2, :], ps[s % 2][0:2, :], ACT.Copy).then_inc(copied, 1)

                for s in (1, 3):
                    load(act, s, s)
                with act.Fori(0, N // S - 1) as i:
                    for s in range(S):
                        copy(S * i + s, s)
                        if s % 2:
                            load(act, S * i + (S + s), s)
                for s in range(S):
                    copy(N - S + s, s)

            @block.tensor
            def _(pe):
                def project(n, s, turn):
                    pe.wait_ge(w_in[s], turn)
                    pe.wait_ge(copied, n + 1)
                    for c in range(DC):
                        last = pe.matmul(ps[s % 2][0:2, :], sc[:, c, :], wt[:, s, c, :],
                                         start=(c == 0), stop=(c == DC - 1))
                    last.then_inc(projected, 1)

                def flip(n, s):
                    pe.wait_ge(copied, n + 3)
                    pe.wait_ge(written, n + 1)
                    for j in range(G):
                        last = pe.matmul(pt[s % 2][:, j, :], row[:, s % 2, j * P:(j + 1) * P], k.ident[:, 0:2],
                                         start=True, stop=True)
                    last.then_inc(flipped, 1)

                pe.sem_inc(projected, S)
                pe.sem_inc(flipped, 2)
                project(0, 0, 16)
                with pe.Fori(0, N // S - 1) as i:
                    for s in range(1, S + 1):
                        project(S * i + s, s % S, 16 * i + (16 + 16 * (s // S)))
                        flip(S * i + (s - 1), s - 1)
                for s in range(1, S):
                    project(N - S + s, s, 16 * (N // S))
                    flip(N - S + s - 1, s - 1)
                flip(N - 1, S - 1)

            @block.vector
            def _(dve):
                dve.sem_inc(copied, 2)
                dve.sem_inc(written, 2)
                with dve.Fori(0, N // 2) as i:
                    for s in range(2):
                        n = 2 * G * i + G * s
                        dve.wait_ge(flipped, 2 * i + (s + 3))
                        dve.tensor_tensor(mod[:, :, bass.ds(n, G)], pt[s][:].rearrange("p n t -> p t n"),
                                          cols[:, bass.ds(n + b_mod, G)].unsqueeze(1).to_broadcast([P, 2, G]),
                                          ALU.add).then_inc(written, 1)
    with stage(nc, "own") as (block, own):
        @block.vector
        def _(dve):
            for m, name in enumerate(("norm1", "norm2")):
                a = COL2[name][0] + DC * layer
                g = cols[:, a:a + DC].unsqueeze(1).to_broadcast([P, 2, DC])
                dve.scalar_tensor_tensor(gains[:, m], mod[:, :, (3 * m + 1) * DC:(3 * m + 2) * DC], 1.0, g,
                                         ALU.add, ALU.mult)


class Ahead:

    def __init__(self, nq, tq, h, raw_w, made):
        self.nq, self.tq, self.h, self.raw_w, self.made = nq, tq, h, raw_w, made
        self.n = nq + 2

    def tokens(self, i):
        return self.tq if i < self.nq else 2 * T


def place_stage(nc, k, nq, tq, rope, made, q, kt, v, extra=()):
    tk = 2 * T
    with ExitStack() as ctx:
        part = ctx.enter_context(sbuf(nc, "part", [P, nq + 1, 2, T], F32))
        rot = [ctx.enter_context(psum(nc, f"rot{i}", [P, 512], F32)) for i in range(nq + 1)] if rope else None
        v_ps = ctx.enter_context(psum(nc, "v_ps", [P, 512], F32))
        with stage(nc, "loaded", "flipped", "rotated", "own") as (block, loaded, flipped, rotated, own):
            @block.sync
            def _(sp):
                for dst, src in extra:
                    sp.dma_start(dst, src).then_inc(loaded, 16)
                if extra:
                    sp.wait_ge(loaded, 16 * len(extra))

            @block.tensor
            def _(pe):
                if rope:
                    for i in range(nq + 1):
                        pe.matmul(rot[i][:, 0:T], k.rot, made[:, i, 0:T], start=True, stop=True).then_inc(rotated, 1)
                for t in range(tk // P):
                    last = pe.transpose(v_ps[:, t * P:(t + 1) * P], made[:, nq + 1, t * P:(t + 1) * P], k.ident)
                last.then_inc(flipped, 1)

            @block.scalar
            def _(act):
                first = T if rope else 0
                for i in range(nq if tq > first else 0):
                    for m in range(2):
                        rows = slice(m * HEAD, (m + 1) * HEAD)
                        act.activation(q[rows, 2 * i + m, first:tq], made[rows, i, first:tq], ACT.Copy)
                act.wait_ge(flipped, 1)
                act.activation(v[:], v_ps[:].rearrange("p (t f) -> p t f", f=P), ACT.Copy)

            @block.vector
            def _(dve):
                first = T if rope else 0
                dve.tensor_copy(kt[:, first:tk], made[:, nq, first:tk])
                for i in range(nq + 1 if rope else 0):
                    dve.tensor_tensor(part[:, i, 0, :], made[:, i, 0:T], k.cos, ALU.mult).then_inc(own, 1)
                    dve.wait_ge(rotated, i + 1)
                    dve.tensor_tensor(part[:, i, 1, :], rot[i][:, 0:T], k.sin, ALU.mult).then_inc(own, 1)
                    dve.wait_ge(own, 2 * i + 2)
                    if i == nq:
                        dve.tensor_tensor(kt[:, 0:T], part[:, i, 0, :], part[:, i, 1, :], ALU.add)
                    else:
                        for m in range(2):
                            rows = slice(m * HEAD, (m + 1) * HEAD)
                            dve.tensor_tensor(q[rows, 2 * i + m, 0:T], part[rows, i, 0, :],
                                              part[rows, i, 1, :], ALU.add)


def attend_stage(nc, k, groups, q, kt, v, width, out, ahead, loads, bias=None, sink=None, lam=None):
    nm = len(groups[0][0]) if groups else 1
    n_ahead = ahead.n if ahead else 0
    per = -(-n_ahead * DC // max(len(groups), 1))
    ends = lambda i: 2 + (DC * (i + 1) - 1) // per
    NB = 2 if nm == 1 else 1
    G = len(groups)
    K = 2 * T
    with ExitStack() as ctx:
        sb = lambda name, shape: ctx.enter_context(sbuf(nc, name, shape, F32))
        p = sb("p", [P, 2, nm, K])
        lg = sb("lg", [P, 2, K]) if bias is not None else None
        pts = sb("pts", [P, 2, K])
        if ahead:
            wh, wl = (ctx.enter_context(sbuf(nc, n, [P, n_ahead, D], F32R)) for n in ("wh", "wl"))
            hh, hl = ahead.h
        neg, tot, inv, snk = (sb(n, [P, max(G, 1) * nm]) for n in ("neg", "tot", "inv", "snk"))
        s_ps = [ctx.enter_context(psum(nc, f"s_ps{i}", [P, 512], F32)) for i in range(2 * nm)]
        pt_ps = [ctx.enter_context(psum(nc, f"pt_ps{i}", [P, 512], F32)) for i in range(NB)]
        o_ps = [ctx.enter_context(psum(nc, f"o_ps{i}", [P, 512], F32)) for i in range(NB)]
        pr_ps = [ctx.enter_context(psum(nc, f"pr_ps{i}", [P, 512], F32)) for i in range(2)]
        with stage(nc, "scored", "biased", "maxed", "exped", "weighted", "flipped", "flip_copied",
                   "gathered", "written", "own", "loaded", "rounded", "split", "projected", "taken") as (
                block, scored, biased, maxed, exped, weighted, flipped, flip_copied, gathered, written, own,
                loaded, rounded, split, projected, taken):
            @block.sync
            def _(sp):
                if loads:
                    sp.wait_ge(split, n_ahead)
                    for dst, src in loads:
                        sp.dma_start(dst, src).then_inc(loaded, 16)
                    sp.wait_ge(loaded, 16 * len(loads))

            @block.tensor
            def _(pe):
                def unit(j):
                    i, c = divmod(j, DC)
                    if c == 0:
                        pe.wait_ge(split, i + 1)
                        if i >= 2:
                            pe.wait_ge(taken, i - 1)
                    ps = pr_ps[i % 2]
                    w = slice(c * P, (c + 1) * P)
                    n = ahead.tokens(i)
                    last = product(pe, ps[:, 0:n], (wh[:, i, w], wl[:, i, w]), (hh[:, c, 0:n], hl[:, c, 0:n]),
                                   c == 0, c == DC - 1)
                    if c == DC - 1:
                        last.then_inc(projected, 1)

                for step in range(G + 2):
                    if step < G:
                        g = step
                        heads, qt, k0 = groups[g][:3]
                        if g >= 2:
                            pe.wait_ge(exped, (g - 1) * nm)
                        for m, head in enumerate(heads):
                            last = pe.matmul(s_ps[(g % 2) * nm + m][:, k0:K], q[:, head, qt * P:(qt + 1) * P],
                                             kt[:, k0:K], start=True, stop=True)
                        last.then_inc(scored, 1)
                    if 0 <= step - 1 < G:
                        g = step - 1
                        k0 = groups[g][2]
                        pe.wait_ge(weighted if nm == 2 else exped, g + 1)
                        if g >= NB:
                            pe.wait_ge(flip_copied, g - NB + 1)
                        for t in range(k0 // P, K // P):
                            last = pe.transpose(pt_ps[g % NB][:, t * P:(t + 1) * P],
                                                p[:, g % 2, 0, t * P:(t + 1) * P], k.ident)
                        last.then_inc(flipped, 1)
                    if 0 <= step - 2 < G:
                        g = step - 2
                        k0, v0 = groups[g][2:4]
                        pe.wait_ge(flip_copied, g + 1)
                        if g >= NB:
                            pe.wait_ge(written, g - NB + 1)
                        for t in range(k0 // P, K // P):
                            last = pe.matmul(o_ps[g % NB][:, 0:width], pts[:, g % 2, t * P:(t + 1) * P],
                                             v[:, t, v0:v0 + width], start=(t == k0 // P), stop=(t == K // P - 1))
                        last.then_inc(gathered, 1)
                    for j in range(max(step - 1, 0) * per, min(step * per, n_ahead * DC)):
                        unit(j)

            @block.scalar
            def _(act):
                def high(i):
                    act.activation(wh[:, i], ahead.raw_w[:, i], ACT.Copy).then_inc(rounded, 1)

                def take(i):
                    n = ahead.tokens(i)
                    act.wait_ge(projected, i + 1)
                    act.activation(ahead.made[:, i, 0:n], pr_ps[i % 2][:, 0:n], ACT.Copy,
                                   scale=HEAD ** -0.5 if i < ahead.nq else 1.0).then_inc(taken, 1)

                for step in range(G + 1):
                    if step < n_ahead:
                        high(step)
                    for i in range(n_ahead):
                        if G and ends(i) == step:
                            take(i)
                    if step < G:
                        g = step
                        k0 = groups[g][2]
                        act.wait_ge(maxed, g + 1)
                        if g >= 2:
                            act.wait_ge(flipped, g - 1)
                        for m in range(nm):
                            i = g * nm + m
                            src = s_ps[(g % 2) * nm + m] if bias is None else lg[:, g % 2, :]
                            act.activation(p[:, g % 2, m, k0:K], src[:, k0:K], ACT.Exp, bias=neg[:, i:i + 1],
                                           accum_out=tot[:, i:i + 1]).then_inc(exped, 1)
                        if sink is not None:
                            col = groups[g][5]
                            act.activation(snk[:, g:g + 1], neg[:, g:g + 1], ACT.Exp, bias=sink[0][:, col:col + 1],
                                           ).then_inc(weighted, 1)
                    if step >= 1:
                        g = step - 1
                        k0 = groups[g][2]
                        act.wait_ge(flipped, g + 1)
                        if g >= 2:
                            act.wait_ge(gathered, g - 1)
                        act.activation(pts[:, g % 2, k0:K], pt_ps[g % NB][:, k0:K], ACT.Copy).then_inc(flip_copied, 1)
                for i in range(G + 1, n_ahead):
                    high(i)
                for i in range(n_ahead):
                    if not G or ends(i) > G:
                        take(i)

            @block.vector
            def _(dve):
                order = Order(dve, own)
                for step in range(G + 2):
                    if step < G:
                        g = step
                        _h, qt, k0, _v, bi, si = groups[g][:6]
                        dve.wait_ge(scored, g + 1)
                        if bias is not None:
                            if g >= 2:
                                dve.wait_ge(exped, g - 1)
                            s = s_ps[g % 2]
                            if k0 == 0:
                                dve.tensor_tensor(lg[:, g % 2, 0:T], s[:, 0:T], bias[bi], ALU.add)
                            order(dve.tensor_copy(lg[:, g % 2, T:K], s[:, T:K]))
                            order(dve.tensor_reduce(neg[:, g:g + 1], lg[:, g % 2, k0:K], AX, ALU.max, negate=True))
                            if sink is not None:
                                order(dve.tensor_tensor(neg[:, g:g + 1], neg[:, g:g + 1],
                                                        sink[1][:, si:si + 1], ALU.min))
                        else:
                            for m in range(nm):
                                i = g * nm + m
                                order(dve.tensor_reduce(neg[:, i:i + 1], s_ps[(g % 2) * nm + m][:, k0:K], AX,
                                                        ALU.max, negate=True))
                        dve.sem_inc(maxed, 1)
                    if 0 <= step - 1 < G:
                        g = step - 1
                        k0 = groups[g][2]
                        dve.wait_ge(exped, (g + 1) * nm)
                        one = slice(g * nm, (g + 1) * nm)
                        if sink is not None:
                            dve.wait_ge(weighted, g + 1)
                            order(dve.tensor_tensor(tot[:, one], tot[:, one], snk[:, one], ALU.add))
                        order(dve.reciprocal(inv[:, one], tot[:, one]))
                        if nm == 2:
                            order(dve.tensor_scalar(inv[:, 2 * g + 1:2 * g + 2], inv[:, 2 * g + 1:2 * g + 2], lam,
                                                    None, ALU.mult))
                            order(dve.tensor_scalar(p[:, g % 2, 0, k0:K], p[:, g % 2, 0, k0:K],
                                                    inv[:, 2 * g:2 * g + 1], None, ALU.mult))
                            dve.scalar_tensor_tensor(p[:, g % 2, 0, k0:K], p[:, g % 2, 1, k0:K],
                                                     inv[:, 2 * g + 1:2 * g + 2], p[:, g % 2, 0, k0:K],
                                                     ALU.mult, ALU.add).then_inc(weighted, 1)
                    if step < n_ahead:
                        dve.wait_ge(rounded, step + 1)
                        dve.tensor_tensor(wl[:, step], ahead.raw_w[:, step], wh[:, step].bitcast(F32),
                                          ALU.subtract).then_inc(split, 1)
                    if 0 <= step - 2 < G:
                        g = step - 2
                        dve.wait_ge(gathered, g + 1)
                        if nm == 2:
                            dve.tensor_copy(out(groups[g][6]), o_ps[g % NB][:, 0:width]).then_inc(written, 1)
                        else:
                            dve.tensor_scalar(out(groups[g][6]), o_ps[g % NB][:, 0:width], inv[:, g:g + 1], None,
                                              ALU.mult).then_inc(written, 1)
                for i in range(G + 2, n_ahead):
                    dve.wait_ge(rounded, i + 1)
                    dve.tensor_tensor(wl[:, i], ahead.raw_w[:, i], wh[:, i].bitcast(F32),
                                      ALU.subtract).then_inc(split, 1)


def to_features_stage(nc, k, o, y, tiles):
    with ExitStack() as ctx:
        ps = [ctx.enter_context(psum(nc, f"ps{i}", [P, 4, P], F32)) for i in range(4)]
        n = tiles * DC // 4
        with stage(nc, "flipped", "copied") as (block, flipped, copied):
            @block.tensor
            def _(pe):
                for i in range(n):
                    if i >= 4:
                        pe.wait_ge(copied, i - 3)
                    for j in range(4):
                        t, c = divmod(4 * i + j, DC)
                        last = pe.transpose(ps[i % 4][:, j, :], o[:, t, c * P:(c + 1) * P], k.ident)
                    last.then_inc(flipped, 1)

            @block.vector
            def _(dve):
                for i in range(n):
                    t, c = divmod(4 * i, DC)
                    dve.wait_ge(flipped, i + 1)
                    dve.tensor_copy(y[:, c:c + 4, t * P:(t + 1) * P], ps[i % 4][:]).then_inc(copied, 1)


def diff_norm_stage(nc, o, tiles, weight, first):
    n = tiles * DIFF_HEADS
    with ExitStack() as ctx:
        sq = ctx.enter_context(sbuf(nc, "sq", [P, n, P], F32))
        ms = ctx.enter_context(sbuf(nc, "ms", [P, n], F32))
        with stage(nc, "own", "inverse", "rooted") as (block, own, inverse, rooted):
            part = lambda t: o[:, t, first:first + DIFF_HEADS * P].rearrange("p (h f) -> p h f", f=P)

            @block.vector
            def _(dve):
                order = Order(dve, own)
                for t in range(tiles):
                    last = dve.tensor_tensor(sq[:, t * 4:t * 4 + 4, :], part(t), part(t), ALU.mult)
                order(last)
                order(dve.tensor_reduce(ms[:], sq[:], AX, ALU.add))
                order(dve.tensor_scalar(ms[:], ms[:], 1.0 / P, EPS, ALU.mult, ALU.add))
                dve.reciprocal(ms[:], ms[:]).then_inc(inverse, 1)
                dve.wait_ge(rooted, 1)
                for t in range(tiles):
                    for hh in range(DIFF_HEADS):
                        i = t * 4 + hh
                        dve.tensor_scalar(part(t)[:, hh, :], part(t)[:, hh, :], ms[:, i:i + 1], 1.0 - LAM_INIT,
                                          ALU.mult, ALU.mult)

            @block.scalar
            def _(act):
                act.wait_ge(inverse, 1)
                act.activation(ms[:], ms[:], ACT.Sqrt).then_inc(rooted, 1)


def lambda_stage(nc, raw, lam):
    with ExitStack() as ctx:
        t = ctx.enter_context(sbuf(nc, "lam_t", [P, 2, HEAD], F32))
        s = ctx.enter_context(sbuf(nc, "lam_s", [P, 2], F32))
        with stage(nc, "own", "summed", "exped") as (block, own, summed, exped):
            @block.vector
            def _(dve):
                order = Order(dve, own)
                pairs = raw.rearrange("p (a b f) -> p a b f", a=2, b=2)
                order(dve.tensor_tensor(t[:], pairs[:, :, 0, :], pairs[:, :, 1, :], ALU.mult))
                dve.tensor_reduce(s[:], t[:], AX, ALU.add).then_inc(summed, 1)
                dve.wait_ge(exped, 1)
                order(dve.tensor_tensor(lam[:], s[:, 1:2], s[:, 0:1], ALU.subtract))
                dve.tensor_scalar(lam[:], lam[:], LAM_INIT, None, ALU.subtract)

            @block.scalar
            def _(act):
                act.wait_ge(summed, 1)
                act.activation(s[:], s[:], ACT.Exp).then_inc(exped, 1)


def clear_stage(nc, tile):
    with stage(nc, "cleared") as (block, _c):
        @block.vector
        def _(dve):
            dve.memset(tile[:], 0.0)


def even_mixer(nc, k, h, hs, x, ctx_x, cols, mod, d):
    with ExitStack() as ctx:
        sb = lambda name, shape: ctx.enter_context(sbuf(nc, name, shape, F32))
        o = sb("o", [P, 4, D])
        q, kt, v = sb("q", [P, 2, 2 * T]), sb("kt", [P, 2 * T]), sb("v", [P, 4, P])
        bias, lam = sb("bias", [P, 2, TT, T]), sb("lam", [P, 1])
        a = COL2["lambda"][0]
        lambda_stage(nc, cols[:, a:a + 4 * HEAD], lam)
        clear_stage(nc, q)
        w = d.w_even
        raw_w = sb("raw_w", [P, 3, D])
        turn = lambda a, c: [(raw_w[:, i], w[c + (a + 4 * i)]) for i in range(3)]
        made = sb("made", [P, 3, 2 * T])
        ahead = Ahead(1, 2 * T, hs, raw_w, made)

        def turns(a, rope, extra, attend):
            load_stage(nc, turn(a, 0))
            attend_stage(nc, k, [], q, kt, v, HEAD, None, ahead, turn(a, 1))

            def step(c, more):
                place_stage(nc, k, 1, 2 * T, rope, made, q, kt, v, extra(c))
                attend(c, ahead if more else None, turn(a + 2, c) if more else ())

            with nc.Fori(0, 3) as c:
                step(c, True)
            step(3, False)

        groups = [((m,), t, 0 if t < TT else T, m * HEAD, (m, t), None, (t, m * HEAD))
                  for t in range(4) for m in range(2)]
        turns(0, False, lambda c: [(bias[:], d.bias[c])],
              lambda c, ahead, loads: attend_stage(
                  nc, k, groups, q, kt, v, HEAD, lambda at: o[:, at[0], bass.ds(c * P + at[1], HEAD)], ahead, loads,
                  bias={(m, t): bias[:, m, t, :] for m in range(2) for t in range(TT)} | {
                      (m, t): None for m in range(2) for t in (2, 3)}))
        pairs = [((0, 1), t, 0 if t < TT else T, 0, None, None, t) for t in range(4)]
        turns(12, True, lambda c: (),
              lambda c, ahead, loads: attend_stage(
                  nc, k, pairs, q, kt, v, P, lambda t: o[:, t, bass.ds(c * P + 4 * P, P)], ahead, loads, lam=lam[:]))
        diff_norm_stage(nc, o, 4, None, 4 * P)
        to_features_stage(nc, k, o, h, 4)
        a = COL2["subln"][0]
        with stage(nc, "own") as (block, own):
            @block.vector
            def _(dve):
                dve.tensor_scalar(h[:, 4:8, :], h[:, 4:8, :], cols[:, a:a + 1], None, ALU.mult)

        def residual(dve, n, ps, done):
            dve.scalar_tensor_tensor(x[:, n, :], ps[:, 0:T], mod[:, 0, bass.ds(n + 2 * DC, 1)], x[:, n, :],
                                     ALU.mult, ALU.add)
            dve.scalar_tensor_tensor(ctx_x[:, n, :], ps[:, T:2 * T], mod[:, 1, bass.ds(n + 2 * DC, 1)],
                                     ctx_x[:, n, :], ALU.mult, ALU.add).then_inc(done, 1)

        split_stage(nc, h, *hs)
        project_stage(nc, d.w_out_even, DC, hs, residual)


def odd_mixer(nc, k, h, hs, x, cols, mod, d):
    with ExitStack() as ctx:
        sb = lambda name, shape: ctx.enter_context(sbuf(nc, name, shape, F32))
        o = sb("o", [P, TT, D])
        q, kt, v = sb("q", [P, 4, T]), sb("kt", [P, 2 * T]), sb("v", [P, 4, P])
        snk, nsnk = sb("snk4", [P, 4]), sb("nsnk4", [P, 4])
        clear_stage(nc, q)
        w = d.w_odd
        a = COL2["sink"][0]
        band = k.band.rearrange("p (t k) -> p t k", t=TT)
        raw_w = sb("raw_w", [P, 4, D])
        turn = lambda n: [(raw_w[:, i], w[4 * n + i]) for i in range(4)]
        made = sb("made", [P, 4, 2 * T])
        ahead = Ahead(2, T, hs, raw_w, made)
        load_stage(nc, turn(0))
        attend_stage(nc, k, [], q, kt, v, HEAD, None, ahead, turn(1))

        def step(n, more):
            place_stage(nc, k, 2, T, True, made, q, kt, v)
            with stage(nc, "own") as (block, own):
                @block.vector
                def _(dve):
                    dve.tensor_copy(snk[:], cols[:, bass.ds(4 * n + a, 4)])
                    dve.tensor_scalar(nsnk[:], cols[:, bass.ds(4 * n + a, 4)], -1.0, None, ALU.mult)
            groups = [((g,), t, 0, 0, t, g, (t, g * HEAD)) for t in range(TT) for g in range(4)]
            attend_stage(nc, k, groups, q, kt, v, HEAD,
                         lambda at: o[:, at[0], bass.ds(n * (4 * HEAD) + at[1], HEAD)],
                         ahead if more else None, turn(n + 2) if more else (),
                         bias=[band[:, t, :] for t in range(TT)], sink=(snk, nsnk))

        with nc.Fori(0, SWA_KV_HEADS - 1) as n:
            step(n, True)
        step(SWA_KV_HEADS - 1, False)
        to_features_stage(nc, k, o, h, TT)
        ys = [a[:, :, 0:T] for a in hs]
        split_stage(nc, h[:, :, 0:T], *ys)
        project_stage(nc, d.w_out_odd, DC, ys,
                      lambda dve, n, ps, done: dve.scalar_tensor_tensor(
                          x[:, n, :], ps[:, 0:T], mod[:, 0, bass.ds(n + 2 * DC, 1)], x[:, n, :],
                          ALU.mult, ALU.add).then_inc(done, 1))


def peer_route(nc, k, h, keys_dram, wq, route):
    R = PEER_TOPK
    rows = ((0, 1, 16, 0), (1, 3, 8, 16), (3, R, 4, 32))
    PAIRS = 32 + (R - 3) * 4
    with ExitStack() as ctx:
        sb = lambda name, shape, dt=F32: ctx.enter_context(sbuf(nc, name, shape, dt))
        qp, keys = sb("qp", [P, 16, T]), sb("keys", [P, 16, P])
        project_stage(nc, wq, 16, h,
                      lambda dve, n, ps, done: dve.tensor_copy(qp[:, n, :], ps[:, 0:T]).then_inc(done, 1),
                      [(keys[:], keys_dram)])
        s, s2 = sb("s", [P, TT, 16, P]), sb("s2", [P, 16, P])
        sv, si, sif = sb("sv", [P, TT, 16, R]), sb("si", [P, TT, 16, R], U32), sb("sif", [P, TT, 16, R])
        cand, cand2 = sb("cand", [P, TT, 8, PAIRS]), sb("cand2", [P, 8, PAIRS])
        fv, fi = sb("fv", [P, TT, 8, R]), sb("fi", [P, 8, R], U32)
        bits, bf = sb("bits", [P, 5, 8 * R], U32), sb("bf", [P, 5, 8 * R])
        past, step, skip, hif = (sb(n, [P, 2, 8 * R]) for n in ("past", "step", "skip", "hif"))
        eq, sm = sb("eq", [P, TT, 2, 8 * R, R]), sb("sm", [P, 8])
        res = sb("res", [P, TT, 3, SLOTS])
        ps = [ctx.enter_context(psum(nc, f"ps{i}", [P, 4, P], F32)) for i in range(4)]
        pt = [ctx.enter_context(psum(nc, f"pt{i}", [P, P], F32)) for i in range(3)]
        with stage(nc, "scored", "copied", "picked", "paired", "centred", "exped", "matched", "valued",
                   "decoded", "flipped", "placed", "own") as (
                block, scored, copied, picked, paired, centred, exped, matched, valued, decoded, flipped,
                placed, own):
            @block.tensor
            def _(pe):
                for t in range(TT):
                    for i in range(16):
                        if t and i % 4 == 0:
                            pe.wait_ge(copied, 4 * (t - 1) + i // 4 + 1)
                        last = pe.matmul(ps[i // 4][:, i % 4, :], qp[:, i, t * P:(t + 1) * P], keys[:, i, :],
                                         start=True, stop=True)
                        if i % 4 == 3:
                            last.then_inc(scored, 1)
                for t in range(TT):
                    pe.wait_ge(decoded, t + 1)
                    for i in range(3):
                        if t:
                            pe.wait_ge(placed, 3 * (t - 1) + i + 1)
                        pe.transpose(pt[i][:], res[:, t, i, :], k.ident).then_inc(flipped, 1)

            @block.scalar
            def _(act):
                for t in range(TT):
                    for i in range(4):
                        act.wait_ge(scored, 4 * t + i + 1)
                        act.activation(s[:, t, 4 * i:4 * i + 4, :], ps[i][:], ACT.Copy).then_inc(copied, 1)
                for t in range(TT):
                    act.wait_ge(centred, t + 1)
                    act.activation(fv[:, t], fv[:, t], ACT.Exp).then_inc(exped, 1)
                for t in range(TT):
                    for i in range(3):
                        act.wait_ge(flipped, 3 * t + i + 1)
                        act.activation(route[:, i, t * P:(t + 1) * P], pt[i][:], ACT.Copy).then_inc(placed, 1)

            @block.gpsimd
            def _(pool):
                for t in range(TT):
                    pool.wait_ge(picked, t + 1)
                    pair = sv[:, t].rearrange("p (h two) r -> p h two r", two=2)
                    for hh in range(8):
                        for a0, a1, nb, at in rows:
                            na = a1 - a0
                            last = pool.tensor_tensor(
                                cand[:, t, hh, at:at + na * nb].rearrange("p (a b) -> p a b", b=nb),
                                pair[:, hh, 0, a0:a1].unsqueeze(2).to_broadcast([P, na, nb]),
                                pair[:, hh, 1, 0:nb].unsqueeze(1).to_broadcast([P, na, nb]), ALU.add)
                    last.then_inc(paired, 1)
                for t in range(TT):
                    sip = sif[:, t].rearrange("p (h two) r -> p h two r", two=2)
                    for half in range(2):
                        pool.wait_ge(matched, 2 * t + half + 1)
                        for hh in range(8):
                            e = eq[:, t, half, hh * R:(hh + 1) * R, :]
                            row = sip[:, hh, half, :].unsqueeze(1).to_broadcast([P, R, R])
                            last = pool.tensor_tensor(e, e, row, ALU.mult)
                        last.then_inc(valued, 1)

            @block.vector
            def _(dve):
                order = Order(dve, own)

                def top(values, rest, best, index, n):
                    for lo in (0, 8):
                        src = values if lo == 0 else rest
                        for i in range(n):
                            last = dve.max(best[:, i, lo:lo + 8], src[:, i, :])
                        order(last)
                        for i in range(n):
                            last = dve.max_index(index[:, i, lo:lo + 8], best[:, i, lo:lo + 8], src[:, i, :])
                            if lo == 0:
                                last = dve.match_replace(rest[:, i, :], best[:, i, 0:8], values[:, i, :], -3e38)
                        order(last)

                for t in range(TT):
                    dve.wait_ge(copied, 4 * t + 4)
                    top(s[:, t], s2, sv[:, t], si[:, t], 16)
                    order(dve.tensor_copy(sif[:, t], si[:, t]))
                    dve.sem_inc(picked, 1)
                io = k.iota[:, 0:R].unsqueeze(1).to_broadcast([P, 8 * R, R])
                for t in range(TT):
                    dve.wait_ge(paired, t + 1)
                    top(cand[:, t], cand2, fv[:, t], fi, 8)
                    fif = fi[:].rearrange("p h r -> p (h r)")
                    dve.tensor_scalar(bits[:, 0, :], fif, 3, None, ALU.logical_shift_right)
                    dve.tensor_scalar(bits[:, 1, :], fif, 2, None, ALU.logical_shift_right)
                    for i, mask in ((2, 15), (3, 7), (4, 3)):
                        last = dve.tensor_scalar(bits[:, i, :], fif, mask, None, ALU.bitwise_and)
                    order(last)
                    order(dve.tensor_copy(bf[:], bits[:]))
                    dve.tensor_scalar(past[:, 0, :], bf[:, 0, :], 2.0, None, ALU.is_ge)
                    dve.tensor_scalar(past[:, 1, :], bf[:, 0, :], 4.0, None, ALU.is_ge)
                    dve.tensor_scalar(step[:, 0, :], bf[:, 0, :], 1.0, None, ALU.subtract)
                    dve.tensor_tensor(step[:, 1, :], bf[:, 3, :], bf[:, 2, :], ALU.subtract)
                    dve.scalar_tensor_tensor(skip[:, 0, :], bf[:, 1, :], 4.0, bf[:, 0, :], ALU.subtract, ALU.subtract)
                    order(dve.tensor_tensor(skip[:, 1, :], bf[:, 4, :], bf[:, 3, :], ALU.subtract))
                    over = lambda i: past[:, i, :].unsqueeze(1).to_broadcast([P, 2, 8 * R])
                    dve.tensor_tensor(step[:], step[:], over(0), ALU.mult)
                    order(dve.tensor_tensor(skip[:], skip[:], over(1), ALU.mult))
                    order(dve.tensor_tensor(hif[:], step[:], skip[:], ALU.add))
                    order(dve.tensor_tensor(hif[:, 1, :], hif[:, 1, :], bf[:, 2, :], ALU.add))
                    for half in range(2):
                        dve.tensor_tensor(eq[:, t, half], hif[:, half, :].unsqueeze(2).to_broadcast([P, 8 * R, R]),
                                          io, ALU.is_equal).then_inc(matched, 1)
                    dve.tensor_tensor(fv[:, t], fv[:, t], res_max(dve, order, sm, fv[:, t]),
                                      ALU.subtract).then_inc(centred, 1)
                    dve.wait_ge(matched, 2 * t + 2)
                for t in range(TT):
                    for half in range(2):
                        dve.wait_ge(valued, 2 * t + half + 1)
                        order(dve.tensor_reduce(res[:, t, half, :], eq[:, t, half], AX, ALU.add))
                    dve.wait_ge(exped, t + 1)
                    order(dve.tensor_reduce(sm[:], fv[:, t], AX, ALU.add))
                    order(dve.reciprocal(sm[:], sm[:]))
                    order(dve.tensor_tensor(res[:, t, 2, :].rearrange("p (h r) -> p h r", r=R), fv[:, t],
                                            sm[:].unsqueeze(2).to_broadcast([P, 8, R]), ALU.mult))
                    dve.sem_inc(decoded, 1)


def res_max(dve, order, sm, fv):
    order(dve.tensor_copy(sm[:], fv[:, :, 0]))
    return sm[:].unsqueeze(2).to_broadcast([P, 8, PEER_TOPK])


def peer_gates(nc, k, route, gates):
    B, S = 8, 4
    with ExitStack() as ctx:
        sb = lambda name, shape: ctx.enter_context(sbuf(nc, name, shape, F32))
        one, two = sb("one", [P, S, B, P]), sb("two", [P, S, B, P])
        ps = [ctx.enter_context(psum(nc, f"ps{i}", [P, B, P], F32)) for i in range(S)]
        with stage(nc, "named", "spelled", "gated", "multiplied", "kept") as (
                block, named, spelled, gated, multiplied, kept):
            def over_keys(part, t):
                return route[:, part, bass.ds(t, B)].unsqueeze(2).to_broadcast([P, B, P])

            @block.vector
            def _(dve):
                io = k.iota.unsqueeze(1).to_broadcast([P, B, P])
                with dve.Fori(0, T // (S * B)) as i:
                    for s in range(S):
                        t = S * B * i + s * B
                        dve.wait_ge(multiplied, S * i + (s + 1))
                        dve.tensor_tensor(one[:, s], io, over_keys(0, t), ALU.is_equal).then_inc(named, 1)
                        dve.tensor_tensor(two[:, s], io, over_keys(1, t), ALU.is_equal).then_inc(spelled, 1)

            @block.gpsimd
            def _(pool):
                with pool.Fori(0, T // (S * B)) as i:
                    for s in range(S):
                        pool.wait_ge(named, S * i + (s + 1))
                        pool.tensor_tensor(one[:, s], one[:, s], over_keys(2, S * B * i + s * B),
                                           ALU.mult).then_inc(gated, 1)

            @block.tensor
            def _(pe):
                pe.sem_inc(multiplied, S)
                with pe.Fori(0, T // (S * B)) as i:
                    for s in range(S):
                        pe.wait_ge(spelled, S * i + (s + 1))
                        pe.wait_ge(gated, S * i + (s + 1))
                        pe.wait_ge(kept, S * i + (s + 1))
                        for j in range(B):
                            last = pe.matmul(ps[s][:, j, :], two[:, s, j, :], one[:, s, j, :], start=True, stop=True)
                        last.then_inc(multiplied, 1)

            @block.scalar
            def _(act):
                act.sem_inc(kept, S)
                with act.Fori(0, T // (S * B)) as i:
                    for s in range(S):
                        act.wait_ge(multiplied, S * i + (s + S + 1))
                        act.activation(gates[:, :, bass.ds(S * B * i + s * B, B)],
                                       ps[s][:].rearrange("p t e -> p e t"), ACT.Copy).then_inc(kept, 1)


def peer_experts(nc, k, h, u, v, gates, room, x, gain):
    C = PEER_NKEYS
    (hh, hl) = h
    with ExitStack() as ctx:
        sb = lambda name, shape, dt=F32: ctx.enter_context(sbuf(nc, name, shape, dt))
        ur, vr = sb("ur", [P, 2, D]), sb("vr", [P, 2, D])
        uh, ul, vh, vl = (sb(n, [P, 2, D], F32R) for n in ("uh", "ul", "vh", "vl"))
        ga, full = room[:, 0:2, :], room[:, 2, :]
        gh, gl = sb("gh", [P, 2, T], F32R), sb("gl", [P, 2, T], F32R)
        f = gates[:, 0:TT * D // T, :].rearrange("p a b -> p (a b)").rearrange("p (t n) -> p t n", t=TT)
        a_ps = [ctx.enter_context(psum(nc, f"a_ps{i}", [P, 512], F32)) for i in range(2)]
        out = [[ctx.enter_context(psum(nc, f"out{t}{i}", [P, 512], F32)) for i in range(2)] for t in range(TT)]
        with stage(nc, "u_in0", "u_in1", "v_in0", "v_in1", "u_rounded", "u_split", "v_rounded", "v_split",
                   "scored", "gelued", "weighted", "gated", "used") as (
                block, u_in0, u_in1, v_in0, v_in1, u_rounded, u_split, v_rounded, v_split, scored,
                gelued, weighted, gated, used):
            u_in, v_in = (u_in0, u_in1), (v_in0, v_in1)

            @block.sync
            def _(sp):
                for s in range(2):
                    sp.dma_start(ur[:, s, :], u[s]).then_inc(u_in[s], 16)
                    sp.dma_start(vr[:, s, :], v[s]).then_inc(v_in[s], 16)
                with sp.Fori(1, C // 2) as i:
                    for s in range(2):
                        sp.wait_ge(u_split, 2 * i + (s - 1))
                        sp.dma_start(ur[:, s, :], u[2 * i + s]).then_inc(u_in[s], 16)
                        sp.wait_ge(v_split, 2 * i + (s - 1))
                        sp.dma_start(vr[:, s, :], v[2 * i + s]).then_inc(v_in[s], 16)

            @block.tensor
            def _(pe):
                def score(n, s):
                    pe.wait_ge(u_split, n + 1)
                    for c in range(DC):
                        w = slice(c * P, (c + 1) * P)
                        last = product(pe, a_ps[s][:, 0:T], (uh[:, s, w], ul[:, s, w]), (hh[:, c, :], hl[:, c, :]),
                                       c == 0, c == DC - 1)
                    last.then_inc(scored, 1)

                def gather(n, s, first=False, last_one=False):
                    pe.wait_ge(v_split, n + 1)
                    pe.wait_ge(gated, n + 3)
                    for t in range(TT):
                        tok = slice(t * P, (t + 1) * P)
                        for i in range(2):
                            part = slice(i * 512, (i + 1) * 512)
                            last = product(pe, out[t][i][:], (gh[:, s, tok], gl[:, s, tok]),
                                           (vh[:, s, part], vl[:, s, part]), first, last_one)
                    last.then_inc(used, 1)

                pe.sem_inc(used, 2)
                score(0, 0)
                score(1, 1)
                gather(0, 0, first=True)
                with pe.Fori(1, C // 2) as i:
                    pe.wait_ge(gelued, 2 * i - 1)
                    score(2 * i, 0)
                    gather(2 * i - 1, 1)
                    pe.wait_ge(gelued, 2 * i)
                    score(2 * i + 1, 1)
                    gather(2 * i, 0)
                gather(C - 1, 1, last_one=True)

            @block.scalar
            def _(act):
                def gelu(n, s):
                    act.wait_ge(scored, n + 1)
                    act.wait_ge(gated, n + 1)
                    act.activation(ga[:, s, :], a_ps[s][:, 0:T], ACT.Gelu).then_inc(gelued, 1)

                def u_high(s, turn):
                    act.wait_ge(u_in[s], turn)
                    act.activation(uh[:, s], ur[:, s], ACT.Copy).then_inc(u_rounded, 1)

                def v_high(n, s, turn):
                    act.wait_ge(v_in[s], turn)
                    act.wait_ge(used, n + 1)
                    act.activation(vh[:, s], vr[:, s], ACT.Copy).then_inc(v_rounded, 1)

                u_high(0, 16)
                u_high(1, 16)
                v_high(0, 0, 16)
                with act.Fori(0, C // 2 - 1) as i:
                    for s in range(2):
                        gelu(2 * i + s, s)
                        u_high(s, 16 * i + 32)
                        v_high(2 * i + (s + 1), 1 - s, 16 * i + (16 + 16 * s))
                gelu(C - 2, 0)
                v_high(C - 1, 1, 8 * C)
                gelu(C - 1, 1)

            @block.vector
            def _(dve):
                def gate(n, s):
                    dve.wait_ge(gelued, n + 1)
                    dve.wait_ge(used, n + 1)
                    g = gates[:, n, :]
                    dve.tensor_tensor(gh[:, s, :], ga[:, s, :], g, ALU.mult).then_inc(weighted, 1)
                    dve.tensor_tensor(full, ga[:, s, :], g, ALU.mult).then_inc(weighted, 1)
                    dve.wait_ge(weighted, 2 * n + 2)
                    dve.tensor_tensor(gl[:, s, :], full, gh[:, s, :].bitcast(F32), ALU.subtract).then_inc(gated, 1)

                def u_low(n, s):
                    dve.wait_ge(u_rounded, n + 1)
                    dve.tensor_tensor(ul[:, s], ur[:, s], uh[:, s].bitcast(F32), ALU.subtract).then_inc(u_split, 1)

                def v_low(n, s):
                    dve.wait_ge(v_rounded, n + 1)
                    dve.tensor_tensor(vl[:, s], vr[:, s], vh[:, s].bitcast(F32), ALU.subtract).then_inc(v_split, 1)

                dve.sem_inc(gated, 2)
                u_low(0, 0)
                u_low(1, 1)
                v_low(0, 0)
                with dve.Fori(0, C // 2 - 1) as i:
                    for s in range(2):
                        gate(2 * i + s, s)
                        dve.wait_ge(gated, 2 * i + (s + 3))
                        u_low(2 * i + (s + 2), s)
                        v_low(2 * i + (s + 1), 1 - s)
                gate(C - 2, 0)
                dve.wait_ge(gated, C + 1)
                v_low(C - 1, 1)
                gate(C - 1, 1)
                dve.wait_ge(used, C + 2)
                for t in range(TT):
                    for i in range(2):
                        dve.tensor_copy(f[:, t, i * 512:(i + 1) * 512], out[t][i][:])
        with stage(nc, "flipped", "added") as (block, flipped, added):
            @block.tensor
            def _(pe):
                for n in range(2 * TT):
                    t, half = divmod(n, 2)
                    for j in range(4):
                        c = 4 * half + j
                        last = pe.transpose(out[t][half][:, j * P:(j + 1) * P], f[:, t, c * P:(c + 1) * P], k.ident)
                    last.then_inc(flipped, 1)

            @block.vector
            def _(dve):
                for n in range(2 * TT):
                    t, half = divmod(n, 2)
                    dve.wait_ge(flipped, n + 1)
                    for j in range(4):
                        c = 4 * half + j
                        xs = x[:, c, t * P:(t + 1) * P]
                        dve.scalar_tensor_tensor(xs, out[t][half][:, j * P:(j + 1) * P], gain[:, c:c + 1], xs,
                                                 ALU.mult, ALU.add)


def peer(nc, k, h, x, gain, layer, d):
    with ExitStack() as ctx:
        route = ctx.enter_context(sbuf(nc, "route", [P, 3, T], F32))
        peer_route(nc, k, h, d.keys[layer], d.wq[layer], route)
        gates = ctx.enter_context(sbuf(nc, "gates", [P, PEER_NKEYS, T], F32))
        peer_gates(nc, k, route, gates)
        peer_experts(nc, k, h, d.u[layer], d.v[layer], gates, route, x, gain)


def second_block(nc, k, x, d):
    with ExitStack() as ctx:
        sb = lambda name, shape, dt=F32: ctx.enter_context(sbuf(nc, name, shape, dt))
        cols, sc = sb("cols2", [P, N_COLS2]), sb("sc", [P, DC, 2])
        mod, gains = sb("mod", [P, 2, 48]), sb("gains", [P, 2, 2, DC])
        ctx_x = sb("ctx_fm", [P, DC, T])
        load_stage(nc, [(cols[:], d.cols2), (ctx_x[:], d.ctx)])
        a = COL2["c"][0]
        with stage(nc, "own") as (block, own):
            @block.scalar
            def _(act):
                act.activation(sc[:].rearrange("p c t -> p (c t)"), cols[:, a:a + 2 * DC], ACT.Silu)
        for layer in range(DEPTH):
            modulation(nc, k, sc, d.w_mod[layer], cols, layer, mod, gains)
            with ExitStack() as part:
                h = part.enter_context(sbuf(nc, "h2", [P, DC, 2 * T], F32))
                hs = [part.enter_context(sbuf(nc, n, [P, DC, 2 * T], F32R)) for n in ("h2_high", "h2_low")]
                cst2 = part.enter_context(sbuf(nc, "cst2_sb", [P, N_CST2], F32))
                k.attention(cst2)
                for kind, res in enumerate((x, ctx_x)):
                    tok = slice(kind * T, (kind + 1) * T)
                    norm_stage(nc, k, res, gains[:, 0, kind], h[:, :, tok], mod[:, kind, 0:DC],
                               [a[:, :, tok] for a in hs], () if kind else [(cst2[:], d.cst2)])
                if layer == 0:
                    even_mixer(nc, k, h, hs, x, ctx_x, cols, mod, d)
                else:
                    odd_mixer(nc, k, h, hs, x, cols, mod, d)
            for kind, res in enumerate((x, ctx_x) if layer == 0 else (x,)):
                with ExitStack() as part:
                    hs = [part.enter_context(sbuf(nc, n, [P, DC, T], F32R)) for n in ("h3_high", "h3_low")]
                    with ExitStack() as own:
                        h = own.enter_context(sbuf(nc, "h3", [P, DC, T], F32))
                        norm_stage(nc, k, res, gains[:, 1, kind], h, mod[:, kind, 3 * DC:4 * DC], hs)
                    peer(nc, k, hs, res, mod[:, kind, 5 * DC:6 * DC], layer, d)


class Data:
    pass


def fm(w):
    *lead, k, n = w.shape
    w = w.reshape(*lead, k // P, P, n // P, P)
    r = len(lead)
    w = w.transpose(*range(r), r + 2, r + 1, r, r + 3)
    return np.ascontiguousarray(w).reshape(*lead, n // P, P, k)


def by_part(v):
    v = v.reshape(*v.shape[:-1], -1, P)
    return np.ascontiguousarray(np.swapaxes(v, -1, -2))


def constants():
    i, j = np.arange(P)[:, None], np.arange(P)[None, :]
    out, out2 = np.zeros((P, N_CST), np.float32), np.zeros((P, N_CST2), np.float32)

    def put(name, v):
        to, (a, n) = (out, CST[name]) if name in CST else (out2, CST2[name])
        to[:, a:a + n] = v.reshape(P, n)

    put("ident", i == j)
    put("ones", np.ones((P, P)))
    put("halves", i // HEAD == j // HEAD)
    put("tri_incl", i <= j)
    put("tri_strict", i < j)
    s = np.arange(2 * P - HEAD - 1)[None, :]
    put("slide", s == (HEAD - 1) + HEAD * (i // HEAD))
    put("iota", np.broadcast_to(j, (P, P)))
    q = HEAD // 4
    rot = np.zeros((P, P))
    for m in range(P):
        if (m // q) % 2 == 0:
            rot[m + q, m] = -1.0
        else:
            rot[m - q, m] = 1.0
    put("rot", rot)
    t = np.arange(T)
    half = HEAD // 2
    inv = ROPE_THETA ** (-np.arange(0, half, 2, dtype=np.float32) / half)
    ar, ac = (t // GRID_W)[:, None] * inv, (t % GRID_W)[:, None] * inv
    ang = np.concatenate([ar, ar, ac, ac], axis=-1).astype(np.float32)
    put("cos", np.tile(np.cos(ang).T, (2, 1)))
    put("sin", np.tile(np.sin(ang).T, (2, 1)))
    qq, kk = np.arange(T).reshape(TT, P).T[:, :, None], np.arange(T)[None, None, :]
    put("band", np.where(np.abs(qq - kk) <= SWA_WINDOW, 0.0, NEG))
    return out, out2


def join_masks():
    i, j = np.arange(P)[:, None], np.arange(P)[None, :]
    level = np.stack([(i // (2 << m) == j // (2 << m)) & ((i >> m) % 2 == 1) & ((j >> m) % 2 == 0)
                      for m in range(7)])
    return np.stack([level.transpose(1, 0, 2), level.transpose(2, 0, 1)], axis=1).astype(np.float32)


def packed(parts, at, n, lead):
    out = np.zeros((*lead, P, n), np.float32)
    for name, v in parts.items():
        a, w = at[name]
        out[..., a:a + w] = v.reshape(*lead, P, w)
    return out


def first_arrays(v):
    w = v["w_in"]
    gd = slice(1024 + 2048, 1024 + 2048 + 8)
    main = np.concatenate([w[:, :, :gd.start], w[:, :, gd.stop:]], axis=2)
    rows = lambda a: np.broadcast_to(a[:, None, :], (DEPTH, P, a.shape[-1]))
    taps = lambda a: np.ascontiguousarray(a.reshape(DEPTH, CONV_W, -1, P).transpose(0, 3, 2, 1))
    cols = packed({
        "norm_ffn1": by_part(v["norm_ffn1"]), "norm_mix": by_part(v["norm_mix"]),
        "norm_ffn2": by_part(v["norm_ffn2"]), "hg_norm": np.tile(v["hg_norm_w"], (1, 2))[:, :, None],
        "gd_norm": v["gd_norm_w"][:, :, None], "gd_conv": taps(v["gd_conv_w"]),
        "rg_conv": taps(v["rg_conv_w"]), "rg_conv_b": by_part(v["rg_conv_b"]),
        "rg_br": by_part(v["rg_br"]), "rg_bi": by_part(v["rg_bi"]), "rg_lambda": by_part(v["rg_lambda"]),
        "gd_a_log": rows(v["gd_a_log"]), "gd_dt_bias": rows(v["gd_dt_bias"]),
    }, COL, N_COLS, (DEPTH,))
    wrg = np.zeros((DEPTH, P, 2, 2, P), np.float32)
    for m, name in enumerate(("rg_wr", "rg_wi")):
        for blk in range(4):
            c, o = blk // 2, 64 * (blk % 2)
            wrg[:, o:o + 64, m, c, o:o + 64] = v[name][:, blk]
    wd = lambda a: fm(a).reshape(DEPTH, DC, P, 2, D_FF // 2).transpose(0, 1, 3, 2, 4).reshape(DEPTH, 2 * DC, P, D_FF // 2)
    return {
        "x": np.ascontiguousarray(v["x"][0].reshape(T, DC, P).transpose(2, 1, 0)),
        "cst": constants()[0], "cst2": constants()[1], "levels": join_masks(), "cols": cols, "hg_lb": np.ascontiguousarray(v["hg_lb"].reshape(DEPTH, 2, P).transpose(2, 0, 1)),
        "wg0": fm(v["ffn1_gate"]), "wu0": fm(v["ffn1_up"]), "wd0": wd(v["ffn1_down"]),
        "wg1": fm(v["ffn2_gate"]), "wu1": fm(v["ffn2_up"]), "wd1": wd(v["ffn2_down"]),
        "w_in": fm(main), "w_out": fm(v["w_out"]),
        "wba": np.ascontiguousarray(w[:, :, gd].reshape(DEPTH, DC, P, 8).transpose(0, 2, 1, 3)),
        "wrg": wrg,
    }


def second_arrays(v):
    g = lambda n: v[n + "_2"]
    rows = lambda a: np.broadcast_to(a.reshape(1, -1), (P, a.size))
    layers = lambda a: by_part(a).transpose(1, 0, 2)
    both = np.stack([g("c")[0], g("c_ctx")])
    cols2 = packed({
        "norm1": layers(g("norm1_g")), "norm2": layers(g("norm2_g")), "b_mod": layers(g("b_mod")),
        "c": by_part(both).transpose(1, 2, 0), "final": by_part(g("final_g")),
        "norm_last": by_part(v["norm_final"]), "subln": g("diff_subln_g")[0],
        "lambda": rows(g("diff_lambda")), "sink": rows(g("swa_sink")),
    }, COL2, N_COLS2, ())
    rpb = g("na_rpb")[0]
    tok = np.arange(T)
    r, c = tok // GRID_W, tok % GRID_W
    start = np.clip(c - NA_WIN_W // 2, 0, GRID_W - NA_WIN_W)
    inside = (c[None, :] >= start[:, None]) & (c[None, :] < start[:, None] + NA_WIN_W)
    dr = r[None, :] - r[:, None] + NA_WIN_H - 1
    dc = np.clip(c[None, :] - c[:, None] + NA_WIN_W - 1, 0, 2 * NA_WIN_W - 2)
    bias = np.where(inside[None], rpb[:, dr, dc], np.float32(NEG))
    bias = bias.reshape(4, 2, TT, P, T).transpose(0, 3, 1, 2, 4)
    odd = g("w_in_odd")[0]
    nq = SWA_Q_HEADS * HEAD
    kv = odd[:, nq:].reshape(D, 2 * SWA_KV_HEADS, 1, HEAD)
    kv = np.broadcast_to(kv, (D, 2 * SWA_KV_HEADS, 2, HEAD)).reshape(D, -1)
    odd = fm(np.concatenate([odd[:, :nq], kv], axis=1))
    order = [c for n in range(SWA_KV_HEADS) for c in (2 * n, 2 * n + 1, 8 + n, 12 + n)]
    behind = lambda w, n: np.concatenate([w, np.zeros((n, P, D), w.dtype)])
    return {
        "cols2": cols2, "bias": np.ascontiguousarray(bias),
        "ctx": np.ascontiguousarray(g("ctx")[0].reshape(T, DC, P).transpose(2, 1, 0)),
        "w_mod": np.ascontiguousarray(g("w_mod").reshape(DEPTH, DC, P, -1, MOD_W).transpose(0, 3, 2, 1, 4)
                                      ).reshape(DEPTH, -1, P, DC * MOD_W),
        "w_even": behind(fm(g("w_in_even")[0]), 1), "w_out_even": fm(g("w_out_even")[0]),
        "w_odd": behind(odd[order], 4), "w_out_odd": fm(g("w_out_odd")[0]),
        "wq": fm(g("peer_wq")),
        "keys": np.ascontiguousarray(g("peer_keys").reshape(DEPTH, 16, PEER_NKEYS, P).transpose(0, 3, 1, 2)),
        "u": fm(g("peer_u").transpose(0, 2, 1)),
        "v": g("peer_v").reshape(DEPTH, PEER_NKEYS, PEER_NKEYS, D),
    }


def build(nc, d, out):
    _names.clear()
    with ExitStack() as ctx:
        sb = lambda name, shape: ctx.enter_context(sbuf(nc, name, shape, F32))
        x, cst, last = sb("x_fm", [P, DC, T]), sb("cst_sb", [P, N_CST]), sb("last_cols", [P, 2 * DC])
        k = Constants(cst)
        a = COL2["final"][0]
        load_stage(nc, [(x[:], d.x), (cst[:], d.cst), (last[:], d.cols2[:, a:a + 2 * DC])])
        first_block(nc, k, x, d)
        norm_stage(nc, k, x, last[:, DC:2 * DC], x)
        second_block(nc, k, x, d)
        norm_stage(nc, k, x, last[:, 0:DC], x)
        with stage(nc, "stored") as (block, stored):
            @block.sync
            def _(sp):
                sp.dma_start(out, x[:]).then_inc(stored, 16)
                sp.wait_ge(stored, 16)


def kernel(**inputs):
    import concourse.bacc as bacc
    from concourse.bass_utils import run_bass_kernel_spmd

    v = {n: np.asarray(a) for n, a in inputs.items()}
    arrays = {**first_arrays(v), **second_arrays(v)}
    nc = bacc.Bacc("TRN2", target_bir_lowering=False, num_devices=1,
                   dynamic_dma_scratch_size=1024)
    d = Data()
    for name, a in arrays.items():
        d.__dict__[name] = nc.dram_tensor(f"in_{name}", a.shape, F32, kind="ExternalInput").ap()
    out = nc.dram_tensor("out", (P, DC, T), F32, kind="ExternalOutput").ap()
    build(nc, d, out)
    r = run_bass_kernel_spmd(nc, [{f"in_{n}": np.ascontiguousarray(a) for n, a in arrays.items()}], core_ids=[0])
    y = np.asarray(r.results[0]["out"])
    return np.ascontiguousarray(y.transpose(2, 1, 0)).reshape(1, T, D)
```
